# Optimizing a Trainium2 kernel written in Bass

```python
import jax, jax.numpy as jnp
from jax import lax
import numpy as np

D_MODEL = 1024
BATCH = 1
SEQ = 1024
DEPTH = 1

CHUNK = 64
D_MIX = D_MODEL
SWA_HEADS = 8
SWA_KV_HEADS = 2
SWA_HEAD_DIM = 64
SWA_GROUP = SWA_HEADS // SWA_KV_HEADS
SWA_WIDTH = SWA_HEADS * SWA_HEAD_DIM
SWA_KV_WIDTH = SWA_KV_HEADS * SWA_HEAD_DIM
WINDOW = 128
WINDOW_CHUNKS = WINDOW // CHUNK
GLA_HEADS = 4
GLA_KEY_DIM = 64
GLA_VAL_DIM = 128
GLA_K_WIDTH = GLA_HEADS * GLA_KEY_DIM
GLA_V_WIDTH = GLA_HEADS * GLA_VAL_DIM
GLA_GATE_RANK = 16
GLA_TAU = 16.0
N_EXPERTS = 32
TOP_K = 4
D_FF_EXPERT = D_MODEL
SWIGLU_LIMIT = 7.0
SWIGLU_ALPHA = 1.702
EXPERT_BLOCK = 128
EPS = 1e-6
IN_SPLITS = (SWA_WIDTH, SWA_KV_WIDTH, SWA_KV_WIDTH, GLA_K_WIDTH, GLA_K_WIDTH, GLA_V_WIDTH, GLA_GATE_RANK, GLA_V_WIDTH)
D_IN_PROJ = sum(IN_SPLITS)

kernel_name = "hymba_gla_swa_sink_moe_adaln_block"

def rms_norm(x, g):
    xf = x.astype(jnp.float32)
    y = xf * lax.rsqrt(jnp.mean(xf * xf, axis=-1, keepdims=True) + EPS)
    return (y * g.astype(jnp.float32)).astype(x.dtype)

def _chunk_band(t):
    n = t.shape[1]
    tp = jnp.concatenate([jnp.zeros_like(t[:, :WINDOW_CHUNKS - 1]), t], axis=1)
    return jnp.concatenate([tp[:, w:w + n] for w in range(WINDOW_CHUNKS)], axis=2)

def _alibi_bias():
    slopes = 2.0 ** (-8.0 * jnp.arange(1, SWA_HEADS + 1, dtype=jnp.float32) / SWA_HEADS)
    a = jnp.arange(CHUNK)[:, None]
    j = jnp.arange(WINDOW_CHUNKS * CHUNK)[None, :]
    dist = jnp.abs((WINDOW_CHUNKS - 1) * CHUNK + a - j).astype(jnp.float32)
    return (-slopes[:, None, None] * dist).reshape(SWA_KV_HEADS, SWA_GROUP, CHUNK, WINDOW_CHUNKS * CHUNK)

def sliding_window_attention(q, k, v, q_norm_g, k_norm_g, sinks):
    B, S, _ = q.shape
    N = S // CHUNK
    WC = WINDOW_CHUNKS * CHUNK
    q = rms_norm(q.reshape(B, S, SWA_HEADS, SWA_HEAD_DIM), q_norm_g)
    k = rms_norm(k.reshape(B, S, SWA_KV_HEADS, SWA_HEAD_DIM), k_norm_g)
    v = v.reshape(B, S, SWA_KV_HEADS, SWA_HEAD_DIM)
    qc = q.reshape(B, N, CHUNK, SWA_KV_HEADS, SWA_GROUP, SWA_HEAD_DIM)
    kb = _chunk_band(k.reshape(B, N, CHUNK, SWA_KV_HEADS, SWA_HEAD_DIM))
    vb = _chunk_band(v.reshape(B, N, CHUNK, SWA_KV_HEADS, SWA_HEAD_DIM))
    scores = jnp.einsum('bnqkgd,bnskd->bnkgqs', qc, kb).astype(jnp.float32) * (SWA_HEAD_DIM ** -0.5)
    scores = scores + _alibi_bias()
    n_idx = jnp.arange(N)[:, None]
    j_idx = jnp.arange(WC)[None, :]
    valid = (n_idx + j_idx // CHUNK - (WINDOW_CHUNKS - 1)) >= 0
    scores = jnp.where(valid[None, :, None, None, None, :], scores, -jnp.inf)
    sink = jnp.broadcast_to(sinks.astype(jnp.float32).reshape(1, 1, SWA_KV_HEADS, SWA_GROUP, 1, 1),
                            scores.shape[:-1] + (1,))
    probs = jax.nn.softmax(jnp.concatenate([scores, sink], axis=-1), axis=-1)[..., :-1]
    out = jnp.einsum('bnkgqs,bnskd->bnqkgd', probs.astype(vb.dtype), vb)
    return out.reshape(B, S, SWA_WIDTH)

def gated_linear_attention(q, k, v, gate_lr, out_gate, w_gate2, b_gate, norm_g):
    B, S, _ = q.shape
    N = S // CHUNK
    log_a = jax.nn.log_sigmoid((gate_lr @ w_gate2 + b_gate).astype(jnp.float32)) / GLA_TAU
    q = q * (GLA_KEY_DIM ** -0.5)

    def to_chunks(t, d):
        return t.reshape(B, N, CHUNK, GLA_HEADS, d).transpose(1, 0, 3, 2, 4)

    causal = jnp.tril(jnp.ones((CHUNK, CHUNK), dtype=bool))

    def step(state, inp):
        qc, kc, vc, gc = inp
        G = jnp.cumsum(gc, axis=2)
        o_inter = jnp.einsum('bhcd,bhde->bhce', qc * jnp.exp(G), state)
        diff = G[:, :, :, None, :] - G[:, :, None, :, :]
        decay = jnp.exp(jnp.where(causal[:, :, None], diff, -jnp.inf))
        A = jnp.einsum('bhtd,bhsd,bhtsd->bhts', qc, kc, decay)
        o = o_inter + jnp.einsum('bhts,bhse->bhte', A, vc)
        G_last = G[:, :, -1:, :]
        state = jnp.exp(G_last[:, :, 0, :])[..., None] * state + \
            jnp.einsum('bhcd,bhce->bhde', kc * jnp.exp(G_last - G), vc)
        return state, o

    state0 = jnp.zeros((B, GLA_HEADS, GLA_KEY_DIM, GLA_VAL_DIM), jnp.float32)
    _, o = lax.scan(step, state0, (to_chunks(q, GLA_KEY_DIM), to_chunks(k, GLA_KEY_DIM),
                                   to_chunks(v, GLA_VAL_DIM), to_chunks(log_a, GLA_KEY_DIM)))
    o = o.transpose(1, 0, 3, 2, 4).reshape(B, S, GLA_HEADS, GLA_VAL_DIM)
    o = rms_norm(o, norm_g).reshape(B, S, GLA_V_WIDTH)
    return o * jax.nn.silu(out_gate)

def routed_experts(h, w_router, b_router, w_gate, b_gate, w_up, b_up, w_down, b_down):
    B, S, D = h.shape
    T = B * S
    TK = T * TOP_K
    xt = h.reshape(T, D)
    logits = (xt @ w_router + b_router).astype(jnp.float32)
    top_vals, top_idx = lax.top_k(logits, TOP_K)
    top_w = jax.nn.softmax(top_vals, axis=-1)
    flat_e = top_idx.reshape(-1).astype(jnp.int32)
    flat_tok = jnp.repeat(jnp.arange(T, dtype=jnp.int32), TOP_K)
    flat_w = top_w.reshape(-1)
    order = jnp.argsort(flat_e, stable=True)
    sorted_e = flat_e[order]
    counts = jnp.bincount(flat_e, length=N_EXPERTS).astype(jnp.int32)
    starts = jnp.cumsum(counts) - counts
    padded = (counts + EXPERT_BLOCK - 1) // EXPERT_BLOCK * EXPERT_BLOCK
    padded_ends = jnp.cumsum(padded)
    padded_starts = padded_ends - padded
    rank = jnp.arange(TK, dtype=jnp.int32) - starts[sorted_e]
    dest = padded_starts[sorted_e] + rank
    n_blocks = -(-TK // EXPERT_BLOCK) + N_EXPERTS
    P = n_blocks * EXPERT_BLOCK
    slot_tok = jnp.zeros((P,), jnp.int32).at[dest].set(flat_tok[order])
    slot_w = jnp.zeros((P,), jnp.float32).at[dest].set(flat_w[order])
    block_start = jnp.arange(n_blocks, dtype=jnp.int32) * EXPERT_BLOCK
    block_expert = jnp.minimum(jnp.searchsorted(padded_ends, block_start, side='right'), N_EXPERTS - 1)

    def expert_block(args):
        tok, e = args
        xb = xt[tok]
        g = xb @ w_gate[e] + b_gate[e]
        u = xb @ w_up[e] + b_up[e]
        g = jnp.minimum(g, SWIGLU_LIMIT)
        u = jnp.clip(u, -SWIGLU_LIMIT, SWIGLU_LIMIT)
        act = g * jax.nn.sigmoid(SWIGLU_ALPHA * g) * (u + 1.0)
        return act @ w_down[e] + b_down[e]

    yb = lax.map(expert_block, (slot_tok.reshape(n_blocks, EXPERT_BLOCK), block_expert))
    y = jnp.zeros((T, D), jnp.float32).at[slot_tok].add(yb.reshape(P, D).astype(jnp.float32) * slot_w[:, None])
    return y.reshape(B, S, D).astype(h.dtype)

def setup_inputs(seed: int = 0) -> dict:
    key = jax.random.key(seed)
    ks = jax.random.split(key, 24)
    L, D, E, F = DEPTH, D_MODEL, N_EXPERTS, D_FF_EXPERT

    def nrm(k, shape, scale):
        return jax.random.normal(k, shape, jnp.float32) * scale

    return {
        "x": nrm(ks[0], (BATCH, SEQ, D), 1.0),
        "c": nrm(ks[1], (BATCH, D), 1.0),
        "norm1_g": 1.0 + nrm(ks[2], (L, D), 0.05),
        "w_ada": nrm(ks[3], (L, D, 6 * D), 0.5 * D ** -0.5),
        "b_ada": nrm(ks[4], (L, 6 * D), 0.02),
        "w_in": nrm(ks[5], (L, D, D_IN_PROJ), D ** -0.5),
        "q_norm_g": 1.0 + nrm(ks[6], (L, SWA_HEAD_DIM), 0.05),
        "k_norm_g": 1.0 + nrm(ks[7], (L, SWA_HEAD_DIM), 0.05),
        "sinks": nrm(ks[8], (L, SWA_HEADS), 0.5),
        "w_gla_gate2": nrm(ks[9], (L, GLA_GATE_RANK, GLA_K_WIDTH), GLA_GATE_RANK ** -0.5),
        "b_gla_gate": nrm(ks[10], (L, GLA_K_WIDTH), 0.1),
        "gla_norm_g": 1.0 + nrm(ks[11], (L, GLA_VAL_DIM), 0.05),
        "w_out": nrm(ks[12], (L, D_MIX, D), D_MIX ** -0.5),
        "norm2_g": 1.0 + nrm(ks[13], (L, D), 0.05),
        "w_router": nrm(ks[14], (L, D, E), D ** -0.5),
        "b_router": nrm(ks[15], (L, E), 0.01),
        "w_gate": nrm(ks[16], (L, E, D, F), D ** -0.5),
        "b_gate": nrm(ks[17], (L, E, F), 0.02),
        "w_up": nrm(ks[18], (L, E, D, F), D ** -0.5),
        "b_up": nrm(ks[19], (L, E, F), 0.02),
        "w_down": nrm(ks[20], (L, E, F, D), F ** -0.5),
        "b_down": nrm(ks[21], (L, E, D), 0.02),
    }

def reference(x, c, norm1_g, w_ada, b_ada, w_in, q_norm_g, k_norm_g, sinks, w_gla_gate2, b_gla_gate,
              gla_norm_g, w_out, norm2_g, w_router, b_router, w_gate, b_gate, w_up, b_up, w_down, b_down):
    split_at = [int(s) for s in np.cumsum(IN_SPLITS)[:-1]]
    for l in range(DEPTH):
        mod = jax.nn.silu(c) @ w_ada[l] + b_ada[l]
        sh1, sc1, g1, sh2, sc2, g2 = jnp.split(mod[:, None, :], 6, axis=-1)
        h = rms_norm(x, norm1_g[l]) * (1.0 + sc1) + sh1
        proj = h @ w_in[l]
        sq, sk, sv, gq, gk, gv, glr, gog = jnp.split(proj, split_at, axis=-1)
        y_swa = sliding_window_attention(sq, sk, sv, q_norm_g[l], k_norm_g[l], sinks[l])
        y_gla = gated_linear_attention(gq, gk, gv, glr, gog, w_gla_gate2[l], b_gla_gate[l], gla_norm_g[l])
        y = jnp.concatenate([y_swa.astype(x.dtype), y_gla.astype(x.dtype)], axis=-1) @ w_out[l]
        x = x + g1 * y
        h = rms_norm(x, norm2_g[l]) * (1.0 + sc2) + sh2
        x = x + g2 * routed_experts(h, w_router[l], b_router[l], w_gate[l], b_gate[l], w_up[l], b_up[l],
                                    w_down[l], b_down[l])
    return x


_drawn_inputs = setup_inputs


def setup_inputs(seed=0):
    import zlib

    import numpy as np

    out = dict(_drawn_inputs(seed))
    spreads = {}
    factors = {'norm1_g': 2.822,
     'q_norm_g': 7.469,
     'k_norm_g': 8.0,
     'sinks': 8.0,
     'b_gla_gate': 4.481,
     'gla_norm_g': 3.776,
     'b_router': 24.985,
     'b_gate': 34.066,
     'b_up': 47.561,
     'b_down': 34.093,
     'norm2_g': 3.872}
    for name, (base, spread) in spreads.items():
        noise = np.random.default_rng([zlib.crc32(name.encode()), seed]).standard_normal(out[name].shape)
        drawn = base * np.exp(spread * noise) if base else spread * noise
        out[name] = __import__('jax').numpy.asarray(drawn.astype(out[name].dtype))
    for name, factor in factors.items():
        out[name] = (out[name] * factor).astype(out[name].dtype)
    return out
```

```python
import math
from contextlib import ExitStack

import numpy as np

import concourse.bass as bass
from concourse import mybir

F32 = mybir.dt.float32
F32R = mybir.dt.float32r
I32 = mybir.dt.int32
U32 = mybir.dt.uint32
ALU = mybir.AluOpType
ACT = mybir.ActivationFunctionType
AX_X = mybir.AxisListType.X

P = 128
D = 1024
T = 1024
KT = D // P
NT = T // P
CH = 64
QH, KVH, HD = 8, 2, 64
GH, GK, GV = 4, 64, 128
RANK = 16
QW, KW, VW = QH * HD, KVH * HD, KVH * HD
GKW, GVW = GH * GK, GH * GV
C_SQ = 0
C_SK = C_SQ + QW
C_GQ = C_SK + KW + VW
C_GV = C_GQ + 2 * GKW
C_LR = C_GV + GVW
C_OG = C_LR + RANK
W_IN = C_OG + GVW
TAU = 16.0
EPS = 1e-6
NE, TOPK = 32, 4
LIMIT, ALPHA = 7.0, 1.702
NEG = -1.0e30

CAP = 192
CAP2 = CAP - P
MAXJ = (T - 1) // CAP
MAXOV = (T * TOPK) // CAP
MAIN = NE * CAP
SLOTS = (NE + MAXOV) * CAP
TABLE = SLOTS + CAP

NF = 7

WCOLS = 256
NCH = 3 * D // WCOLS
NRAW, NHL = 4, 6
LEAD = 4
POOL_CHUNKS = (2, 5, 8, 11)
NARROW = 144
NROWS = 8
CHOSEN_AT = 3 + NT
assert TABLE % P == 0
LEVELS = (32, 16, 8)
BASE = 8


def constants():
    u = np.arange(P)[:, None]
    t = np.arange(P)[None, :]
    same = lambda b: (u // b) == (t // b)
    mid = BASE * (t // BASE) + BASE // 2 - 1
    base_q = ((u > mid) & (u <= t)).astype(np.float32) - ((u > t) & (u <= mid)).astype(np.float32)
    e = [base_q, (same(CH) & (u <= t)).astype(np.float32)]
    for b in LEVELS:
        bound = 2 * b * (t // (2 * b)) + b - 1
        e.append((((u > bound) & (u <= t)) | ((u > t) & (u <= bound))).astype(np.float32))
    e += [-base_q, (same(CH) & (u > t)).astype(np.float32)]
    steps = np.stack(e, 1) / TAU
    mask = [same(2 * b) & (u % (2 * b) < b) & (t % (2 * b) >= b) for b in LEVELS]
    mask = np.stack(mask + [same(BASE) & (u <= t)], 1).astype(np.float32)
    slopes = 2.0 ** (-8.0 * np.arange(1, QH + 1, dtype=np.float32) / QH)
    a = np.arange(CH)[:, None]
    j = np.arange(2 * CH)[None, :]
    dist = np.abs(CH + a - j).astype(np.float32)
    alibi = (-slopes[:, None, None] * dist).reshape(QH // 2, P, P).transpose(1, 0, 2)
    parts = {
        "ident": np.eye(P, dtype=np.float32),
        "ones": np.ones((P, P), np.float32),
        "before": (u < t).astype(np.float32),
        "steps": steps.reshape(P, NF * P),
        "mask": mask.reshape(P, 4 * P),
        "alibi": alibi.reshape(P, 4 * P),
        "experts": np.tile(np.arange(NE, dtype=np.float32), (P, 1)),
        "slot0": np.tile(np.arange(NE, dtype=np.float32) * CAP, (P, 1)),
        "over": np.tile(np.repeat(np.arange(MAXOV, dtype=np.float32), NE), (P, 1)),
        "token": (np.arange(NT)[None, :] * P + np.arange(P)[:, None]).astype(np.float32),
        "minus_half": np.full((P, 1), -0.5, np.float32),
    }
    where, at = {}, 0
    for name, v in parts.items():
        where[name] = (at, v.shape[1])
        at += v.shape[1]
    return np.ascontiguousarray(np.concatenate(list(parts.values()), 1), dtype=np.float32), where


CONST, CONST_AT = constants()


def chunk_of(ci):
    return (2, ci - 8) if ci >= 8 else (ci % 2, ci // 2)


def wait(eng, sem, value):
    if isinstance(value, int) and value <= 0:
        return
    eng.wait_ge(sem, value)


class Steps:

    def __init__(self, eng, sem, tile, count):
        self.eng, self.sem, self.base, self.count, self.n = eng, sem, tile * count, count, 0

    def __call__(self, instruction, then_wait=True):
        instruction.then_inc(self.sem, 1)
        self.n += 1
        if then_wait:
            self.eng.wait_ge(self.sem, self.base + self.n)

    def end(self):
        assert self.n == self.count, (self.n, self.count)



def build(nc, a, out):
    ctx = ExitStack()
    with ctx:
        def sem(name):
            return ctx.enter_context(nc.semaphore(name))

        def sb(stack, name, shape, dt=F32):
            return stack.enter_context(nc.sbuf_tensor(name, shape, dt))

        y_dram = nc.dram_tensor("y_dram", [NT, P, KT * P], F32, kind="Internal").ap()
        x1_dram = nc.dram_tensor("x1_dram", [T, D], F32, kind="Internal").ap()
        h2_dram = nc.dram_tensor("h2_dram", [T, D], F32, kind="Internal").ap()
        slot_dram = nc.dram_tensor("slot_dram", [TABLE, 1], I32, kind="Internal").ap()
        rows_dram = nc.dram_tensor("rows_dram", [SLOTS, D], F32, kind="Internal").ap()

        tr0, tr1, pj0, pj1, pj2, sa, s_b, gb = [
            ctx.enter_context(nc.psum_tensor(n, [P, 512], F32))
            for n in ("tr0", "tr1", "pj0", "pj1", "pj2", "sa", "s_b", "gb")]

        const = sb(ctx, "const", [P, CONST.shape[1]])
        g2 = sb(ctx, "g2", [P, D])
        onehot = sb(ctx, "onehot", [P, NT, TOPK, NE])
        weights = sb(ctx, "weights", [P, NT, TOPK])
        slot_all = sb(ctx, "slot_all", [P, NT * TOPK], I32)
        slot_main = sb(ctx, "slot_main", [P, NT * TOPK], I32)
        slot_over = sb(ctx, "slot_over", [P, NT * TOPK], I32)
        w_main = sb(ctx, "w_main", [P, NT * TOPK])
        w_over = sb(ctx, "w_over", [P, NT * TOPK])
        blocks = sb(ctx, "blocks", [1, 3], I32)
        token_i = sb(ctx, "token_i", [P, NT], I32)
        expert_of = sb(ctx, "expert_of", [1, NE + MAXOV], I32)
        wide_of = sb(ctx, "wide_of", [1, NE + MAXOV], I32)

        def cst(name, rows=P):
            at, n = CONST_AT[name]
            return const[0:rows, at:at + n]

        ident = cst("ident")

        mix = ExitStack()
        sh1 = sb(mix, "sh1", [P, D])
        gs1 = sb(mix, "gs1", [P, D])
        g1 = sb(mix, "g1", [P, D])
        sh2 = sb(mix, "sh2", [P, D])
        gs2 = sb(mix, "gs2", [P, D])
        mods = [sh1, gs1, g1, sh2, gs2, g2]
        early = ExitStack()
        w_in = sb(early, "w_in_sb", [P, KT, W_IN])
        part_a = ExitStack()
        c_col = sb(part_a, "c_col", [P, KT])
        c_exp = sb(part_a, "c_exp", [P, KT])
        c_act = sb(part_a, "c_act", [P, KT])
        c_wide = sb(part_a, "c_wide", [P, KT, P])
        n_wide = sb(part_a, "n_wide", [P, 2, D])
        b_row = [sb(part_a, f"b_row{i}", [1, 512]) for i in range(3)]
        ada = [sb(part_a, f"ada{i}", [P, KT, 512]) for i in range(3)]
        fma = sb(part_a, "fma", [P, 512])
        part_a.close()
        x_in = sb(early, "x_in", [P, D])
        h = sb(early, "h", [P, D])
        ssx = sb(early, "ssx", [P, 2])
        hT = sb(early, "hT", [P, KT, P])
        qn = sb(early, "qn", [P, QW + KW])
        ssq = sb(early, "ssq", [P, QH + KVH])
        rq = sb(early, "rq", [P, QH + KVH])
        qk_g = sb(early, "qk_g", [P, 2])
        qT = sb(early, "qT", [HD, 2, QH, CH])
        kTw = sb(early, "kTw", [HD, KVH, CH + P])
        v_a = sb(early, "v_a", [P, VW])
        v_b = sb(early, "v_b", [P, VW])
        sc = sb(early, "sc", [P, 2, 512])
        stat = sb(early, "stat", [P, 6, 8])
        sink = sb(early, "sink", [P, 8])
        pT = sb(early, "pT", [P, 2, 512])
        alibi_a = sb(early, "alibi_a", [P, 512])
        yT = sb(early, "yT", [P, KT, P])
        gqk = sb(early, "gqk", [P, 4, P])
        fac = sb(early, "fac", [P, NF, P])
        sqs = sb(early, "sqs", [P, QW + KW])
        qf = sb(early, "qf", [P, 2, 5, P])
        kf = sb(early, "kf", [P, 2, 5, P])
        dec = sb(early, "dec", [P, 2, 2])
        at = sb(early, "at", [P, GH, P])
        kg = sb(early, "kg", [P, 2, 2, P])
        gv = sb(early, "gv", [P, GVW])
        gate = sb(early, "gate", [P, GVW])
        ge = sb(early, "ge", [P, GVW])
        y = sb(early, "y", [P, GVW])
        osq = sb(early, "osq", [P, GVW])
        sso = sb(early, "sso", [P, GH])
        ro = sb(early, "ro", [P, GH])
        s0 = sb(early, "s0", [P, 2, GV])
        s1 = sb(early, "s1", [P, 2, GV])
        la = sb(early, "la", [P, GKW])
        zb = sb(early, "zb", [P, GKW])
        zt = sb(early, "zt", [P, GKW])
        glrT = sb(early, "glrT", [RANK, P])
        w_g2 = sb(early, "w_g2", [RANK, GKW])
        bg_wide = sb(early, "bg_wide", [P, GKW])
        gn_wide = sb(early, "gn_wide", [P, GV])
        early.close()
        w_o = sb(mix, "w_o", [P, KT, D])
        y_in = [sb(mix, f"y_in{i}", [P, KT, P]) for i in range(2)]
        x_res = [sb(mix, f"x_res{i}", [P, D]) for i in range(2)]
        h2 = [sb(mix, f"h2_{i}", [P, D]) for i in range(2)]
        h2T = sb(mix, "h2T", [P, KT, P])
        w_r = sb(mix, "w_r", [P, KT, NE])
        br_wide = sb(mix, "br_wide", [P, NE])
        ss2 = sb(mix, "ss2", [P, 2])
        lg = sb(mix, "lg", [P, NE])
        top = sb(mix, "top", [P, 8])
        topi = sb(mix, "topi", [P, 8], U32)
        topf = sb(mix, "topf", [P, 4])
        tope = sb(mix, "tope", [P, 4])
        tops = sb(mix, "tops", [P, 2])
        zero_i = sb(mix, "zero_i", [P, TABLE // P], I32)
        chosen = sb(mix, "chosen", [P, NT, NE])
        prior = sb(mix, "prior", [P, NT + 1, NE])
        slotmap = sb(mix, "slotmap", [P, NT, NE])
        far = sb(mix, "far", [P, NT, NE])
        count = sb(mix, "count", [P, NE])
        more = sb(mix, "more", [P, MAXJ, NE])
        incl = sb(mix, "incl", [P, NE])
        base2 = sb(mix, "base2", [P, 2, NE])
        picked = sb(mix, "picked", [P, NT * TOPK, NE])
        slotf = sb(mix, "slotf", [P, 4, NT * TOPK])
        ovf = sb(mix, "ovf", [1, MAXOV, NE])
        ovs = sb(mix, "ovs", [1, MAXOV])
        mix.close()

        part_d = ExitStack()
        b_cols = sb(part_d, "b_cols", [P, 3, KT, NE])
        b_now = sb(part_d, "b_now", [P, 3, KT])
        slot_ids = sb(part_d, "slot_ids", [P, 2], I32)
        x_got = sb(part_d, "x_got", [P, 2, D])
        xT = sb(part_d, "xT", [P, KT, 2, CAP], F32R)
        g_sb = sb(part_d, "g_sb", [P, 2, CAP])
        u_sb = sb(part_d, "u_sb", [P, 2, CAP])
        sg_sb = sb(part_d, "sg_sb", [P, 2, CAP])
        av_sb = sb(part_d, "av_sb", [P, 2, CAP])
        actT = sb(part_d, "actT", [P, KT, 2, CAP], F32R)
        yT2 = sb(part_d, "yT2", [P, 4, 2, CAP])
        y_out = sb(part_d, "y_out", [P, 2, D])
        start_d = ExitStack()
        b_rows = sb(start_d, "b_rows", [NE, 3, D])
        start_d.close()
        w_hi, w_lo = [[sb(part_d, f"{n}{i}", [P, KT, WCOLS], F32R) for i in reversed(range(NHL))][::-1]
                      for n in ("w_hi", "w_lo")]
        raw = [sb(part_d, f"raw{i}", [P, KT, WCOLS]) for i in range(NRAW)]
        part_d.close()
        part_e = ExitStack()
        rows = [sb(part_e, f"rows{i}", [P, D]) for i in range(NROWS)]
        res = [sb(part_e, f"res{i}", [P, D]) for i in range(2)]
        acc = [sb(part_e, f"acc{i}", [P, D]) for i in range(2)]
        part_e.close()

        c_loaded, const_loaded, norms_loaded = sem("c_loaded"), sem("const_loaded"), sem("norms_loaded")
        ada_loaded = [sem(f"ada_loaded{i}") for i in range(3)]
        c_exp_ready, c_steps, c_wide_ready = sem("c_exp_ready"), sem("c_steps"), sem("c_wide_ready")
        fma_steps, fma_ready = sem("fma_steps"), sem("fma_ready")
        mod_filled = sem("mod_filled")
        mod_taken = [sem(f"mod_taken{i}") for i in range(3)]
        w_in_loaded, small_loaded, x_loaded = sem("w_in_loaded"), sem("small_loaded"), sem("x_loaded")
        init_ready = sem("init_ready")
        h_steps = sem("h_steps")
        hT_filled, hT_lo, hT_hi = sem("hT_filled"), sem("hT_lo"), sem("hT_hi")
        sq_filled, sq_squared, skv_filled, skv_squared = sem("sq_filled"), sem("sq_squared"), sem("skv_filled"), sem("skv_squared")
        ss_ready, rq_steps, rq_ready, qn_ready = sem("ss_ready"), sem("rq_steps"), sem("rq_ready"), sem("qn_ready")
        v_steps, v_ready = sem("v_steps"), sem("v_ready")
        qk_filled, k_moved, qkT_a, qkT_b = sem("qk_filled"), sem("k_moved"), sem("qkT_a"), sem("qkT_b")
        sc_filled, soft_steps, max_ready, p_ready, den_steps, p_norm = (
            sem("sc_filled"), sem("soft_steps"), sem("max_ready"), sem("p_ready"), sem("den_steps"), sem("p_norm"))
        pt_filled, pt_a, pt_b, pv_filled, pv_a, pv_b = (
            sem("pt_filled"), sem("pt_a"), sem("pt_b"), sem("pv_filled"), sem("pv_a"), sem("pv_b"))
        gqk_filled, gqk_ready, gv_filled, gv_ready = sem("gqk_filled"), sem("gqk_ready"), sem("gv_filled"), sem("gv_ready")
        og_filled, ge_ready, gate_steps, gate_ready = sem("og_filled"), sem("ge_ready"), sem("gate_steps"), sem("gate_ready")
        z_filled, z_steps, z_neg, zl_steps, zl_ready, la_ready = (
            sem("z_filled"), sem("z_steps"), sem("z_neg"), sem("zl_steps"), sem("zl_ready"), sem("la_ready"))
        e_filled, fac_ready, qkf_ready = sem("e_filled"), sem("fac_ready"), sem("qkf_ready")
        kg_filled, kg_ready = sem("kg_filled"), sem("kg_ready")
        at_filled, at_masked, at_ready = sem("at_filled"), sem("at_masked"), sem("at_ready")
        dl_filled, s1_ready, s0_ready = sem("dl_filled"), sem("s1_ready"), sem("s0_ready")
        even_filled, o_filled, so_ready, ro_steps, ro_ready, y_ready = (
            sem("even_filled"), sem("o_filled"), sem("so_ready"), sem("ro_steps"), sem("ro_ready"), sem("y_ready"))
        yt_filled, yT_ready, y_stored = sem("yt_filled"), sem("yT_ready"), sem("y_stored")
        rt_loaded = sem("rt_loaded")
        yx_loaded = [sem(f"yx_loaded{i}") for i in range(2)]
        wo_filled, x1_steps, x1_ready = sem("wo_filled"), sem("x1_steps"), sem("x1_ready")
        ss2_ready, r2_steps, r2_ready = sem("ss2_ready"), sem("r2_steps"), sem("r2_ready")
        h2_steps, h2_ready = sem("h2_steps"), sem("h2_ready")
        c_stored = [sem(f"c_stored{i}") for i in range(2)]
        h2t_filled, h2t_lo, h2t_hi, lg_filled = sem("h2t_filled"), sem("h2t_lo"), sem("h2t_hi"), sem("lg_filled")
        lg_steps, top_ready, tope_ready = sem("lg_steps"), sem("top_ready"), sem("tope_ready")
        table_zero, table_cleared, ct_steps, rank_filled = (
            sem("table_zero"), sem("table_cleared"), sem("ct_steps"), sem("rank_filled"))
        tail_filled = sem("tail_filled")
        slots_ready, table_written = sem("slots_ready"), sem("table_written")
        bias_loaded, bias_filled, bias_ready = sem("bias_loaded"), sem("bias_filled"), sem("bias_ready")
        raw_loaded = [sem(f"raw_loaded{i}") for i in range(NRAW)]
        hi_ready, lo_dve, lo_pool = sem("hi_ready"), sem("lo_dve"), sem("lo_pool")
        ids_loaded, x_gathered = sem("ids_loaded"), sem("x_gathered")
        xt_filled, xt_hi, xt_lo = sem("xt_filled"), sem("xt_hi"), sem("xt_lo")
        b_now_ready = sem("b_now_ready")
        m_filled, up_right, up_taken, down_right, down_taken = (
            sem("m_filled"), sem("up_right"), sem("up_taken"), sem("down_right"), sem("down_taken"))
        g_clipped, u_clipped, sig_ready, gs_ready, av_ready, act_hi, act_lo = (
            sem("g_clipped"), sem("u_clipped"), sem("sig_ready"), sem("gs_ready"), sem("av_ready"), sem("act_hi"), sem("act_lo"))
        yt2_filled, y_taken, rows_stored = sem("yt2_filled"), sem("y_taken"), sem("rows_stored")
        row_loaded = [sem(f"row_loaded{i}") for i in range(NROWS)]
        res_loaded = [sem(f"res_loaded{i}") for i in range(2)]
        add_steps, row_used = sem("add_steps"), sem("row_used")
        out_stored = [sem(f"out_stored{i}") for i in range(2)]
        passed = sem("passed")

        block = ctx.enter_context(nc.Block())

        def apart(eng):
            eng.sem_inc(passed, 1)

        @block.sync
        def _(sp):
            sp.dma_start(c_col[:], a["c"].rearrange("b (k p) -> p (b k)", p=P),
                         allow_slow_non_contiguous=True).then_inc(c_loaded, 16)
            sp.dma_start(const[:], a["const"]).then_inc(const_loaded, 16)
            w_ada = a["w_ada"][0].rearrange("(k p) n -> p k n", p=P)
            for i in range(12):
                s = i % 3
                if i >= 3:
                    sp.wait_ge(mod_filled, i - 2)
                sp.dma_start(ada[s][:], w_ada[:, :, i * 512:(i + 1) * 512]).then_inc(ada_loaded[s], 16)
                sp.dma_start(b_row[s][:], a["b_ada"][:, i * 512:(i + 1) * 512]).then_inc(ada_loaded[s], 16)
                if i == 1:
                    sp.dma_start(n_wide[:, 0, :], a["norm1_g"].broadcast_to([P, D])).then_inc(norms_loaded, 16)
                    sp.dma_start(n_wide[:, 1, :], a["norm2_g"].broadcast_to([P, D])).then_inc(norms_loaded, 16)
            sp.dma_start(w_in[:], a["w_in"][0].rearrange("(k p) n -> p k n", p=P)).then_inc(w_in_loaded, 16)
            for s in range(3):
                sp.wait_ge(mod_taken[s], 4)
            sp.dma_start(x_in[:], a["x"][0, 0:P, :]).then_inc(x_loaded, 16)
            sp.dma_start(w_g2[:], a["w_gla_gate2"][0]).then_inc(small_loaded, 16)
            sp.dma_start(bg_wide[:], a["b_gla_gate"].broadcast_to([P, GKW])).then_inc(small_loaded, 16)
            sp.dma_start(gn_wide[:], a["gla_norm_g"].broadcast_to([P, GV])).then_inc(small_loaded, 16)
            for half in range(2):
                lo, hi = half * HD, half * HD + HD
                sp.dma_start(qk_g[lo:hi, 0:1], a["q_norm_g"].rearrange("a d -> d a"),
                             allow_slow_non_contiguous=True).then_inc(small_loaded, 16)
                sp.dma_start(qk_g[lo:hi, 1:2], a["k_norm_g"].rearrange("a d -> d a"),
                             allow_slow_non_contiguous=True).then_inc(small_loaded, 16)
                for chunk in range(2):
                    sp.dma_start(sink[lo:hi, 4 * chunk:4 * chunk + 4],
                                 a["sinks"].rearrange("a (j two) -> a two j", two=2)[:, half, :].broadcast_to([CH, 4]),
                                 allow_slow_non_contiguous=True).then_inc(small_loaded, 16)

            def load_x(n):
                sp.wait_ge(h_steps, n * 6 - 2)
                sp.dma_start(x_in[:], a["x"][0, bass.ds(n * P, P), :]).then_inc(x_loaded, 16)

            def store_y(m):
                sp.wait_ge(pv_a, m + 1)
                sp.wait_ge(pv_b, m + 1)
                sp.wait_ge(yT_ready, m + 1)
                sp.dma_start(y_dram[bass.ds(m, 1)].rearrange("a p n -> (a p) n"),
                             yT[:].rearrange("p k t -> p (k t)")).then_inc(y_stored, 16)

            load_x(1)
            with sp.Fori(0, NT - 2) as m:
                load_x(m + 2)
                store_y(m)
            store_y(NT - 2)
            sp.wait_ge(og_filled, NT)
            sp.wait_ge(z_filled, NT)
            sp.dma_start(w_o[:], a["w_out"][0].rearrange("(k p) n -> p k n", p=P)).then_inc(rt_loaded, 16)
            sp.dma_start(w_r[:], a["w_router"][0].rearrange("(k p) e -> p k e", p=P)).then_inc(rt_loaded, 16)
            sp.dma_start(br_wide[:], a["b_router"].broadcast_to([P, NE])).then_inc(rt_loaded, 16)

            def load_c(t, s):
                sp.dma_start(y_in[s][:].rearrange("p k t -> p (k t)"),
                             y_dram[bass.ds(t, 1)].rearrange("a p n -> (a p) n")).then_inc(yx_loaded[s], 16)
                sp.dma_start(x_res[s][:], a["x"][0, bass.ds(t * P, P), :]).then_inc(yx_loaded[s], 16)

            sp.wait_ge(y_stored, 16 * (NT - 1))
            load_c(0, 0)
            load_c(1, 1)
            store_y(NT - 1)
            w_of = [a["w_gate"][0], a["w_up"][0], a["w_down"][0]]
            last_b = [(la_ready, NT), (y_ready, NT), (s0_ready, NT)]

            def load_w(e, b, ci):
                which, c = chunk_of(ci)
                s = ci % NRAW
                g = b * NCH + ci - NRAW + 1
                if not (isinstance(g, int) and g <= 0):
                    wait_split(sp, b, ci - NRAW, g)
                src = w_of[which]
                src = src[bass.ds(e, 1)].rearrange("a (k p) n -> p (a k) n", p=P)
                sp.dma_start(raw[s][:], src[:, :, c * WCOLS:(c + 1) * WCOLS]).then_inc(raw_loaded[s], 16)

            def wait_split(eng, b, ci, g):
                eng.wait_ge(hi_ready, g)
                apart(eng)
                bb, cc = (b, ci) if ci >= 0 else (b - 1, ci + NCH)
                on_pool = sum(1 for x in range(cc + 1) if x in POOL_CHUNKS)
                pool_count = bb * len(POOL_CHUNKS) + on_pool
                dve_count = bb * (NCH - len(POOL_CHUNKS)) + (cc + 1 - on_pool)
                if cc in POOL_CHUNKS:
                    eng.wait_ge(lo_pool, pool_count)
                else:
                    eng.wait_ge(lo_dve, dve_count)

            for sm, v in last_b:
                sp.wait_ge(sm, v)
            sp.wait_ge(y_stored, 16 * NT)
            for ci in range(NRAW):
                load_w(0, 0, ci)

            def store_c(t, s):
                sp.wait_ge(x1_ready, t + 1)
                sp.dma_start(x1_dram[bass.ds(t * P, P), :], x_res[s][:]).then_inc(c_stored[s], 16)
                sp.wait_ge(h2_ready, t + 1)
                sp.dma_start(h2_dram[bass.ds(t * P, P), :], h2[s][:]).then_inc(c_stored[s], 16)

            with sp.Fori(0, NT // 2 - 1) as i:
                for s in range(2):
                    store_c(i * 2 + s, s)
                    sp.wait_ge(c_stored[s], i * 32 + 32)
                    load_c(i * 2 + s + 2, s)
            for s in range(2):
                store_c(NT - 2 + s, s)
            sp.wait_ge(slots_ready, 1)
            for s in range(2):
                sp.wait_ge(c_stored[s], 16 * NT)
            for j, name in enumerate(("b_gate", "b_up", "b_down")):
                sp.dma_start(b_rows[:, j, :], a[name][0]).then_inc(bias_loaded, 16)
            for ci in range(NRAW, NCH):
                load_w(0, 0, ci)
            with sp.Fori(1, NE) as b:
                for ci in range(NCH):
                    load_w(b, b, ci)
            sp.wait_ge(slots_ready, 2)
            further = sp.value_load(blocks[0:1, 1:2], min_val=0, max_val=MAXOV)
            with sp.If(further > 0):
                total = sp.value_load(blocks[0:1, 0:1], min_val=NE + 1, max_val=NE + MAXOV)
                with sp.Fori(NE, total) as b:
                    e = sp.value_load(expert_of[0:1, bass.ds(b, 1)], min_val=0, max_val=NE - 1)
                    for ci in range(NCH):
                        load_w(e, b, ci)
            with sp.Else():
                sp.nop()
            def residuals(dst, first):
                for t in range(NT):
                    s = t % 2
                    n = first + t
                    if n >= 2:
                        sp.wait_ge(out_stored[s], 16 * (n // 2))
                    sp.dma_start(res[s][:], x1_dram[t * P:(t + 1) * P, :]).then_inc(res_loaded[s], 16)
                    if t >= 1:
                        sp.wait_ge(add_steps, 2 * n)
                        sp.dma_start(dst[(t - 1) * P:t * P, :], res[1 - s][:]).then_inc(out_stored[1 - s], 16)
                sp.wait_ge(add_steps, 2 * (first + NT))
                sp.dma_start(dst[(NT - 1) * P:, :], res[1][:]).then_inc(out_stored[1], 16)

            def after_experts():
                n_blocks = sp.value_load(blocks[0:1, 0:1], min_val=NE, max_val=NE + MAXOV)
                sp.wait_ge(rows_stored, n_blocks * 32)
                sp.wait_ge(xt_hi, n_blocks * 4 + 4)
                sp.wait_ge(xt_lo, n_blocks * 4 + 4)
                apart(sp)
            after_experts()
            with sp.If(further > 0):
                residuals(x1_dram, 0)
                for s in range(2):
                    sp.wait_ge(out_stored[s], 16 * (NT // 2))
                residuals(out[0], NT)
                for s in range(2):
                    sp.wait_ge(out_stored[s], 16 * NT)
            with sp.Else():
                residuals(out[0], 0)
                for s in range(2):
                    sp.wait_ge(out_stored[s], 16 * (NT // 2))
            sp.nop()

        @block.gpsimd
        def _(pool):
            for s in range(3):
                pool.wait_ge(mod_taken[s], 4)

            def norm_in(n):
                st = Steps(pool, h_steps, n, 6)
                st.n = 1
                pool.wait_ge(h_steps, n * 6 + 1)
                apart(pool)
                st(nc.gpsimd.tensor_scalar(ssx[:, 0:1], ssx[:, 0:1], 1.0 / D, EPS, ALU.mult, ALU.add))
                st(nc.gpsimd.tensor_tensor(ssx[:, 1:2], ssx[:, 0:1], cst("minus_half"), ALU.pow))
                apart(pool)
                st(nc.gpsimd.tensor_scalar(h[:], x_in[:], ssx[:, 1:2], None, ALU.mult))
                st(nc.gpsimd.tensor_tensor(h[:], h[:], gs1[:], ALU.mult))
                st(nc.gpsimd.tensor_tensor(h[:], h[:], sh1[:], ALU.add))
                st.end()

            def rq_pow(n):
                st = Steps(pool, rq_steps, n, 1)
                pool.wait_ge(ss_ready, n * 2 + 2)
                apart(pool)
                st(nc.gpsimd.tensor_scalar(rq[:], ssq[:], 1.0 / HD, EPS, ALU.mult, ALU.add))
                nc.gpsimd.tensor_tensor(rq[:], rq[:], cst("minus_half").broadcast_to([P, QH + KVH]), ALU.pow).then_inc(rq_ready, 1)
                st.end()

            def ro_pow(m):
                st = Steps(pool, ro_steps, m, 1)
                pool.wait_ge(so_ready, m + 1)
                apart(pool)
                st(nc.gpsimd.tensor_scalar(ro[:], sso[:], 1.0 / GV, EPS, ALU.mult, ALU.add))
                nc.gpsimd.tensor_tensor(ro[:], ro[:], cst("minus_half").broadcast_to([P, GH]), ALU.pow).then_inc(ro_ready, 1)
                st.end()

            norm_in(0)
            rq_pow(0)
            norm_in(1)
            with pool.Fori(0, NT - 2) as m:
                rq_pow(m + 1)
                norm_in(m + 2)
                ro_pow(m)
            rq_pow(NT - 1)
            ro_pow(NT - 2)
            ro_pow(NT - 1)

            def r2_pow(t):
                st = Steps(pool, r2_steps, t, 1)
                pool.wait_ge(ss2_ready, t + 1)
                apart(pool)
                st(nc.gpsimd.tensor_scalar(ss2[:, 0:1], ss2[:, 0:1], 1.0 / D, EPS, ALU.mult, ALU.add))
                nc.gpsimd.tensor_tensor(ss2[:, 1:2], ss2[:, 0:1], cst("minus_half"), ALU.pow).then_inc(r2_ready, 1)
                st.end()

            pool.wait_ge(wo_filled, 1)
            nc.gpsimd.memset(zero_i[:], 0).then_inc(table_zero, 1)
            pool.wait_ge(table_zero, 1)
            pool.dma_start(slot_dram.rearrange("(p n) a -> p (n a)", p=P), zero_i[:]).then_inc(table_cleared, 16)
            with pool.Fori(0, NT) as t:
                r2_pow(t)
            pool.wait_ge(table_cleared, 16)
            pool.wait_ge(slots_ready, 1)
            for j in range(NT * TOPK):
                nc.gpsimd.indirect_dma_start(slot_dram, bass.IndirectOffsetOnAxis(slot_all[:, j:j + 1], 0),
                                             token_i[:, j // TOPK:j // TOPK + 1], None).then_inc(table_written, 16)
            pool.wait_ge(table_written, 16 * NT * TOPK)

            for s in range(2):
                pool.wait_ge(c_stored[s], 16 * NT)

            def load_ids(b):
                wait(pool, x_gathered, b * 32)
                pool.dma_start(slot_ids[:, 0:1], slot_dram[bass.ds(b * CAP, P), :]).then_inc(ids_loaded, 16)
                pool.dma_start(slot_ids[0:CAP2, 1:2], slot_dram[bass.ds(b * CAP + P, CAP2), :]).then_inc(ids_loaded, 16)

            def gather(b):
                pool.wait_ge(ids_loaded, b * 32 + 32)
                wait(pool, xt_filled, b * 4)
                apart(pool)
                nc.gpsimd.indirect_dma_start(x_got[:, 0, :], None, h2_dram,
                                             bass.IndirectOffsetOnAxis(slot_ids[:, 0:1], 0)).then_inc(x_gathered, 16)
                nc.gpsimd.indirect_dma_start(x_got[0:CAP2, 1, :], None, h2_dram,
                                             bass.IndirectOffsetOnAxis(slot_ids[0:CAP2, 1:2], 0)).then_inc(x_gathered, 16)

            load_ids(0)
            gather(0)
            pool.wait_ge(slots_ready, 2)
            n_blocks = pool.value_load(blocks[0:1, 0:1], min_val=NE, max_val=NE + MAXOV)
            with pool.Fori(0, n_blocks) as b:
                load_ids(b + 1)
                for i, ci in enumerate(POOL_CHUNKS):
                    pool.wait_ge(hi_ready, b * NCH + ci + 1)
                    nc.gpsimd.tensor_tensor(w_lo[ci % NHL][:], raw[ci % NRAW][:], w_hi[ci % NHL][:].bitcast(F32),
                                            ALU.subtract).then_inc(lo_pool, 1)
                    if i == 0:
                        gather(b + 1)

            further = pool.value_load(blocks[0:1, 1:2], min_val=0, max_val=MAXOV)
            pool.wait_ge(rows_stored, n_blocks * 32)
            pool.wait_ge(xt_hi, n_blocks * 4 + 4)
            pool.wait_ge(xt_lo, n_blocks * 4 + 4)
            apart(pool)

            def fetch(table, source, first):
                for j in range(NT * TOPK):
                    n = first + j
                    if n >= NROWS:
                        pool.wait_ge(row_used, n - NROWS + 1)
                    nc.gpsimd.indirect_dma_start(rows[n % NROWS][:], None, source,
                                                 bass.IndirectOffsetOnAxis(table[:, j:j + 1], 0)
                                                 ).then_inc(row_loaded[n % NROWS], 16)

            with pool.If(further > 0):
                fetch(slot_over, rows_dram, 0)
                fetch(slot_main, rows_dram[0:MAIN, :], NT * TOPK)
            with pool.Else():
                fetch(slot_main, rows_dram[0:MAIN, :], 0)
            pool.nop()

        @block.scalar
        def _(act):
            act.wait_ge(c_loaded, 16)
            nc.scalar.activation(c_exp[:], c_col[:], ACT.Exp, scale=-1.0).then_inc(c_exp_ready, 1)
            for i in range(12):
                if i // 2 in (1, 4):
                    continue
                act.wait_ge(mod_filled, i + 1)
                nc.scalar.copy(mods[i // 2][:, (i % 2) * 512:(i % 2) * 512 + 512],
                               (pj0, pj1, pj2)[i % 3][:]).then_inc(mod_taken[i % 3], 1)
            for s in range(3):
                act.wait_ge(mod_taken[s], 4)
            act.wait_ge(small_loaded, 11 * 16)
            act.wait_ge(init_ready, 3)

            def take_hT(n):
                act.wait_ge(hT_filled, n + 1)
                nc.scalar.copy(hT[:, 0:4, :].rearrange("p k t -> p (k t)"), tr0[:]).then_inc(hT_lo, 1)

            def square_x(n):
                act.wait_ge(x_loaded, n * 16 + 16)
                wait(act, hT_filled, n)
                nc.scalar.activation(h[:], x_in[:], ACT.Square, accum_out=ssx[:, 0:1]).then_inc(h_steps, 1)

            def square_q(n):
                act.wait_ge(sq_filled, n + 1)
                wait(act, qn_ready, n * 2)
                nc.scalar.activation(sqs[:, 0:QW], pj0[:], ACT.Square).then_inc(sq_squared, 1)

            def square_k(n):
                act.wait_ge(skv_filled, n + 1)
                nc.scalar.activation(sqs[:, QW:], pj1[:, 0:KW], ACT.Square)
                nc.scalar.copy(glrT[:], pj1[0:RANK, 256:256 + P]).then_inc(skv_squared, 1)

            def take_q(n):
                act.wait_ge(qk_filled, n + 1)
                wait(act, sc_filled, n)
                nc.scalar.activation(qT[:, :, 0:QH:2, :].rearrange("p c h t -> p h c t"),
                                     tr0[0:HD, :].rearrange("p (h c t) -> p h c t", t=CH, c=2),
                                     ACT.Copy, scale=qk_g[0:HD, 0:1])
                act.wait_ge(k_moved, n + 1)
                nc.scalar.activation(kTw[:, 0, CH:], sa[0:HD, 0:P], ACT.Copy,
                                     scale=qk_g[0:HD, 1:2]).then_inc(qkT_a, 1)

            def take_gqk(n):
                act.wait_ge(gqk_filled, n + 1)
                wait(act, qkf_ready, n * 2)
                nc.scalar.activation(gqk[:, 0:2, :].rearrange("p c t -> p (c t)"), pj2[:, 0:2 * P], ACT.Copy,
                                     scale=GK ** -0.5)
                nc.scalar.copy(gqk[:, 2:4, :].rearrange("p c t -> p (c t)"), pj2[:, 2 * P:]).then_inc(gqk_ready, 1)

            def exp_gate(n):
                act.wait_ge(og_filled, n + 1)
                wait(act, gate_ready, n)
                nc.scalar.activation(ge[:], pj1[:], ACT.Exp, scale=-1.0).then_inc(ge_ready, 1)

            def softplus(n):
                st = Steps(act, zl_steps, n, 1)
                act.wait_ge(z_neg, n + 1)
                st(nc.scalar.activation(zt[:], zt[:], ACT.Exp))
                nc.scalar.activation(zt[:], zt[:], ACT.Ln, bias=1.0).then_inc(zl_ready, 1)
                st.end()

            def softmax_exp(m):
                act.wait_ge(max_ready, m + 1)
                for c in range(2):
                    for j in range(4):
                        nc.scalar.activation(sc[:, c, j * P:(j + 1) * P], sc[:, c, j * P:(j + 1) * P], ACT.Exp,
                                             bias=stat[:, 1, 4 * c + j:4 * c + j + 1],
                                             accum_out=stat[:, 3, 4 * c + j:4 * c + j + 1])
                nc.scalar.activation(stat[:, 4, :], stat[:, 2, :], ACT.Exp).then_inc(p_ready, 1)

            def take_pT(m):
                act.wait_ge(pt_filled, m + 1)
                wait(act, pv_filled, m)
                nc.scalar.copy(pT[:, 0, :], sa[:]).then_inc(pt_a, 1)

            def take_pv(m):
                act.wait_ge(pv_filled, m + 1)
                wait(act, y_stored, m * 16)
                v = sa[0:HD, :].rearrange("p (h q) -> p h q", q=CH)
                nc.scalar.copy(yT[0:HD, 0:4, 0:CH], v[:, 0:QH:2, :])
                nc.scalar.copy(yT[HD:P, 0:4, 0:CH], v[:, 1:QH:2, :]).then_inc(pv_a, 1)

            def factors(m, c):
                act.wait_ge(e_filled, m * 2 + c + 1)
                wait(act, qkf_ready, m * 2 + c)
                nc.scalar.activation(fac[:, 0:4, :].rearrange("p f t -> p (f t)"), gb[:], ACT.Exp)
                nc.scalar.activation(fac[:, 4:7, :].rearrange("p f t -> p (f t)"), tr1[:, 0:3 * P],
                                     ACT.Exp).then_inc(fac_ready, 1)

            def take_kg(m):
                act.wait_ge(kg_filled, m + 1)
                for chunk in range(2):
                    rows_of = slice(chunk * CH, (chunk + 1) * CH)
                    ins = nc.scalar.copy(kg[rows_of, chunk].rearrange("p c d -> p (c d)"), tr0[rows_of, 0:2 * P])
                ins.then_inc(kg_ready, 1)

            def square_o(m):
                act.wait_ge(o_filled, m + 1)
                wait(act, ro_ready, m)
                for hd in range(GH):
                    ins = nc.scalar.activation(osq[:, hd * GV:(hd + 1) * GV], sa[:, hd * GV:(hd + 1) * GV],
                                               ACT.Square, accum_out=sso[:, hd:hd + 1])
                ins.then_inc(so_ready, 1)

            def take_yT(m):
                act.wait_ge(yt_filled, m + 1)
                nc.scalar.copy(yT[:, 4:8, :].rearrange("p k t -> p (k t)"), tr0[:]).then_inc(yT_ready, 1)

            def mixer_tile(m, more_tiles, more_x):
                n = m + 1
                if more_tiles:
                    take_hT(n)
                softmax_exp(m)
                if more_tiles:
                    square_q(n)
                if more_x:
                    square_x(n + 1)
                take_pT(m)
                if more_tiles:
                    square_k(n)
                take_pv(m)
                factors(m, 0)
                if more_tiles:
                    take_q(n)
                factors(m, 1)
                if more_tiles:
                    take_gqk(n)
                take_kg(m)
                square_o(m)
                if more_tiles:
                    exp_gate(n)
                    softplus(n)
                take_yT(m)

            square_x(0)
            take_hT(0)
            square_x(1)
            square_q(0)
            square_k(0)
            take_q(0)
            take_gqk(0)
            exp_gate(0)
            softplus(0)
            mixer_tile(0, True, True)
            with act.Fori(1, NT - 2) as m:
                mixer_tile(m, True, True)
            mixer_tile(NT - 2, True, False)
            mixer_tile(NT - 1, False, False)

            def square_x1(t, s):
                act.wait_ge(x1_ready, t + 1)
                nc.scalar.activation(h2[s][:], x_res[s][:], ACT.Square, accum_out=ss2[:, 0:1]).then_inc(ss2_ready, 1)

            def take_h2T(t):
                act.wait_ge(h2t_filled, t + 1)
                nc.scalar.copy(h2T[:, 0:4, :].rearrange("p k t -> p (k t)"), tr0[:]).then_inc(h2t_lo, 1)

            def exp_top(t):
                act.wait_ge(top_ready, t + 1)
                nc.scalar.activation(tope[:], topf[:], ACT.Exp, accum_out=tops[:, 0:1]).then_inc(tope_ready, 1)

            square_x1(0, 0)
            square_x1(1, 1)
            take_h2T(0)
            exp_top(0)
            with act.Fori(1, NT // 2) as i:
                for s in range(2):
                    square_x1(i * 2 + s, s)
                    take_h2T(i * 2 + s - 1)
                    exp_top(i * 2 + s - 1)
            take_h2T(NT - 1)
            exp_top(NT - 1)

            act.wait_ge(slots_ready, 2)
            act.wait_ge(bias_filled, 1)
            nc.scalar.copy(b_cols[:, 0].rearrange("p k e -> p (k e)"), pj0[:, 0:KT * NE])
            nc.scalar.activation(b_cols[:, 1].rearrange("p k e -> p (k e)"), pj1[:, 0:KT * NE], ACT.Copy, bias=1.0)
            nc.scalar.copy(b_cols[:, 2].rearrange("p k e -> p (k e)"), pj2[:, 0:KT * NE]).then_inc(bias_ready, 1)

            def high_part(b, ci):
                act.wait_ge(raw_loaded[ci % NRAW], (b * (NCH // NRAW) + ci // NRAW + 1) * 16)
                if ci >= NHL:
                    act.wait_ge(m_filled, (b * NCH + ci - NHL + 1) * 2)
                elif not isinstance(b, int):
                    act.wait_ge(m_filled, (b * NCH + ci - NHL + 1) * 2)
                nc.scalar.copy(w_hi[ci % NHL][:], raw[ci % NRAW][:]).then_inc(hi_ready, 1)

            def x_high(b, q):
                act.wait_ge(xt_filled, b * 4 + q + 1)
                bank = (tr0, tr1)[q % 2]
                nc.scalar.copy(xT[:, 2 * q:2 * q + 2, 0, :],
                               bank[:, 0:2 * CAP].rearrange("p (k t) -> p k t", t=CAP)).then_inc(xt_hi, 1)

            def right_part(b, ci):
                which, pair = chunk_of(ci)
                if which == 0:
                    wait(act, gs_ready, b * 4 + pair)
                else:
                    wait(act, av_ready, b * 4 + pair)
                for f in range(2):
                    q = 2 * ci + f
                    act.wait_ge(m_filled, b * 24 + q + 1)
                    nc.scalar.activation((g_sb, u_sb)[which][:, f, :], (pj0, pj1, pj2, sa)[q % 4][:, CAP:2 * CAP],
                                         ACT.Identity, bias=b_now[:, which, 2 * pair + f:2 * pair + f + 1]
                                         ).then_inc(up_right, 1)

            def sigmoid(b, pair):
                act.wait_ge(g_clipped, b * 4 + pair + 1)
                wait(act, gs_ready, b * 4 + pair)
                nc.scalar.activation(sg_sb[:], g_sb[:], ACT.Sigmoid, scale=ALPHA).then_inc(sig_ready, 1)

            def act_high(b, pair):
                act.wait_ge(av_ready, b * 4 + pair + 1)
                nc.scalar.copy(actT[:, 2 * pair:2 * pair + 2, 0, :], av_sb[:]).then_inc(act_hi, 1)

            def down_right_part(b, pair):
                wait(act, yt2_filled, b * 4)
                for f in range(2):
                    q = 16 + 2 * pair + f
                    act.wait_ge(m_filled, b * 24 + q + 1)
                    nc.scalar.activation(yT2[:, pair, f, :], (pj0, pj1, pj2, sa)[q % 4][:, CAP:2 * CAP], ACT.Identity,
                                         bias=b_now[:, 2, 2 * pair + f:2 * pair + f + 1]).then_inc(down_right, 1)

            def take_rows(b, half):
                act.wait_ge(yt2_filled, b * 4 + 2 * half + 2)
                wait(act, rows_stored, b * 32)
                nc.scalar.copy(y_out[:, 0, half * 512:half * 512 + 512], s_b[:])
                nc.scalar.copy(y_out[0:CAP2, 1, half * 512:half * 512 + 512], gb[0:CAP2, :]).then_inc(y_taken, 1)

            for q in range(4):
                x_high(0, q)
            n_blocks = act.value_load(blocks[0:1, 0:1], min_val=NE, max_val=NE + MAXOV)

            def last_part(b, then, high_parts):
                if high_parts:
                    high_part(then, 0)
                x_high(then, 2)
                if high_parts:
                    high_part(then, 1)
                down_right_part(b, 2)
                x_high(then, 3)
                if high_parts:
                    high_part(then, 2)
                down_right_part(b, 3)
                if high_parts:
                    high_part(then, 3)
                take_rows(b, 0)

            def first_part(b, before=None):
                act.wait_ge(b_now_ready, b + 1)
                for slot in range(8):
                    high_part(b, slot + LEAD)
                    if slot % 2:
                        sigmoid(b, slot // 2)
                    elif slot:
                        act_high(b, slot // 2 - 1)
                    right_part(b, slot)
                    if slot == 1 and before is not None:
                        take_rows(before, 1)
                        store_rows(before)
                act_high(b, 3)
                down_right_part(b, 0)
                x_high(b + 1, 0)
                x_high(b + 1, 1)
                down_right_part(b, 1)

            def store_rows(b):
                act.wait_ge(y_taken, b * 2 + 2)
                act.dma_start(rows_dram[bass.ds(b * CAP, P), :], y_out[:, 0, :]).then_inc(rows_stored, 16)
                act.dma_start(rows_dram[bass.ds(b * CAP + P, CAP2), :], y_out[0:CAP2, 1, :]).then_inc(rows_stored, 16)

            further = act.value_load(blocks[0:1, 1:2], min_val=0, max_val=MAXOV)
            with act.If(further > 0):
                for s in range(2):
                    act.wait_ge(c_stored[s], 16 * NT)
                for at_row in range(MAIN, SLOTS, T):
                    n = min(T, SLOTS - at_row)
                    act.dma_start(rows_dram[at_row:at_row + n, :], h2_dram[0:n, :]).then_inc(tail_filled, 16)
                act.wait_ge(tail_filled, 16 * math.ceil((SLOTS - MAIN) / T))
                act.nop()
            with act.Else():
                act.nop()
            for ci in range(LEAD):
                high_part(0, ci)
            first_part(0)
            with act.Fori(1, n_blocks) as b:
                last_part(b - 1, b, True)
                first_part(b, b - 1)
            last = act.value_load(blocks[0:1, 2:3], min_val=NE - 1, max_val=NE + MAXOV - 1)
            last_part(last, n_blocks, False)
            take_rows(last, 1)
            store_rows(last)
            act.wait_ge(rows_stored, n_blocks * 32)
            apart(act)
            act.nop()

        @block.vector
        def _(dve):
            st = Steps(dve, c_steps, 0, 3)
            dve.wait_ge(c_exp_ready, 1)
            dve.wait_ge(const_loaded, 16)
            st(nc.vector.tensor_scalar(c_exp[:], c_exp[:], 1.0, None, ALU.add))
            st(nc.vector.reciprocal(c_exp[:], c_exp[:]))
            st(nc.vector.tensor_tensor(c_act[:], c_col[:], c_exp[:], ALU.mult))
            for k in range(KT):
                ins = nc.vector.tensor_scalar(c_wide[:, k, :], cst("ones"), c_act[:, k:k + 1], None, ALU.mult)
            ins.then_inc(c_wide_ready, 1)
            for i in range(12):
                if i % 3 == 2:
                    st = Steps(dve, fma_steps, i // 3, KT - 1)
                    dve.wait_ge(ada_loaded[2], (i // 3 + 1) * 32)
                    wait(dve, mod_filled, i - 2)
                    st(nc.vector.tensor_scalar(fma[:], ada[2][:, 0, :], c_act[:, 0:1], None, ALU.mult))
                    for k in range(1, KT):
                        ins = nc.vector.scalar_tensor_tensor(fma[:], ada[2][:, k, :], c_act[:, k:k + 1], fma[:],
                                                             ALU.mult, ALU.add)
                        if k < KT - 1:
                            st(ins)
                    ins.then_inc(fma_ready, 1)
                    st.end()
                if i // 2 in (1, 4):
                    which, half = i // 2, i % 2
                    dve.wait_ge(norms_loaded, 32)
                    dve.wait_ge(mod_filled, i + 1)
                    nc.vector.scalar_tensor_tensor(
                        mods[which][:, half * 512:half * 512 + 512], (pj0, pj1, pj2)[i % 3][:], 1.0,
                        n_wide[:, which // 4, half * 512:half * 512 + 512], ALU.add, ALU.mult,
                    ).then_inc(mod_taken[i % 3], 1)
            for s in range(3):
                dve.wait_ge(mod_taken[s], 4)
            st = Steps(dve, init_ready, 0, 2)
            nc.vector.memset(kTw[:], 0.0)
            nc.vector.memset(v_b[:], 0.0)
            nc.vector.memset(kg[:], 0.0)
            nc.vector.memset(s0[:], 0.0)
            st(nc.vector.tensor_copy(alibi_a[:], cst("alibi")))
            st(nc.vector.memset(alibi_a[:].rearrange("p (j k) -> p j k", k=P)[:, :, 0:CH], NEG))
            dve.wait_ge(small_loaded, 11 * 16)
            nc.vector.tensor_scalar(qk_g[:, 0:1], qk_g[:, 0:1], HD ** -0.5, None, ALU.mult).then_inc(init_ready, 1)
            dve.wait_ge(init_ready, 3)
            st.end()

            def take_hT(n):
                dve.wait_ge(hT_filled, n + 1)
                nc.vector.tensor_copy(hT[:, 4:8, :].rearrange("p k t -> p (k t)"), tr1[:]).then_inc(hT_hi, 1)

            def heads_squared(n):
                dve.wait_ge(sq_squared, n + 1)
                wait(dve, rq_ready, n)
                nc.vector.tensor_reduce(ssq[:, 0:QH], sqs[:, 0:QW].rearrange("p (h d) -> p h d", d=HD),
                                        AX_X, ALU.add).then_inc(ss_ready, 1)

            def keys_squared(n):
                dve.wait_ge(skv_squared, n + 1)
                nc.vector.tensor_reduce(ssq[:, QH:], sqs[:, QW:].rearrange("p (h d) -> p h d", d=HD),
                                        AX_X, ALU.add).then_inc(ss_ready, 1)

            def normed_qk(n):
                dve.wait_ge(rq_ready, n + 1)
                wait(dve, qk_filled, n)
                nc.vector.tensor_tensor(qn[:, 0:QW].rearrange("p (h d) -> p h d", d=HD),
                                        pj0[:].rearrange("p (h d) -> p h d", d=HD),
                                        rq[:, 0:QH].unsqueeze(2).broadcast_to([P, QH, HD]),
                                        ALU.mult).then_inc(qn_ready, 1)
                nc.vector.tensor_tensor(qn[:, QW:].rearrange("p (h d) -> p h d", d=HD),
                                        pj1[:, 0:KW].rearrange("p (h d) -> p h d", d=HD),
                                        rq[:, QH:].unsqueeze(2).broadcast_to([P, KVH, HD]),
                                        ALU.mult).then_inc(qn_ready, 1)

            def take_v(n):
                st = Steps(dve, v_steps, n, 1)
                wait(dve, pv_filled, n)
                st(nc.vector.tensor_copy(v_a[0:CH, :], v_b[CH:P, :]))
                nc.vector.tensor_copy(v_a[CH:P, :], pj1[0:CH, KW:KW + VW])
                nc.vector.tensor_copy(v_b[:], pj1[:, KW:KW + VW]).then_inc(v_ready, 1)
                st.end()

            def take_qk(n):
                wait(dve, sc_filled, n)
                nc.vector.tensor_copy(kTw[:, :, 0:CH], kTw[:, :, P:P + CH]).then_inc(k_moved, 1)
                dve.wait_ge(qk_filled, n + 1)
                nc.vector.tensor_scalar(qT[:, :, 1:QH:2, :].rearrange("p c h t -> p h c t"),
                                        tr0[HD:P, :].rearrange("p (h c t) -> p h c t", t=CH, c=2),
                                        qk_g[HD:P, 0:1], None, ALU.mult)
                dve.wait_ge(k_moved, n + 1)
                nc.vector.tensor_scalar(kTw[:, 1, CH:], sa[HD:P, 0:P], qk_g[HD:P, 1:2], None,
                                        ALU.mult).then_inc(qkT_b, 1)

            def take_gv(n):
                dve.wait_ge(gv_filled, n + 1)
                wait(dve, o_filled, n)
                nc.vector.tensor_copy(gv[:], pj0[:]).then_inc(gv_ready, 1)

            def out_gate(n):
                st = Steps(dve, gate_steps, n, 3)
                dve.wait_ge(ge_ready, n + 1)
                st(nc.vector.tensor_scalar(ge[:], ge[:], 1.0, None, ALU.add))
                st(nc.vector.reciprocal(ge[:], ge[:]))
                wait(dve, y_ready, n)
                st(nc.vector.tensor_tensor(ge[:], pj1[:], ge[:], ALU.mult))
                nc.vector.tensor_tensor(gate[:].rearrange("p (h e) -> p h e", e=GV),
                                        ge[:].rearrange("p (h e) -> p h e", e=GV),
                                        gn_wide[:].unsqueeze(1).broadcast_to([P, GH, GV]),
                                        ALU.mult).then_inc(gate_ready, 1)
                st.end()

            def forget_in(n):
                st = Steps(dve, z_steps, n, 1)
                dve.wait_ge(z_filled, n + 1)
                st(nc.vector.tensor_tensor(zb[:], s_b[:, 0:GKW], bg_wide[:], ALU.add))
                nc.vector.scalar_tensor_tensor(zt[:], zb[:], -1.0, zb[:], ALU.mult, ALU.min).then_inc(z_neg, 1)
                st.end()

            def forget_out(n):
                dve.wait_ge(zl_ready, n + 1)
                wait(dve, e_filled, n * 2)
                nc.vector.scalar_tensor_tensor(la[:], zb[:], 0.0, zt[:], ALU.min, ALU.subtract).then_inc(la_ready, 1)

            def softmax_max(m):
                st = Steps(dve, soft_steps, m, 6)
                dve.wait_ge(sc_filled, m + 1)
                st(nc.vector.tensor_tensor(sc[:, 0, :], sa[:], alibi_a[:], ALU.add), False)
                st(nc.vector.tensor_tensor(sc[:, 1, :], s_b[:], cst("alibi"), ALU.add))
                st(nc.vector.tensor_copy(alibi_a[:], cst("alibi")), False)
                st(nc.vector.tensor_reduce(stat[:, 0, :], sc[:].rearrange("p c (j k) -> p (c j) k", k=P), AX_X, ALU.max))
                st(nc.vector.tensor_tensor(stat[:, 0, :], stat[:, 0, :], sink[:], ALU.max))
                st(nc.vector.tensor_scalar(stat[:, 1, :], stat[:, 0, :], -1.0, None, ALU.mult))
                nc.vector.tensor_tensor(stat[:, 2, :], sink[:], stat[:, 1, :], ALU.add).then_inc(max_ready, 1)
                st.end()

            def softmax_norm(m):
                st = Steps(dve, den_steps, m, 2)
                dve.wait_ge(p_ready, m + 1)
                st(nc.vector.tensor_tensor(stat[:, 3, :], stat[:, 3, :], stat[:, 4, :], ALU.add))
                st(nc.vector.reciprocal(stat[:, 5, :], stat[:, 3, :]))
                v = sc[:].rearrange("p c (j k) -> p (c j) k", k=P)
                nc.vector.tensor_tensor(v, v, stat[:, 5, :].unsqueeze(2).broadcast_to([P, 8, P]),
                                        ALU.mult).then_inc(p_norm, 1)
                st.end()

            def take_pT(m):
                dve.wait_ge(pt_filled, m + 1)
                wait(dve, pv_filled, m)
                nc.vector.tensor_copy(pT[:, 1, :], s_b[:]).then_inc(pt_b, 1)

            def take_pv(m):
                dve.wait_ge(pv_filled, m + 1)
                wait(dve, y_stored, m * 16)
                v = s_b[0:HD, :].rearrange("p (h q) -> p h q", q=CH)
                nc.vector.tensor_copy(yT[0:HD, 0:4, CH:P], v[:, 0:QH:2, :])
                nc.vector.tensor_copy(yT[HD:P, 0:4, CH:P], v[:, 1:QH:2, :]).then_inc(pv_b, 1)

            def decayed(m, c):
                dve.wait_ge(fac_ready, m * 2 + c + 1)
                dve.wait_ge(gqk_ready, m + 1)
                wait(dve, o_filled, m)
                wait(dve, s0_ready, m)
                nc.vector.tensor_tensor(qf[:, c], fac[:, 0:5, :],
                                        gqk[:, c, :].unsqueeze(1).broadcast_to([P, 5, P]), ALU.mult)
                nc.vector.tensor_copy(dec[:, c, :], fac[:, 1, CH - 1:P:CH])
                nc.vector.tensor_tensor(kf[:, c], fac[:, 2:7, :],
                                        gqk[:, 2 + c, :].unsqueeze(1).broadcast_to([P, 5, P]),
                                        ALU.mult).then_inc(qkf_ready, 1)

            def scores_within(m, hd):
                dve.wait_ge(at_filled, m * 4 + hd + 1)
                bank = (gb, tr1)[hd % 2]
                if hd >= 2:
                    dve.wait_ge(at_ready, m * 4 + hd - 1)
                else:
                    dve.wait_ge(pt_filled, m + 1)
                    wait(dve, at_ready, m * 4)
                    wait(dve, o_filled, m)
                nc.vector.tensor_tensor(sc[:, hd % 2, :], bank[:], cst("mask"), ALU.mult).then_inc(at_masked, 1)
                dve.wait_ge(at_masked, m * 4 + hd + 1)
                nc.vector.tensor_reduce(at[:, hd, :], sc[:, hd % 2, :].rearrange("p (l t) -> p t l", t=P),
                                        AX_X, ALU.add).then_inc(at_ready, 1)

            def state_mid(m):
                dve.wait_ge(dl_filled, m + 1)
                wait(dve, s0_ready, m)
                for c in range(2):
                    ins = nc.vector.scalar_tensor_tensor(s1[:, c, :], s0[:, c, :], dec[:, c, 0:1],
                                                         s_b[:, (2 * c) * GV:(2 * c + 1) * GV], ALU.mult, ALU.add)
                ins.then_inc(s1_ready, 1)

            def state_end(m):
                dve.wait_ge(o_filled, m + 1)
                dve.wait_ge(s1_ready, m + 1)
                for c in range(2):
                    ins = nc.vector.scalar_tensor_tensor(s0[:, c, :], s1[:, c, :], dec[:, c, 1:2],
                                                         s_b[:, (2 * c + 1) * GV:(2 * c + 2) * GV], ALU.mult, ALU.add)
                ins.then_inc(s0_ready, 1)

            def normed_o(m):
                dve.wait_ge(ro_ready, m + 1)
                dve.wait_ge(gate_ready, m + 1)
                wait(dve, yt_filled, m)
                for hd in range(GH):
                    ins = nc.vector.scalar_tensor_tensor(y[:, hd * GV:(hd + 1) * GV], sa[:, hd * GV:(hd + 1) * GV],
                                                         ro[:, hd:hd + 1], gate[:, hd * GV:(hd + 1) * GV],
                                                         ALU.mult, ALU.mult)
                ins.then_inc(y_ready, 1)

            def mixer_tile(m, more_tiles):
                n = m + 1
                if more_tiles:
                    take_hT(n)
                softmax_max(m)
                softmax_norm(m)
                if more_tiles:
                    heads_squared(n)
                take_pT(m)
                if more_tiles:
                    keys_squared(n)
                    normed_qk(n)
                take_pv(m)
                if more_tiles:
                    take_v(n)
                decayed(m, 0)
                if more_tiles:
                    take_qk(n)
                decayed(m, 1)
                for hd in range(GH):
                    scores_within(m, hd)
                state_mid(m)
                state_end(m)
                normed_o(m)
                if more_tiles:
                    take_gv(n)
                    out_gate(n)
                    forget_in(n)
                    forget_out(n)

            take_hT(0)
            heads_squared(0)
            keys_squared(0)
            normed_qk(0)
            take_v(0)
            take_qk(0)
            take_gv(0)
            out_gate(0)
            forget_in(0)
            forget_out(0)
            mixer_tile(0, True)
            with dve.Fori(1, NT - 1) as m:
                mixer_tile(m, True)
                apart(dve)
            mixer_tile(NT - 1, False)

            def residual(t, s):
                st = Steps(dve, x1_steps, t, 1)
                dve.wait_ge(wo_filled, t + 1)
                dve.wait_ge(yx_loaded[s], (t - s) * 16 + 32)
                if not (isinstance(t, int) and t < 2):
                    dve.wait_ge(c_stored[s], (t - s) * 16)
                lo, hi = ((pj0, pj1), (pj2, sa))[s]
                nc.vector.tensor_tensor(h2[s][:, 0:512], lo[:], g1[:, 0:512], ALU.mult)
                st(nc.vector.tensor_tensor(h2[s][:, 512:], hi[:], g1[:, 512:], ALU.mult))
                nc.vector.tensor_tensor(x_res[s][:], x_res[s][:], h2[s][:], ALU.add).then_inc(x1_ready, 1)
                st.end()

            def norm_out(t, s):
                st = Steps(dve, h2_steps, t, 1)
                dve.wait_ge(r2_ready, t + 1)
                st(nc.vector.scalar_tensor_tensor(h2[s][:], x_res[s][:], ss2[:, 1:2], gs2[:], ALU.mult, ALU.mult))
                nc.vector.tensor_tensor(h2[s][:], h2[s][:], sh2[:], ALU.add).then_inc(h2_ready, 1)
                st.end()

            def take_h2T(t):
                dve.wait_ge(h2t_filled, t + 1)
                nc.vector.tensor_copy(h2T[:, 4:8, :].rearrange("p k t -> p (k t)"), tr1[:]).then_inc(h2t_hi, 1)

            def choose(t):
                st = Steps(dve, lg_steps, t, 6)
                dve.wait_ge(lg_filled, t + 1)
                dve.wait_ge(rt_loaded, 48)
                st(nc.vector.tensor_tensor(lg[:], gb[:, 0:NE], br_wide[:], ALU.add))
                apart(dve)
                st(nc.vector.max(top[:], lg[:]))
                wait(dve, tope_ready, t)
                nc.vector.tensor_scalar(topf[:], top[:, 0:4], top[:, 0:1], None, ALU.subtract).then_inc(top_ready, 1)
                st(nc.vector.max_index(topi[:], top[:], lg[:]))
                dve.wait_ge(tope_ready, t + 1)
                st(nc.vector.tensor_copy(topf[:], topi[:, 0:4]))
                st(nc.vector.tensor_tensor(onehot[:, bass.ds(t, 1)].rearrange("p a k e -> p (a k) e"),
                                           topf[:].unsqueeze(2).broadcast_to([P, TOPK, NE]),
                                           cst("experts").unsqueeze(1).broadcast_to([P, TOPK, NE]), ALU.is_equal), False)
                st(nc.vector.reciprocal(tops[:, 1:2], tops[:, 0:1]))
                nc.vector.tensor_scalar(weights[:, bass.ds(t, 1)].rearrange("p a k -> p (a k)"), tope[:],
                                        tops[:, 1:2], None, ALU.mult)
                st.end()

            residual(0, 0)
            norm_out(0, 0)
            residual(1, 1)
            take_h2T(0)
            norm_out(1, 1)
            choose(0)
            with dve.Fori(1, NT // 2) as i:
                for s in range(2):
                    t = i * 2 + s
                    residual(t, s)
                    take_h2T(t - 1)
                    norm_out(t, s)
                    choose(t - 1)
            take_h2T(NT - 1)
            choose(NT - 1)

            st = Steps(dve, ct_steps, 0, 0)
            st(nc.vector.tensor_copy(token_i[:], cst("token")), False)
            st(nc.vector.memset(prior[:, 0, :], 0.0), False)
            st(nc.vector.tensor_reduce(chosen[:], onehot[:].rearrange("p t k e -> p t e k"), AX_X, ALU.add))
            for t in range(NT):
                st(nc.vector.tensor_tensor(prior[:, t + 1, :], prior[:, t, :], chosen[:, t, :], ALU.add))
            assert st.n == CHOSEN_AT
            dve.wait_ge(rank_filled, 1)
            st(nc.vector.tensor_copy(count[:], pj1[:, 0:NE]), False)
            st(nc.vector.tensor_copy(slotmap[:].rearrange("p t e -> p (t e)"), pj0[:, 0:NT * NE]))
            st(nc.vector.tensor_scalar(more[:, 0, :], count[:], float(CAP), None, ALU.is_gt))
            for j in range(1, MAXJ):
                st(nc.vector.scalar_tensor_tensor(more[:, j, :], count[:], float(CAP * (j + 1)), more[:, j - 1, :],
                                                  ALU.is_gt, ALU.add))
            st(nc.vector.tensor_tensor_scan(incl[:], cst("ones")[:, 0:NE], more[:, MAXJ - 1, :], 0.0, ALU.mult, ALU.add))
            st(nc.vector.tensor_tensor(base2[:, 0, :], incl[:], more[:, MAXJ - 1, :], ALU.subtract))
            st(nc.vector.tensor_scalar(base2[:, 0, :], base2[:, 0, :], float(CAP), float((NE - 1) * CAP), ALU.mult, ALU.add))
            st(nc.vector.tensor_tensor(base2[:, 1, :], base2[:, 0, :], cst("slot0"), ALU.subtract))
            st(nc.vector.tensor_scalar(far[:], slotmap[:], float(CAP), None, ALU.is_ge))
            st(nc.vector.tensor_tensor(far[:], far[:], base2[:, 1, :].unsqueeze(1).broadcast_to([P, NT, NE]), ALU.mult))
            st(nc.vector.tensor_tensor(slotmap[:], slotmap[:],
                                       cst("slot0").unsqueeze(1).broadcast_to([P, NT, NE]), ALU.add))
            st(nc.vector.tensor_tensor(slotmap[:], slotmap[:], far[:], ALU.add))
            for t in range(NT):
                st(nc.vector.tensor_tensor(picked[:, t * TOPK:(t + 1) * TOPK, :], onehot[:, t],
                                           slotmap[:, t, :].unsqueeze(1).broadcast_to([P, TOPK, NE]), ALU.mult), t == NT - 1)
            st(nc.vector.tensor_reduce(slotf[:, 0, :], picked[:], AX_X, ALU.add))
            st(nc.vector.tensor_copy(slot_all[:], slotf[:, 0, :]))
            nc.vector.tensor_scalar(slotf[:, 1, :], slotf[:, 0, :], float(MAIN - 1), None, ALU.min).then_inc(slots_ready, 1)
            dve.wait_ge(slots_ready, 1)
            w_all = weights[:].rearrange("p t k -> p (t k)")
            st(nc.vector.tensor_copy(slot_main[:], slotf[:, 1, :]), False)
            st(nc.vector.tensor_scalar(slotf[:, 2, :], slotf[:, 0, :], float(MAIN), None, ALU.is_ge))
            st(nc.vector.tensor_tensor(slotf[:, 3, :], slotf[:, 2, :], slotf[:, 0, :], ALU.mult), False)
            st(nc.vector.tensor_tensor(w_over[:], slotf[:, 2, :], w_all, ALU.mult))
            st(nc.vector.tensor_copy(slot_over[:], slotf[:, 3, :]), False)
            st(nc.vector.tensor_tensor(w_main[:], w_all, w_over[:], ALU.subtract), False)
            for i, more_than in enumerate((NE, 0, NE - 1)):
                st(nc.vector.tensor_scalar(blocks[:, i:i + 1], incl[0:1, NE - 1:NE], float(more_than), None, ALU.add), i == 2)
            st(nc.vector.tensor_scalar(wide_of[:, 0:NE], count[0:1, :], float(NARROW), None, ALU.is_gt), False)
            st(nc.vector.memset(wide_of[:, NE:], 1), False)
            st(nc.vector.tensor_tensor(ovf[:], incl[0:1, :].unsqueeze(1).broadcast_to([1, MAXOV, NE]),
                                       cst("over", 1).rearrange("p (b e) -> p b e", e=NE), ALU.is_le))
            st(nc.vector.tensor_reduce(ovs[:], ovf[:], AX_X, ALU.add))
            st(nc.vector.tensor_scalar(ovs[:], ovs[:], float(NE - 1), None, ALU.min))
            st(nc.vector.tensor_copy(expert_of[:, 0:NE], cst("experts", 1)), False)
            nc.vector.tensor_copy(expert_of[:, NE:], ovs[:]).then_inc(slots_ready, 1)
            dve.wait_ge(slots_ready, 2)

            n_blocks = dve.value_load(blocks[0:1, 0:1], min_val=NE, max_val=NE + MAXOV)
            dve.wait_ge(bias_ready, 1)

            def low_part(b, ci):
                if ci in POOL_CHUNKS:
                    return
                dve.wait_ge(hi_ready, b * NCH + ci + 1)
                nc.vector.tensor_tensor(w_lo[ci % NHL][:], raw[ci % NRAW][:], w_hi[ci % NHL][:].bitcast(F32),
                                        ALU.subtract).then_inc(lo_dve, 1)

            def x_low(b, q):
                dve.wait_ge(xt_hi, b * 4 + q + 1)
                bank = (tr0, tr1)[q % 2]
                nc.vector.tensor_tensor(xT[:, 2 * q:2 * q + 2, 1, :],
                                        bank[:, 0:2 * CAP].rearrange("p (k t) -> p k t", t=CAP),
                                        xT[:, 2 * q:2 * q + 2, 0, :].bitcast(F32), ALU.subtract).then_inc(xt_lo, 1)

            def biases(b):
                e = dve.value_load(expert_of[0:1, bass.ds(b, 1)], min_val=0, max_val=NE - 1)
                nc.vector.tensor_copy(b_now[:], b_cols[:, :, :, bass.ds(e, 1)].rearrange("p j k e -> p j (k e)")
                                      ).then_inc(b_now_ready, 1)
                dve.wait_ge(b_now_ready, b + 1)

            m_banks = (pj0, pj1, pj2, sa)

            def add_left(b, q, dst):
                dve.wait_ge(up_right, b * 16 + q + 1)
                nc.vector.tensor_tensor(dst, m_banks[q % 4][:, 0:CAP], dst, ALU.add).then_inc(up_taken, 1)

            def take_gate(b, pair):
                for f in range(2):
                    add_left(b, 4 * pair + f, g_sb[:, f, :])
                dve.wait_ge(up_taken, b * 16 + 4 * pair + 2)
                nc.vector.tensor_scalar(g_sb[:], g_sb[:], LIMIT, None, ALU.min).then_inc(g_clipped, 1)

            def take_up(b, pair):
                for f in range(2):
                    add_left(b, 4 * pair + 2 + f, u_sb[:, f, :])
                dve.wait_ge(up_taken, b * 16 + 4 * pair + 4)
                nc.vector.tensor_scalar(u_sb[:], u_sb[:], 1.0 + LIMIT, 1.0 - LIMIT, ALU.min, ALU.max).then_inc(u_clipped, 1)

            def activate(b, pair):
                dve.wait_ge(sig_ready, b * 4 + pair + 1)
                nc.vector.tensor_tensor(sg_sb[:], g_sb[:], sg_sb[:], ALU.mult).then_inc(gs_ready, 1)
                take_up(b, pair)
                dve.wait_ge(gs_ready, b * 4 + pair + 1)
                dve.wait_ge(u_clipped, b * 4 + pair + 1)
                nc.vector.tensor_tensor(av_sb[:], u_sb[:], sg_sb[:], ALU.mult).then_inc(av_ready, 1)

            def take_down(b, pair):
                for f in range(2):
                    q = 16 + 2 * pair + f
                    dst = yT2[:, pair, f, :]
                    dve.wait_ge(down_right, b * 8 + 2 * pair + f + 1)
                    nc.vector.tensor_tensor(dst, m_banks[q % 4][:, 0:CAP], dst, ALU.add).then_inc(down_taken, 1)

            def act_low(b, pair):
                dve.wait_ge(act_hi, b * 4 + pair + 1)
                nc.vector.tensor_tensor(actT[:, 2 * pair:2 * pair + 2, 1, :], av_sb[:],
                                        actT[:, 2 * pair:2 * pair + 2, 0, :].bitcast(F32),
                                        ALU.subtract).then_inc(act_lo, 1)

            def first_part(b):
                biases(b)
                for pair in range(4):
                    low_part(b, 2 * pair + LEAD)
                    take_gate(b, pair)
                    if pair:
                        act_low(b, pair - 1)
                    low_part(b, 2 * pair + 1 + LEAD)
                    activate(b, pair)
                act_low(b, 3)
                take_down(b, 0)
                x_low(b + 1, 0)
                x_low(b + 1, 1)
                take_down(b, 1)

            def last_part(b, then, low_parts):
                if low_parts:
                    low_part(then, 0)
                x_low(then, 2)
                if low_parts:
                    low_part(then, 1)
                take_down(b, 2)
                x_low(then, 3)
                if low_parts:
                    low_part(then, 2)
                take_down(b, 3)
                if low_parts:
                    low_part(then, 3)

            for q in range(4):
                x_low(0, q)
            for ci in range(LEAD):
                low_part(0, ci)
            first_part(0)
            with dve.Fori(1, n_blocks) as b:
                last_part(b - 1, b, True)
                first_part(b)
            last = dve.value_load(blocks[0:1, 2:3], min_val=NE - 1, max_val=NE + MAXOV - 1)
            last_part(last, n_blocks, False)

            further = dve.value_load(blocks[0:1, 1:2], min_val=0, max_val=MAXOV)
            dve.wait_ge(rows_stored, n_blocks * 32)
            apart(dve)

            def combine(w, first):
                for t in range(NT):
                    n = first + t
                    s = n % 2
                    st = Steps(dve, add_steps, n, 2)
                    if n >= 2:
                        dve.wait_ge(add_steps, (n - 1) * 2)
                    for k in range(TOPK):
                        j = n * TOPK + k
                        wk = w[:, t * TOPK + k:t * TOPK + k + 1]
                        r = rows[j % NROWS]
                        dve.wait_ge(row_loaded[j % NROWS], 16 * (j // NROWS + 1))
                        if k == 0:
                            ins = nc.vector.tensor_scalar(acc[s][:], r[:], wk, None, ALU.mult)
                        else:
                            ins = nc.vector.scalar_tensor_tensor(acc[s][:], r[:], wk, acc[s][:], ALU.mult, ALU.add)
                        ins.then_inc(row_used, 1)
                        dve.wait_ge(row_used, j + 1)
                    st(nc.vector.tensor_tensor(acc[s][:], acc[s][:], g2[:], ALU.mult))
                    dve.wait_ge(res_loaded[s], 16 * (n // 2 + 1))
                    st(nc.vector.tensor_tensor(res[s][:], res[s][:], acc[s][:], ALU.add), False)
                    st.end()

            with dve.If(further > 0):
                combine(w_over, 0)
                combine(w_main, NT)
            with dve.Else():
                combine(w_main, 0)
            dve.nop()

        @block.tensor
        def _(pe):
            pe.wait_ge(c_wide_ready, 1)
            for i in range(12):
                bank = (pj0, pj1, pj2)[i % 3]
                pe.wait_ge(ada_loaded[i % 3], (i // 3 + 1) * 32)
                wait(pe, mod_taken[i % 3], i // 3)
                nc.tensor.matmul(bank[:], cst("ones", 1), b_row[i % 3][:], start=True, stop=False)
                if i % 3 == 2:
                    pe.wait_ge(fma_ready, i // 3 + 1)
                    nc.tensor.matmul(bank[:], cst("ones"), fma[:], start=False, stop=True).then_inc(mod_filled, 1)
                    continue
                for k in range(KT):
                    ins = nc.tensor.matmul(bank[:], c_wide[:, k, :], ada[i % 3][:, k, :], start=False, stop=(k == KT - 1))
                ins.then_inc(mod_filled, 1)
            pe.wait_ge(w_in_loaded, 16)
            pe.wait_ge(small_loaded, 11 * 16)

            def transpose_h(n):
                pe.wait_ge(h_steps, n * 6 + 6)
                wait(pe, qkT_a, n)
                wait(pe, qkT_b, n)
                wait(pe, yT_ready, n - 1)
                wait(pe, at_masked, (n - 1) * 4)
                for k in range(KT):
                    ins = nc.tensor.transpose((tr0, tr1)[k // 4][:, (k % 4) * P:(k % 4 + 1) * P],
                                              h[:, k * P:(k + 1) * P], ident)
                ins.then_inc(hT_filled, 1)

            def project(bank, col, width):
                for k in range(KT):
                    ins = nc.tensor.matmul(bank, hT[:, k, :], w_in[:, k, col:col + width],
                                           start=(k == 0), stop=(k == KT - 1))
                return ins

            def project_across(bank, col, width):
                for k in range(KT):
                    ins = nc.tensor.matmul(bank, w_in[:, k, col:col + width], hT[:, k, :],
                                           start=(k == 0), stop=(k == KT - 1))
                return ins

            def project_q(n):
                pe.wait_ge(hT_lo, n + 1)
                pe.wait_ge(hT_hi, n + 1)
                wait(pe, gv_ready, n)
                project(pj0[:], C_SQ, QW).then_inc(sq_filled, 1)

            def project_kv(n):
                wait(pe, gate_ready, n)
                project(pj1[:, 0:KW + VW], C_SK, KW + VW)
                project_across(pj1[0:RANK, 256:256 + P], C_LR, RANK).then_inc(skv_filled, 1)

            def transpose_qk(n):
                pe.wait_ge(qn_ready, n * 2 + 2)
                wait(pe, pv_a, n)
                for j in range(4):
                    nc.tensor.transpose(tr0[:, j * P:(j + 1) * P], qn[:, j * P:(j + 1) * P], ident)
                nc.tensor.transpose(sa[:, 0:P], qn[:, QW:], ident).then_inc(qk_filled, 1)

            def project_gqk(n):
                wait(pe, gqk_ready, n)
                for j in range(4):
                    ins = project_across(pj2[:, j * P:(j + 1) * P], C_GQ + j * P, P)
                ins.then_inc(gqk_filled, 1)

            def project_gv(n):
                pe.wait_ge(qn_ready, n * 2 + 2)
                project(pj0[:], C_GV, GVW).then_inc(gv_filled, 1)

            def project_og(n):
                pe.wait_ge(v_ready, n + 1)
                project(pj1[:], C_OG, GVW).then_inc(og_filled, 1)

            def forget(n):
                pe.wait_ge(skv_squared, n + 1)
                wait(pe, s0_ready, n)
                nc.tensor.matmul(s_b[:, 0:GKW], glrT[:], w_g2[:], start=True, stop=True).then_inc(z_filled, 1)

            def window_scores(m):
                pe.wait_ge(qkT_a, m + 1)
                pe.wait_ge(qkT_b, m + 1)
                pe.wait_ge(z_neg, m + 1)
                wait(pe, y_ready, m)
                for c in range(2):
                    for j in range(4):
                        ins = nc.tensor.matmul((sa, s_b)[c][:, j * P:(j + 1) * P],
                                               qT[:, c, 2 * j:2 * j + 2, :].rearrange("p h t -> p (h t)"),
                                               kTw[:, j // 2, c * CH:c * CH + P], start=True, stop=True)
                ins.then_inc(sc_filled, 1)

            def transpose_p(m):
                pe.wait_ge(p_norm, m + 1)
                for c in range(2):
                    for j in range(4):
                        ins = nc.tensor.transpose((sa, s_b)[c][:, j * P:(j + 1) * P], sc[:, c, j * P:(j + 1) * P], ident)
                ins.then_inc(pt_filled, 1)

            def window_values(m):
                pe.wait_ge(pt_a, m + 1)
                pe.wait_ge(pt_b, m + 1)
                pe.wait_ge(v_ready, m + 1)
                for c in range(2):
                    for kv in range(KVH):
                        ins = nc.tensor.matmul((sa, s_b)[c][0:HD, kv * 256:(kv + 1) * 256],
                                               (v_a, v_b)[c][:, kv * HD:(kv + 1) * HD],
                                               pT[:, c, kv * 256:(kv + 1) * 256], start=True, stop=True)
                ins.then_inc(pv_filled, 1)

            def decay_sums(m, c):
                pe.wait_ge(la_ready, m + 1)
                if c == 1:
                    pe.wait_ge(fac_ready, m * 2 + 1)
                nc.tensor.matmul(gb[:], la[:, c * P:(c + 1) * P], cst("steps")[:, 0:512], start=True, stop=True)
                nc.tensor.matmul(tr1[:, 0:3 * P], la[:, c * P:(c + 1) * P], cst("steps")[:, 512:NF * P],
                                 start=True, stop=True).then_inc(e_filled, 1)

            def transpose_kg(m):
                pe.wait_ge(qkf_ready, m * 2 + 2)
                for c in range(2):
                    ins = nc.tensor.transpose(tr0[:, c * P:(c + 1) * P], kf[:, c, 4, :], ident)
                ins.then_inc(kg_filled, 1)

            def linear_scores(m):
                pe.wait_ge(fac_ready, m * 2 + 2)
                for hd in range(GH):
                    c, lo = hd // 2, (hd % 2) * GK
                    if hd >= 2:
                        pe.wait_ge(at_masked, m * 4 + hd - 1)
                    for lv in range(4):
                        q_at = (2, 3, 4, 0)[lv]
                        ins = nc.tensor.matmul((gb, tr1)[hd % 2][:, lv * P:(lv + 1) * P],
                                               kf[lo:lo + GK, c, lv, :], qf[lo:lo + GK, c, q_at, :],
                                               start=True, stop=True)
                    ins.then_inc(at_filled, 1)

            def state_terms(m):
                pe.wait_ge(kg_ready, m + 1)
                pe.wait_ge(gv_ready, m + 1)
                pe.wait_ge(pv_b, m + 1)
                for c in range(2):
                    for chunk in range(2):
                        for hh in range(2):
                            ins = nc.tensor.matmul(
                                s_b[hh * GK:(hh + 1) * GK, (2 * c + chunk) * GV:(2 * c + chunk + 1) * GV],
                                kg[:, chunk, c, hh * GK:(hh + 1) * GK],
                                gv[:, (2 * c + hh) * GV:(2 * c + hh + 1) * GV],
                                start=True, stop=True)
                ins.then_inc(dl_filled, 1)

            def linear_out(m):
                pe.wait_ge(s1_ready, m + 1)
                pe.wait_ge(at_ready, m * 4 + 4)
                wait(pe, s0_ready, m)
                for hd in (0, 2, 1, 3):
                    if hd == 1:
                        ins.then_inc(even_filled, 1)
                        pe.wait_ge(even_filled, m + 1)
                    c, lo = hd // 2, (hd % 2) * GK
                    col = slice(hd * GV, (hd + 1) * GV)
                    nc.tensor.matmul(sa[:, col], at[:, hd, :], gv[:, col], start=True, stop=False, skip_group_check=True)
                    for chunk, state in enumerate((s0, s1)):
                        ins = nc.tensor.matmul(sa[chunk * CH:(chunk + 1) * CH, col],
                                               qf[lo:lo + GK, c, 1, chunk * CH:(chunk + 1) * CH],
                                               state[lo:lo + GK, c, :], start=False, stop=True, skip_group_check=True)
                ins.then_inc(o_filled, 1)

            def transpose_y(m):
                pe.wait_ge(y_ready, m + 1)
                for j in range(4):
                    ins = nc.tensor.transpose(tr0[:, j * P:(j + 1) * P], y[:, j * P:(j + 1) * P], ident)
                ins.then_inc(yt_filled, 1)

            def mixer_tile(m, more_tiles):
                n = m + 1
                if more_tiles:
                    transpose_h(n)
                window_scores(m)
                if more_tiles:
                    project_q(n)
                transpose_p(m)
                if more_tiles:
                    project_kv(n)
                window_values(m)
                decay_sums(m, 0)
                if more_tiles:
                    transpose_qk(n)
                    project_gqk(n)
                decay_sums(m, 1)
                transpose_kg(m)
                if more_tiles:
                    project_gv(n)
                linear_scores(m)
                state_terms(m)
                if not more_tiles:
                    pe.wait_ge(pv_a, m + 1)
                linear_out(m)
                if more_tiles:
                    project_og(n)
                    forget(n)
                transpose_y(m)

            transpose_h(0)
            project_q(0)
            project_kv(0)
            transpose_qk(0)
            project_gqk(0)
            project_gv(0)
            project_og(0)
            forget(0)
            mixer_tile(0, True)
            with pe.Fori(1, NT - 1) as m:
                mixer_tile(m, True)
            mixer_tile(NT - 1, False)

            def project_out(t, s):
                pe.wait_ge(yx_loaded[s], (t - s) * 16 + 32)
                if not (isinstance(t, int) and t < 2):
                    pe.wait_ge(x1_ready, t - 1)
                banks = ((pj0, pj1), (pj2, sa))[s]
                for half in range(2):
                    for k in range(KT):
                        ins = nc.tensor.matmul(banks[half][:], y_in[s][:, k, :], w_o[:, k, half * 512:(half + 1) * 512],
                                               start=(k == 0), stop=(k == KT - 1))
                ins.then_inc(wo_filled, 1)

            def router(t, s):
                pe.wait_ge(h2_ready, t + 1)
                for k in range(KT):
                    ins = nc.tensor.transpose((tr0, tr1)[k // 4][:, (k % 4) * P:(k % 4 + 1) * P],
                                              h2[s][:, k * P:(k + 1) * P], ident)
                ins.then_inc(h2t_filled, 1)
                pe.wait_ge(h2t_lo, t + 1)
                pe.wait_ge(h2t_hi, t + 1)
                wait(pe, lg_steps, t * 6 - 5)
                for k in range(KT):
                    ins = nc.tensor.matmul(gb[:, 0:NE], h2T[:, k, :], w_r[:, k, :], start=(k == 0), stop=(k == KT - 1))
                ins.then_inc(lg_filled, 1)

            pe.wait_ge(gv_ready, NT)
            pe.wait_ge(gate_ready, NT)
            pe.wait_ge(gqk_ready, NT)
            pe.wait_ge(y_ready, NT)
            pe.wait_ge(yT_ready, NT)
            pe.wait_ge(at_masked, NT * 4)
            pe.wait_ge(rt_loaded, 48)
            project_out(0, 0)
            project_out(1, 1)
            router(0, 0)
            with pe.Fori(1, NT // 2) as i:
                project_out(i * 2, 0)
                router(i * 2 - 1, 1)
                project_out(i * 2 + 1, 1)
                router(i * 2, 0)
            router(NT - 1, 1)
            pe.wait_ge(ct_steps, CHOSEN_AT)
            nc.tensor.matmul(pj0[:, 0:NT * NE], cst("before"), chosen[:].rearrange("p t e -> p (t e)"),
                             start=True, stop=False)
            nc.tensor.matmul(pj0[:, 0:NT * NE], cst("ones"), prior[:, 0:NT, :].rearrange("p t e -> p (t e)"),
                             start=False, stop=True)
            nc.tensor.matmul(pj1[:, 0:NE], cst("ones"), prior[:, NT, :], start=True, stop=True).then_inc(rank_filled, 1)

            m_banks = (pj0, pj1, pj2, sa)
            pe.wait_ge(slots_ready, 2)
            pe.wait_ge(bias_loaded, 48)
            for j in range(3):
                for k in range(KT):
                    ins = nc.tensor.transpose(m_banks[j][:, k * NE:(k + 1) * NE], b_rows[:, j, k * P:(k + 1) * P],
                                              ident[0:NE, 0:NE])
            ins.then_inc(bias_filled, 1)

            def split_ready(b, ci):
                on_pool = sum(1 for x in range(ci + 1) if x in POOL_CHUNKS)
                if ci in POOL_CHUNKS:
                    pe.wait_ge(lo_pool, b * len(POOL_CHUNKS) + on_pool)
                else:
                    pe.wait_ge(lo_dve, b * (NCH - len(POOL_CHUNKS)) + (ci + 1 - on_pool))

            def transpose_x(b, q):
                if q < 2:
                    pe.wait_ge(x_gathered, b * 32 + 32)
                    wait(pe, xt_lo, b * 4 + q - 2)
                else:
                    pe.wait_ge(xt_lo, b * 4 + q - 1)
                bank = (tr0, tr1)[q % 2]
                for kk in range(2):
                    k = 2 * q + kk
                    nc.tensor.transpose(bank[:, kk * CAP:kk * CAP + P], x_got[:, 0, k * P:(k + 1) * P], ident)
                    ins = nc.tensor.transpose(bank[:, kk * CAP + P:(kk + 1) * CAP],
                                              x_got[0:CAP2, 1, k * P:(k + 1) * P], ident[0:CAP2, 0:CAP2])
                ins.then_inc(xt_filled, 1)

            def bank_free(b, q):
                if 4 <= q < 20:
                    pe.wait_ge(up_taken, b * 16 + q - 3)
                elif q >= 20:
                    pe.wait_ge(down_taken, b * 8 + q - 19)
                elif not isinstance(b, int):
                    pe.wait_ge(down_taken, b * 8 + q - 3)

            def products(b, ci, moving, width, ks=range(KT)):
                if ks[0] == 0:
                    split_ready(b, ci)
                for f in range(WCOLS // P):
                    q = 2 * ci + f
                    if ks[0] == 0:
                        bank_free(b, q)
                    bank = m_banks[q % 4]
                    both = bank[:, 0:2 * CAP].rearrange("p (two t) -> p two t", two=2)[:, :, 0:width]
                    cols = slice(f * P, (f + 1) * P)
                    for k in ks:
                        nc.tensor.matmul(both, w_hi[ci % NHL][:, k, cols], moving[:, k, :, 0:width],
                                         start=(k == 0), stop=(k == KT - 1), skip_group_check=True)
                        ins = nc.tensor.matmul(bank[:, 0:width], w_lo[ci % NHL][:, k, cols], moving[:, k, 0, 0:width],
                                               start=False, stop=(k == KT - 1), skip_group_check=True)
                    if ks[-1] == KT - 1:
                        ins.then_inc(m_filled, 1)

            def transpose_rows(b, pair):
                pe.wait_ge(down_taken, b * 8 + 2 * pair + 2)
                if pair % 2 == 0:
                    wait(pe, y_taken, b * 2 + pair // 2)
                for f in range(2):
                    col = ((pair % 2) * 2 + f) * P
                    nc.tensor.transpose(s_b[:, col:col + P], yT2[:, pair, f, 0:P], ident)
                    ins = nc.tensor.transpose(gb[0:CAP2, col:col + P], yT2[:, pair, f, P:CAP], ident)
                ins.then_inc(yt2_filled, 1)

            def all_products(b, width, before=None):
                for ci in range(8):
                    products(b, ci, xT, width)
                    if ci < 2 and before is not None:
                        transpose_rows(before, 2 + ci)
                pe.wait_ge(act_lo, b * 4 + 3)
                products(b, 8, actT, width, range(KT - 2))
                products(b, 9, actT, width, range(KT - 2))
                pe.wait_ge(act_lo, b * 4 + 4)
                products(b, 8, actT, width, range(KT - 2, KT))
                transpose_x(b + 1, 0)
                transpose_x(b + 1, 1)
                products(b, 9, actT, width, range(KT - 2, KT))
                transpose_x(b + 1, 2)
                products(b, 10, actT, width)
                transpose_x(b + 1, 3)
                transpose_rows(b, 0)
                products(b, 11, actT, width)
                transpose_rows(b, 1)

            for q in range(4):
                transpose_x(0, q)
            n_blocks = pe.value_load(blocks[0:1, 0:1], min_val=NE, max_val=NE + MAXOV)
            pe.wait_ge(bias_ready, 1)
            pe.wait_ge(xt_lo, 4)
            all_products(0, CAP)
            with pe.Fori(1, n_blocks) as b:
                pe.wait_ge(xt_lo, b * 4 + 4)
                wide = pe.value_load(wide_of[0:1, bass.ds(b, 1)], min_val=0, max_val=1)
                with pe.If(wide > 0):
                    all_products(b, CAP, b - 1)
                with pe.Else():
                    all_products(b, NARROW, b - 1)
            last = pe.value_load(blocks[0:1, 2:3], min_val=NE - 1, max_val=NE + MAXOV - 1)
            transpose_rows(last, 2)
            transpose_rows(last, 3)


_INS = ["x", "c", "norm1_g", "w_ada", "b_ada", "w_in", "q_norm_g", "k_norm_g", "sinks", "w_gla_gate2",
        "b_gla_gate", "gla_norm_g", "w_out", "norm2_g", "w_router", "b_router", "w_gate", "b_gate", "w_up",
        "b_up", "w_down", "b_down"]


def kernel(**inputs):
    import concourse.bacc as bacc
    from concourse.bass_utils import run_bass_kernel_spmd

    nc = bacc.Bacc("TRN2", target_bir_lowering=False, num_devices=1)
    arrays, args = {}, {}
    for name in _INS:
        v = np.ascontiguousarray(inputs[name])
        arrays[f"in_{name}"] = v
        args[name] = nc.dram_tensor(f"in_{name}", v.shape, mybir.dt.from_np(v.dtype), kind="ExternalInput").ap()
    arrays["in_const"] = CONST
    args["const"] = nc.dram_tensor("in_const", CONST.shape, F32, kind="ExternalInput").ap()
    out = nc.dram_tensor("out_0", (1, T, D), F32, kind="ExternalOutput").ap()
    build(nc, args, out)
    r = run_bass_kernel_spmd(nc, [arrays], core_ids=[0])
    return r.results[0]["out_0"]
```

```python
import math
from contextlib import ExitStack

import numpy as np

import concourse.bass as bass
from concourse import mybir

F32 = mybir.dt.float32
F32R = mybir.dt.float32r
I32 = mybir.dt.int32
U32 = mybir.dt.uint32
ALU = mybir.AluOpType
ACT = mybir.ActivationFunctionType
AX_X = mybir.AxisListType.X

P = 128
D = 1024
T = 1024
KT = D // P
NT = T // P
CH = 64
QH, KVH, HD = 8, 2, 64
GH, GK, GV = 4, 64, 128
RANK = 16
QW, KW, VW = QH * HD, KVH * HD, KVH * HD
GKW, GVW = GH * GK, GH * GV
C_SQ = 0
C_SK = C_SQ + QW
C_GQ = C_SK + KW + VW
C_GV = C_GQ + 2 * GKW
C_LR = C_GV + GVW
C_OG = C_LR + RANK
W_IN = C_OG + GVW
TAU = 16.0
EPS = 1e-6
NE, TOPK = 32, 4
LIMIT, ALPHA = 7.0, 1.702
NEG = -1.0e30

CAP = 192
CAP2 = CAP - P
MAXJ = (T - 1) // CAP
MAXOV = (T * TOPK) // CAP
MAIN = NE * CAP
SLOTS = (NE + MAXOV) * CAP
LOOKED_UP = SLOTS + CAP
TABLE = LOOKED_UP + P * TOPK

NF = 7

WCOLS = 256
NCH = 3 * D // WCOLS
NRAW, NHL = 6, 4
LEAD = 3
assert 8 + LEAD == NCH - 1
POOL_CHUNKS = (1, 4, 7, 10)
ACOLS = 512
NA = 6 * D // ACOLS
EARLY = 5
EARLY_TAKEN = [len(range(s, EARLY, 3)) for s in range(3)]
assert NA - EARLY == NT - 1
WIDTHS = (136, 160, CAP)
NROWS = 4
CHOOSE, PLACE = 8, 7
assert TABLE % P == 0
LEVELS = (32, 16, 8)
BASE = 8


def constants():
    u = np.arange(P)[:, None]
    t = np.arange(P)[None, :]
    same = lambda b: (u // b) == (t // b)
    mid = BASE * (t // BASE) + BASE // 2 - 1
    base_q = ((u > mid) & (u <= t)).astype(np.float32) - ((u > t) & (u <= mid)).astype(np.float32)
    e = [base_q, (same(CH) & (u <= t)).astype(np.float32)]
    for b in LEVELS:
        bound = 2 * b * (t // (2 * b)) + b - 1
        e.append((((u > bound) & (u <= t)) | ((u > t) & (u <= bound))).astype(np.float32))
    e += [-base_q, (same(CH) & (u > t)).astype(np.float32)]
    steps = np.stack(e, 1) / TAU
    mask = [same(2 * b) & (u % (2 * b) < b) & (t % (2 * b) >= b) for b in LEVELS]
    mask = np.stack(mask + [same(BASE) & (u <= t)], 1).astype(np.float32)
    slopes = 2.0 ** (-8.0 * np.arange(1, QH + 1, dtype=np.float32) / QH)
    a = np.arange(CH)[:, None]
    j = np.arange(2 * CH)[None, :]
    dist = np.abs(CH + a - j).astype(np.float32)
    alibi = (-slopes[:, None, None] * dist).reshape(QH // 2, P, P).transpose(1, 0, 2)
    parts = {
        "ident": np.eye(P, dtype=np.float32),
        "ones": np.ones((P, P), np.float32),
        "before": (u < t).astype(np.float32),
        "steps": steps.reshape(P, NF * P),
        "mask": mask.reshape(P, 4 * P),
        "alibi": alibi.reshape(P, 4 * P),
        "experts": np.tile(np.arange(NE, dtype=np.float32), (P, 1)),
        "slot0": np.tile(np.arange(NE, dtype=np.float32) * CAP, (P, 1)),
        "over": np.tile(np.repeat(np.arange(MAXOV, dtype=np.float32), NE), (P, 1)),
        "token": (np.arange(NT)[None, :] * P + np.arange(P)[:, None]).astype(np.float32),
        "unread": (LOOKED_UP + np.arange(P * TOPK).reshape(P, TOPK)).astype(np.float32),
        "minus_half": np.full((P, 1), -0.5, np.float32),
    }
    where, at = {}, 0
    for name, v in parts.items():
        where[name] = (at, v.shape[1])
        at += v.shape[1]
    return np.ascontiguousarray(np.concatenate(list(parts.values()), 1), dtype=np.float32), where


CONST, CONST_AT = constants()


def chunk_of(ci):
    return (2, ci - 8) if ci >= 8 else (ci % 2, ci // 2)


def wait(eng, sem, value):
    if isinstance(value, int) and value <= 0:
        return
    eng.wait_ge(sem, value)


class Steps:

    def __init__(self, eng, sem, tile, count):
        self.eng, self.sem, self.base, self.count, self.n = eng, sem, tile * count, count, 0

    def __call__(self, instruction, then_wait=True):
        instruction.then_inc(self.sem, 1)
        self.n += 1
        if then_wait:
            self.eng.wait_ge(self.sem, self.base + self.n)

    def end(self):
        assert self.n == self.count, (self.n, self.count)



def build(nc, a, out):
    ctx = ExitStack()
    with ctx:
        def sem(name):
            return ctx.enter_context(nc.semaphore(name))

        def sb(stack, name, shape, dt=F32):
            return stack.enter_context(nc.sbuf_tensor(name, shape, dt))

        y_dram = nc.dram_tensor("y_dram", [NT, P, KT * P], F32, kind="Internal").ap()
        x1_dram = nc.dram_tensor("x1_dram", [T, D], F32, kind="Internal").ap()
        h2_dram = nc.dram_tensor("h2_dram", [T, D], F32, kind="Internal").ap()
        slot_dram = nc.dram_tensor("slot_dram", [TABLE, 1], I32, kind="Internal").ap()
        rows_dram = nc.dram_tensor("rows_dram", [SLOTS, D], F32, kind="Internal").ap()

        tr0, tr1, pj0, pj1, pj2, sa, s_b, gb = [
            ctx.enter_context(nc.psum_tensor(n, [P, 512], F32))
            for n in ("tr0", "tr1", "pj0", "pj1", "pj2", "sa", "s_b", "gb")]

        const = sb(ctx, "const", [P, CONST.shape[1]])
        late = sb(ctx, "late", [P, 8, ACOLS])
        onehot = sb(ctx, "onehot", [P, NT, TOPK, NE])
        weights = sb(ctx, "weights", [P, NT, TOPK])
        slot_all = sb(ctx, "slot_all", [P, NT * TOPK], I32)
        slot_main = sb(ctx, "slot_main", [P, NT * TOPK], I32)
        slot_over = sb(ctx, "slot_over", [P, NT * TOPK], I32)
        w_main = sb(ctx, "w_main", [P, NT * TOPK])
        w_over = sb(ctx, "w_over", [P, NT * TOPK])
        blocks = sb(ctx, "blocks", [1, 3], I32)
        token_i = sb(ctx, "token_i", [P, NT], I32)
        now_i = sb(ctx, "now_i", [P, TOPK], I32)
        now_token = sb(ctx, "now_token", [P, 1], I32)
        expert_of = sb(ctx, "expert_of", [1, NE + MAXOV], I32)
        wide_of = sb(ctx, "wide_of", [1, NE + MAXOV], I32)

        def cst(name, rows=P):
            at, n = CONST_AT[name]
            return const[0:rows, at:at + n]

        ident = cst("ident")

        mix = ExitStack()
        sh1 = sb(mix, "sh1", [P, D])
        gs1 = sb(mix, "gs1", [P, D])
        g1, sh2, gs2, g2 = [late[:, 2 * i:2 * i + 2, :].rearrange("p a n -> p (a n)") for i in range(4)]
        c_act = sb(mix, "c_act", [P, KT])
        early = ExitStack()
        w_in = sb(early, "w_in_sb", [P, KT, W_IN])
        part_a = ExitStack()
        c_col = sb(part_a, "c_col", [P, KT])
        c_exp = sb(part_a, "c_exp", [P, KT])
        c_wide = sb(part_a, "c_wide", [P, KT, P])
        n1_wide = sb(part_a, "n1_wide", [P, D])
        b_row = [sb(part_a, f"b_row{i}", [1, 512]) for i in range(3)]
        ada = [sb(part_a, f"ada{i}", [P, KT, 512]) for i in range(3)]
        fma = sb(part_a, "fma", [P, 512])
        part_a.close()
        x_in = sb(early, "x_in", [P, D])
        h = sb(early, "h", [P, D])
        ssx = sb(early, "ssx", [P, 2])
        hT = sb(early, "hT", [P, KT, P])
        qn = sb(early, "qn", [P, QW + KW])
        ssq = sb(early, "ssq", [P, QH + KVH])
        rq = sb(early, "rq", [P, QH + KVH])
        qk_g = sb(early, "qk_g", [P, 2])
        qT = sb(early, "qT", [HD, 2, QH, CH])
        kTw = sb(early, "kTw", [HD, KVH, CH + P])
        v_a = sb(early, "v_a", [P, VW])
        v_b = sb(early, "v_b", [P, VW])
        sc = sb(early, "sc", [P, 2, 512])
        stat = sb(early, "stat", [P, 6, 8])
        sink = sb(early, "sink", [P, 8])
        pT = sb(early, "pT", [P, 2, 512])
        alibi_a = sb(early, "alibi_a", [P, 512])
        yT = sb(early, "yT", [P, KT, P])
        gqk = sb(early, "gqk", [P, 4, P])
        fac = sb(early, "fac", [P, NF, P])
        sqs = sb(early, "sqs", [P, QW + KW])
        qf = sb(early, "qf", [P, 2, 5, P])
        kf = sb(early, "kf", [P, 2, 5, P])
        dec = sb(early, "dec", [P, 2, 2])
        at = sb(early, "at", [P, GH, P])
        kg = sb(early, "kg", [P, 2, 2, P])
        gv = sb(early, "gv", [P, GVW])
        gate = sb(early, "gate", [P, GVW])
        ge = sb(early, "ge", [P, GVW])
        y = sb(early, "y", [P, GVW])
        osq = sb(early, "osq", [P, GVW])
        sso = sb(early, "sso", [P, GH])
        ro = sb(early, "ro", [P, GH])
        s0 = sb(early, "s0", [P, 2, GV])
        s1 = sb(early, "s1", [P, 2, GV])
        la = sb(early, "la", [P, GKW])
        zb = sb(early, "zb", [P, GKW])
        zt = sb(early, "zt", [P, GKW])
        glrT = sb(early, "glrT", [RANK, P])
        w_g2 = sb(early, "w_g2", [RANK, GKW])
        bg_wide = sb(early, "bg_wide", [P, GKW])
        gn_wide = sb(early, "gn_wide", [P, GV])
        ada_late = sb(early, "ada_late", [P, KT, ACOLS])
        b_row_late = sb(early, "b_row_late", [1, ACOLS])
        early.close()
        w_o = sb(mix, "w_o", [P, KT, D])
        y_in = [sb(mix, f"y_in{i}", [P, KT, P]) for i in range(2)]
        x_res = [sb(mix, f"x_res{i}", [P, D]) for i in range(2)]
        h2 = [sb(mix, f"h2_{i}", [P, D]) for i in range(2)]
        h2T = sb(mix, "h2T", [P, KT, P])
        w_r = sb(mix, "w_r", [P, KT, NE])
        n2_wide = sb(mix, "n2_wide", [P, D])
        br_wide = sb(mix, "br_wide", [P, NE])
        ss2 = sb(mix, "ss2", [P, 2])
        lg = sb(mix, "lg", [P, NE])
        top = sb(mix, "top", [P, 8])
        topi = sb(mix, "topi", [P, 8], U32)
        topf = sb(mix, "topf", [P, 4])
        tope = sb(mix, "tope", [P, 4])
        tops = sb(mix, "tops", [P, 2])
        zero_i = sb(mix, "zero_i", [P, TABLE // P], I32)
        chosen = sb(mix, "chosen", [P, NT, NE])
        prior = sb(mix, "prior", [P, NT + 1, NE])
        slotmap = sb(mix, "slotmap", [P, NT, NE])
        far = sb(mix, "far", [P, NT, NE])
        count = sb(mix, "count", [P, NE])
        more = sb(mix, "more", [P, MAXJ, NE])
        incl = sb(mix, "incl", [P, NE])
        base2 = sb(mix, "base2", [P, 2, NE])
        picked = sb(mix, "picked", [P, NT * TOPK, NE])
        slotf = sb(mix, "slotf", [P, 4, NT * TOPK])
        now = sb(mix, "now", [P, 2, NE])
        now_picked = sb(mix, "now_picked", [P, TOPK, NE])
        now_slot = sb(mix, "now_slot", [P, TOPK])
        ovf = sb(mix, "ovf", [1, MAXOV, NE])
        ovs = sb(mix, "ovs", [1, MAXOV])
        mix.close()

        part_d = ExitStack()
        b_cols = sb(part_d, "b_cols", [P, 3, KT, NE])
        b_now = sb(part_d, "b_now", [P, 3, KT])
        slot_ids = sb(part_d, "slot_ids", [P, 2], I32)
        x_got = sb(part_d, "x_got", [P, 2, D])
        xT = sb(part_d, "xT", [P, KT, 2, CAP], F32R)
        g_sb = sb(part_d, "g_sb", [P, 2, CAP])
        u_sb = sb(part_d, "u_sb", [P, 2, CAP])
        sg_sb = sb(part_d, "sg_sb", [P, 2, CAP])
        av_sb = sb(part_d, "av_sb", [P, 2, CAP])
        actT = sb(part_d, "actT", [P, KT, 2, CAP], F32R)
        yT2 = sb(part_d, "yT2", [P, 4, 2, CAP])
        y_out = sb(part_d, "y_out", [P, 2, D])
        start_d = ExitStack()
        b_rows = sb(start_d, "b_rows", [NE, 3, D])
        start_d.close()
        w_hi, w_lo = [[sb(part_d, f"{n}{i}", [P, KT, WCOLS], F32R) for i in reversed(range(NHL))][::-1]
                      for n in ("w_hi", "w_lo")]
        raw = [sb(part_d, f"raw{i}", [P, KT, WCOLS]) for i in range(NRAW)]
        part_d.close()
        part_e = ExitStack()
        rows = [sb(part_e, f"rows{i}", [P, D]) for i in range(NROWS)]
        res = [sb(part_e, f"res{i}", [P, D]) for i in range(2)]
        acc = [sb(part_e, f"acc{i}", [P, D]) for i in range(2)]
        part_e.close()

        c_loaded, const_loaded, norms_loaded = sem("c_loaded"), sem("const_loaded"), sem("norms_loaded")
        ada_loaded = [sem(f"ada_loaded{i}") for i in range(3)]
        c_exp_ready, c_steps, c_wide_ready = sem("c_exp_ready"), sem("c_steps"), sem("c_wide_ready")
        fma_steps, fma_ready = sem("fma_steps"), sem("fma_ready")
        mod_filled = sem("mod_filled")
        mod_taken = [sem(f"mod_taken{i}") for i in range(3)]
        w_in_loaded, small_loaded, x_loaded = sem("w_in_loaded"), sem("small_loaded"), sem("x_loaded")
        init_ready = sem("init_ready")
        h_steps = sem("h_steps")
        hT_filled, hT_lo, hT_hi = sem("hT_filled"), sem("hT_lo"), sem("hT_hi")
        sq_filled, sq_squared, skv_filled, skv_squared = sem("sq_filled"), sem("sq_squared"), sem("skv_filled"), sem("skv_squared")
        ss_ready, rq_steps, rq_ready, qn_ready = sem("ss_ready"), sem("rq_steps"), sem("rq_ready"), sem("qn_ready")
        v_steps, v_ready = sem("v_steps"), sem("v_ready")
        qk_filled, k_moved, qkT_a, qkT_b = sem("qk_filled"), sem("k_moved"), sem("qkT_a"), sem("qkT_b")
        sc_filled, soft_steps, max_ready, p_ready, den_steps, p_norm = (
            sem("sc_filled"), sem("soft_steps"), sem("max_ready"), sem("p_ready"), sem("den_steps"), sem("p_norm"))
        pt_filled, pt_a, pt_b, pv_filled, pv_a, pv_b = (
            sem("pt_filled"), sem("pt_a"), sem("pt_b"), sem("pv_filled"), sem("pv_a"), sem("pv_b"))
        gqk_filled, gqk_ready, gv_filled, gv_ready = sem("gqk_filled"), sem("gqk_ready"), sem("gv_filled"), sem("gv_ready")
        og_filled, ge_ready, gate_steps, gate_ready = sem("og_filled"), sem("ge_ready"), sem("gate_steps"), sem("gate_ready")
        z_filled, z_steps, z_neg, zl_steps, zl_ready, la_ready = (
            sem("z_filled"), sem("z_steps"), sem("z_neg"), sem("zl_steps"), sem("zl_ready"), sem("la_ready"))
        e_filled, fac_ready, qkf_ready = sem("e_filled"), sem("fac_ready"), sem("qkf_ready")
        kg_filled, kg_ready = sem("kg_filled"), sem("kg_ready")
        at_filled, at_masked, at_ready = sem("at_filled"), sem("at_masked"), sem("at_ready")
        dl_filled, s1_ready, s0_ready = sem("dl_filled"), sem("s1_ready"), sem("s0_ready")
        even_filled, o_filled, so_ready, ro_steps, ro_ready, y_ready = (
            sem("even_filled"), sem("o_filled"), sem("so_ready"), sem("ro_steps"), sem("ro_ready"), sem("y_ready"))
        yt_filled, yT_ready, y_stored = sem("yt_filled"), sem("yT_ready"), sem("y_stored")
        rt_loaded = sem("rt_loaded")
        yx_loaded = [sem(f"yx_loaded{i}") for i in range(2)]
        wo_filled, x1_steps, x1_ready = sem("wo_filled"), sem("x1_steps"), sem("x1_ready")
        ss2_ready, r2_steps, r2_ready = sem("ss2_ready"), sem("r2_steps"), sem("r2_ready")
        h2_steps, h2_ready = sem("h2_steps"), sem("h2_ready")
        c_stored = [sem(f"c_stored{i}") for i in range(2)]
        h2t_filled, h2t_lo, h2t_hi, lg_filled = sem("h2t_filled"), sem("h2t_lo"), sem("h2t_hi"), sem("lg_filled")
        lg_steps, top_ready, tope_ready = sem("lg_steps"), sem("top_ready"), sem("tope_ready")
        table_zero, table_cleared, ct_steps, rank_filled = (
            sem("table_zero"), sem("table_cleared"), sem("ct_steps"), sem("rank_filled"))
        tail_filled, ranked, slots_now = sem("tail_filled"), sem("ranked"), sem("slots_now")
        slots_ready, table_written = sem("slots_ready"), sem("table_written")
        bias_loaded, bias_filled, bias_ready = sem("bias_loaded"), sem("bias_filled"), sem("bias_ready")
        raw_loaded = [sem(f"raw_loaded{i}") for i in range(NRAW)]
        hi_ready, lo_dve, lo_pool = sem("hi_ready"), sem("lo_dve"), sem("lo_pool")
        ids_loaded, x_gathered = sem("ids_loaded"), sem("x_gathered")
        xt_filled, xt_hi, xt_lo = sem("xt_filled"), sem("xt_hi"), sem("xt_lo")
        b_now_ready = sem("b_now_ready")
        m_filled, up_right, up_taken, down_right, down_taken = (
            sem("m_filled"), sem("up_right"), sem("up_taken"), sem("down_right"), sem("down_taken"))
        g_clipped, u_clipped, sig_ready, gs_ready, av_ready, act_hi, act_lo = (
            sem("g_clipped"), sem("u_clipped"), sem("sig_ready"), sem("gs_ready"), sem("av_ready"), sem("act_hi"), sem("act_lo"))
        yt2_filled, y_taken, rows_stored = sem("yt2_filled"), sem("y_taken"), sem("rows_stored")
        row_loaded = [sem(f"row_loaded{i}") for i in range(NROWS)]
        res_loaded = [sem(f"res_loaded{i}") for i in range(2)]
        add_steps, row_used = sem("add_steps"), sem("row_used")
        out_stored = [sem(f"out_stored{i}") for i in range(2)]
        passed = sem("passed")

        block = ctx.enter_context(nc.Block())

        def apart(eng):
            eng.sem_inc(passed, 1)

        @block.sync
        def _(sp):
            sp.dma_start(c_col[:], a["c"].rearrange("b (k p) -> p (b k)", p=P),
                         allow_slow_non_contiguous=True).then_inc(c_loaded, 16)
            sp.dma_start(const[:], a["const"]).then_inc(const_loaded, 16)
            w_ada = a["w_ada"][0].rearrange("(k p) n -> p k n", p=P)
            for i in range(EARLY):
                s = i % 3
                if i >= 3:
                    sp.wait_ge(mod_filled, i - 2)
                sp.dma_start(ada[s][:], w_ada[:, :, i * 512:(i + 1) * 512]).then_inc(ada_loaded[s], 16)
                sp.dma_start(b_row[s][:], a["b_ada"][:, i * 512:(i + 1) * 512]).then_inc(ada_loaded[s], 16)
                if i == 1:
                    sp.dma_start(n1_wide[:], a["norm1_g"].broadcast_to([P, D])).then_inc(norms_loaded, 16)
            sp.dma_start(w_in[:], a["w_in"][0].rearrange("(k p) n -> p k n", p=P)).then_inc(w_in_loaded, 16)
            for s in range(3):
                sp.wait_ge(mod_taken[s], EARLY_TAKEN[s])
            sp.dma_start(x_in[:], a["x"][0, 0:P, :]).then_inc(x_loaded, 16)
            sp.dma_start(w_g2[:], a["w_gla_gate2"][0]).then_inc(small_loaded, 16)
            sp.dma_start(bg_wide[:], a["b_gla_gate"].broadcast_to([P, GKW])).then_inc(small_loaded, 16)
            sp.dma_start(gn_wide[:], a["gla_norm_g"].broadcast_to([P, GV])).then_inc(small_loaded, 16)
            for half in range(2):
                lo, hi = half * HD, half * HD + HD
                sp.dma_start(qk_g[lo:hi, 0:1], a["q_norm_g"].rearrange("a d -> d a"),
                             allow_slow_non_contiguous=True).then_inc(small_loaded, 16)
                sp.dma_start(qk_g[lo:hi, 1:2], a["k_norm_g"].rearrange("a d -> d a"),
                             allow_slow_non_contiguous=True).then_inc(small_loaded, 16)
                for chunk in range(2):
                    sp.dma_start(sink[lo:hi, 4 * chunk:4 * chunk + 4],
                                 a["sinks"].rearrange("a (j two) -> a two j", two=2)[:, half, :].broadcast_to([CH, 4]),
                                 allow_slow_non_contiguous=True).then_inc(small_loaded, 16)

            def load_x(n):
                sp.wait_ge(h_steps, n * 6 - 2)
                sp.dma_start(x_in[:], a["x"][0, bass.ds(n * P, P), :]).then_inc(x_loaded, 16)

            def store_y(m):
                sp.wait_ge(pv_a, m + 1)
                sp.wait_ge(pv_b, m + 1)
                sp.wait_ge(yT_ready, m + 1)
                sp.dma_start(y_dram[bass.ds(m, 1)].rearrange("a p n -> (a p) n"),
                             yT[:].rearrange("p k t -> p (k t)")).then_inc(y_stored, 16)

            def load_late(j):
                wait(sp, mod_filled, EARLY + j if not isinstance(j, int) or j else 0)
                sp.dma_start(ada_late[:], w_ada[:, :, bass.ds(j * ACOLS + EARLY * ACOLS, ACOLS)]).then_inc(ada_loaded[0], 16)
                sp.dma_start(b_row_late[:], a["b_ada"][:, bass.ds(j * ACOLS + EARLY * ACOLS, ACOLS)]).then_inc(ada_loaded[0], 16)

            load_x(1)
            load_late(0)
            load_x(2)
            with sp.Fori(0, NT - 3) as m:
                load_x(m + 3)
                store_y(m)
                load_late(m + 1)
            store_y(NT - 3)
            load_late(NT - 2)
            sp.wait_ge(og_filled, NT)
            sp.wait_ge(z_filled, NT)
            sp.dma_start(w_o[:], a["w_out"][0].rearrange("(k p) n -> p k n", p=P)).then_inc(rt_loaded, 16)
            sp.dma_start(w_r[:], a["w_router"][0].rearrange("(k p) e -> p k e", p=P)).then_inc(rt_loaded, 16)
            sp.dma_start(br_wide[:], a["b_router"].broadcast_to([P, NE])).then_inc(rt_loaded, 16)
            sp.dma_start(n2_wide[:], a["norm2_g"].broadcast_to([P, D])).then_inc(rt_loaded, 16)

            def load_c(t, s):
                sp.dma_start(y_in[s][:].rearrange("p k t -> p (k t)"),
                             y_dram[bass.ds(t, 1)].rearrange("a p n -> (a p) n")).then_inc(yx_loaded[s], 16)
                sp.dma_start(x_res[s][:], a["x"][0, bass.ds(t * P, P), :]).then_inc(yx_loaded[s], 16)

            store_y(NT - 2)
            sp.wait_ge(y_stored, 16 * (NT - 1))
            load_c(0, 0)
            load_c(1, 1)
            store_y(NT - 1)
            w_of = [a["w_gate"][0], a["w_up"][0], a["w_down"][0]]
            last_b = [(la_ready, NT), (y_ready, NT), (s0_ready, NT)]

            def load_w(e, b, ci):
                which, c = chunk_of(ci)
                s = ci % NRAW
                g = b * NCH + ci - NRAW + 1
                if not (isinstance(g, int) and g <= 0):
                    wait_split(sp, b, ci - NRAW, g)
                src = w_of[which]
                src = src[bass.ds(e, 1)].rearrange("a (k p) n -> p (a k) n", p=P)
                sp.dma_start(raw[s][:], src[:, :, c * WCOLS:(c + 1) * WCOLS]).then_inc(raw_loaded[s], 16)

            def wait_split(eng, b, ci, g):
                eng.wait_ge(hi_ready, g)
                apart(eng)
                bb, cc = (b, ci) if ci >= 0 else (b - 1, ci + NCH)
                on_pool = sum(1 for x in range(cc + 1) if x in POOL_CHUNKS)
                pool_count = bb * len(POOL_CHUNKS) + on_pool
                dve_count = bb * (NCH - len(POOL_CHUNKS)) + (cc + 1 - on_pool)
                if cc in POOL_CHUNKS:
                    eng.wait_ge(lo_pool, pool_count)
                else:
                    eng.wait_ge(lo_dve, dve_count)

            sp.wait_ge(y_stored, 16 * NT)

            def store_c(t, s):
                sp.wait_ge(x1_ready, t + 1)
                sp.dma_start(x1_dram[bass.ds(t * P, P), :], x_res[s][:]).then_inc(c_stored[s], 16)
                sp.wait_ge(h2_ready, t + 1)
                sp.dma_start(h2_dram[bass.ds(t * P, P), :], h2[s][:]).then_inc(c_stored[s], 16)

            with sp.Fori(0, NT // 2 - 1) as i:
                for s in range(2):
                    store_c(i * 2 + s, s)
                    sp.wait_ge(c_stored[s], i * 32 + 32)
                    load_c(i * 2 + s + 2, s)
            for sm, v in last_b:
                sp.wait_ge(sm, v)
            for ci in range(NRAW):
                load_w(0, 0, ci)
            for s in range(2):
                store_c(NT - 2 + s, s)
            sp.wait_ge(slots_ready, 1)
            for s in range(2):
                sp.wait_ge(c_stored[s], 16 * NT)
            for j, name in enumerate(("b_gate", "b_up", "b_down")):
                sp.dma_start(b_rows[:, j, :], a[name][0]).then_inc(bias_loaded, 16)
            for ci in range(NRAW, NCH):
                load_w(0, 0, ci)
            with sp.Fori(1, NE) as b:
                for ci in range(NCH):
                    load_w(b, b, ci)
            sp.wait_ge(slots_ready, 2)
            further = sp.value_load(blocks[0:1, 1:2], min_val=0, max_val=MAXOV)
            with sp.If(further > 0):
                total = sp.value_load(blocks[0:1, 0:1], min_val=NE + 1, max_val=NE + MAXOV)
                with sp.Fori(NE, total) as b:
                    e = sp.value_load(expert_of[0:1, bass.ds(b, 1)], min_val=0, max_val=NE - 1)
                    for ci in range(NCH):
                        load_w(e, b, ci)
            with sp.Else():
                sp.nop()
            def residuals(dst, first):
                for t in range(NT):
                    s = t % 2
                    n = first + t
                    if n >= 2:
                        sp.wait_ge(out_stored[s], 16 * (n // 2))
                    sp.dma_start(res[s][:], x1_dram[t * P:(t + 1) * P, :]).then_inc(res_loaded[s], 16)
                    if t >= 1:
                        sp.wait_ge(add_steps, 2 * n)
                        sp.dma_start(dst[(t - 1) * P:t * P, :], res[1 - s][:]).then_inc(out_stored[1 - s], 16)
                sp.wait_ge(add_steps, 2 * (first + NT))
                sp.dma_start(dst[(NT - 1) * P:, :], res[1][:]).then_inc(out_stored[1], 16)

            def after_experts():
                n_blocks = sp.value_load(blocks[0:1, 0:1], min_val=NE, max_val=NE + MAXOV)
                sp.wait_ge(rows_stored, n_blocks * 32)
                sp.wait_ge(xt_hi, n_blocks * 4 + 4)
                sp.wait_ge(xt_lo, n_blocks * 4 + 4)
                apart(sp)
            after_experts()
            with sp.If(further > 0):
                residuals(x1_dram, 0)
                for s in range(2):
                    sp.wait_ge(out_stored[s], 16 * (NT // 2))
                residuals(out[0], NT)
                for s in range(2):
                    sp.wait_ge(out_stored[s], 16 * NT)
            with sp.Else():
                residuals(out[0], 0)
                for s in range(2):
                    sp.wait_ge(out_stored[s], 16 * (NT // 2))
            sp.nop()

        @block.gpsimd
        def _(pool):
            for s in range(3):
                pool.wait_ge(mod_taken[s], EARLY_TAKEN[s])

            def norm_in(n):
                st = Steps(pool, h_steps, n, 6)
                st.n = 1
                pool.wait_ge(h_steps, n * 6 + 1)
                apart(pool)
                st(nc.gpsimd.tensor_scalar(ssx[:, 0:1], ssx[:, 0:1], 1.0 / D, EPS, ALU.mult, ALU.add))
                st(nc.gpsimd.tensor_tensor(ssx[:, 1:2], ssx[:, 0:1], cst("minus_half"), ALU.pow))
                apart(pool)
                st(nc.gpsimd.tensor_scalar(h[:], x_in[:], ssx[:, 1:2], None, ALU.mult))
                st(nc.gpsimd.tensor_tensor(h[:], h[:], gs1[:], ALU.mult))
                st(nc.gpsimd.tensor_tensor(h[:], h[:], sh1[:], ALU.add))
                st.end()

            def rq_pow(n):
                st = Steps(pool, rq_steps, n, 1)
                pool.wait_ge(ss_ready, n * 2 + 2)
                apart(pool)
                st(nc.gpsimd.tensor_scalar(rq[:], ssq[:], 1.0 / HD, EPS, ALU.mult, ALU.add))
                nc.gpsimd.tensor_tensor(rq[:], rq[:], cst("minus_half").broadcast_to([P, QH + KVH]), ALU.pow).then_inc(rq_ready, 1)
                st.end()

            def ro_pow(m):
                st = Steps(pool, ro_steps, m, 1)
                pool.wait_ge(so_ready, m + 1)
                apart(pool)
                st(nc.gpsimd.tensor_scalar(ro[:], sso[:], 1.0 / GV, EPS, ALU.mult, ALU.add))
                nc.gpsimd.tensor_tensor(ro[:], ro[:], cst("minus_half").broadcast_to([P, GH]), ALU.pow).then_inc(ro_ready, 1)
                st.end()

            norm_in(0)
            rq_pow(0)
            norm_in(1)
            with pool.Fori(0, NT - 2) as m:
                rq_pow(m + 1)
                norm_in(m + 2)
                ro_pow(m)
            rq_pow(NT - 1)
            ro_pow(NT - 2)
            ro_pow(NT - 1)

            def r2_pow(t):
                st = Steps(pool, r2_steps, t, 1)
                pool.wait_ge(ss2_ready, t + 1)
                apart(pool)
                st(nc.gpsimd.tensor_scalar(ss2[:, 0:1], ss2[:, 0:1], 1.0 / D, EPS, ALU.mult, ALU.add))
                nc.gpsimd.tensor_tensor(ss2[:, 1:2], ss2[:, 0:1], cst("minus_half"), ALU.pow).then_inc(r2_ready, 1)
                st.end()

            pool.wait_ge(wo_filled, 1)
            nc.gpsimd.memset(zero_i[:], 0).then_inc(table_zero, 1)
            pool.wait_ge(table_zero, 1)
            table = slot_dram.rearrange("(p n) a -> p (n a)", p=P)
            pool.dma_start(table[0:CH, :], zero_i[0:CH, :]).then_inc(table_cleared, 16)
            pool.dma_start(table[CH:, :], zero_i[CH:, :]).then_inc(table_written, 16)
            pool.wait_ge(table_cleared, 16)
            pool.wait_ge(table_written, 16)

            def place(t):
                pool.wait_ge(slots_now, t + 1)
                apart(pool)
                for k in range(TOPK):
                    nc.gpsimd.indirect_dma_start(slot_dram, bass.IndirectOffsetOnAxis(now_i[:, k:k + 1], 0),
                                                 now_token[:], None).then_inc(table_written, 16)

            for t in range(3):
                r2_pow(t)
            with pool.Fori(3, NT) as t:
                r2_pow(t)
                place(t - 3)
            for t in range(NT - 3, NT):
                place(t)
            pool.wait_ge(table_written, 16 + 16 * NT * TOPK)
            for s in range(2):
                pool.wait_ge(c_stored[s], 16 * NT)

            def load_ids(b):
                wait(pool, x_gathered, b * 32)
                pool.dma_start(slot_ids[:, 0:1], slot_dram[bass.ds(b * CAP, P), :]).then_inc(ids_loaded, 16)
                pool.dma_start(slot_ids[0:CAP2, 1:2], slot_dram[bass.ds(b * CAP + P, CAP2), :]).then_inc(ids_loaded, 16)

            def gather(b):
                pool.wait_ge(ids_loaded, b * 32 + 32)
                wait(pool, xt_filled, b * 4)
                apart(pool)
                nc.gpsimd.indirect_dma_start(x_got[:, 0, :], None, h2_dram,
                                             bass.IndirectOffsetOnAxis(slot_ids[:, 0:1], 0)).then_inc(x_gathered, 16)
                nc.gpsimd.indirect_dma_start(x_got[0:CAP2, 1, :], None, h2_dram,
                                             bass.IndirectOffsetOnAxis(slot_ids[0:CAP2, 1:2], 0)).then_inc(x_gathered, 16)

            load_ids(0)
            gather(0)
            pool.wait_ge(slots_ready, 2)
            n_blocks = pool.value_load(blocks[0:1, 0:1], min_val=NE, max_val=NE + MAXOV)
            further = pool.value_load(blocks[0:1, 1:2], min_val=0, max_val=MAXOV)
            with pool.If(further > 0):
                for j in range(NT * TOPK):
                    nc.gpsimd.indirect_dma_start(slot_dram, bass.IndirectOffsetOnAxis(slot_all[:, j:j + 1], 0),
                                                 token_i[:, j // TOPK:j // TOPK + 1], None).then_inc(table_written, 16)
                pool.wait_ge(table_written, 16 + 32 * NT * TOPK)
                pool.nop()
            with pool.Else():
                pool.nop()
            with pool.Fori(0, n_blocks) as b:
                load_ids(b + 1)
                for i, ci in enumerate(POOL_CHUNKS):
                    pool.wait_ge(hi_ready, b * NCH + ci + 1)
                    nc.gpsimd.tensor_tensor(w_lo[ci % NHL][:], raw[ci % NRAW][:], w_hi[ci % NHL][:].bitcast(F32),
                                            ALU.subtract).then_inc(lo_pool, 1)
                    if i == 0:
                        gather(b + 1)

            further = pool.value_load(blocks[0:1, 1:2], min_val=0, max_val=MAXOV)
            pool.wait_ge(rows_stored, n_blocks * 32)
            pool.wait_ge(xt_hi, n_blocks * 4 + 4)
            pool.wait_ge(xt_lo, n_blocks * 4 + 4)
            apart(pool)

            def fetch(table, source, first):
                for j in range(NT * TOPK):
                    n = first + j
                    if n >= NROWS:
                        pool.wait_ge(row_used, n - NROWS + 1)
                    nc.gpsimd.indirect_dma_start(rows[n % NROWS][:], None, source,
                                                 bass.IndirectOffsetOnAxis(table[:, j:j + 1], 0)
                                                 ).then_inc(row_loaded[n % NROWS], 16)

            with pool.If(further > 0):
                fetch(slot_over, rows_dram, 0)
                fetch(slot_main, rows_dram[0:MAIN, :], NT * TOPK)
            with pool.Else():
                fetch(slot_main, rows_dram[0:MAIN, :], 0)
            pool.nop()

        @block.scalar
        def _(act):
            act.wait_ge(c_loaded, 16)
            nc.scalar.activation(c_exp[:], c_col[:], ACT.Exp, scale=-1.0).then_inc(c_exp_ready, 1)
            for i in (0, 1, 4):
                dst = sh1[:, i * ACOLS:(i + 1) * ACOLS] if i < 2 else late[:, 0, :]
                act.wait_ge(mod_filled, i + 1)
                nc.scalar.copy(dst, (pj0, pj1, pj2)[i % 3][:]).then_inc(mod_taken[i % 3], 1)
            for s in range(3):
                act.wait_ge(mod_taken[s], EARLY_TAKEN[s])
            act.wait_ge(small_loaded, 11 * 16)
            act.wait_ge(init_ready, 3)

            def take_hT(n):
                act.wait_ge(hT_filled, n + 1)
                nc.scalar.copy(hT[:, 0:4, :].rearrange("p k t -> p (k t)"), tr0[:]).then_inc(hT_lo, 1)

            def square_x(n):
                act.wait_ge(x_loaded, n * 16 + 16)
                wait(act, hT_filled, n)
                nc.scalar.activation(h[:], x_in[:], ACT.Square, accum_out=ssx[:, 0:1]).then_inc(h_steps, 1)

            def square_q(n):
                act.wait_ge(sq_filled, n + 1)
                wait(act, qn_ready, n * 2)
                nc.scalar.activation(sqs[:, 0:QW], pj0[:], ACT.Square).then_inc(sq_squared, 1)

            def square_k(n):
                act.wait_ge(skv_filled, n + 1)
                nc.scalar.activation(sqs[:, QW:], pj1[:, 0:KW], ACT.Square)
                nc.scalar.copy(glrT[:], pj1[0:RANK, 256:256 + P]).then_inc(skv_squared, 1)

            def take_q(n):
                act.wait_ge(qk_filled, n + 1)
                wait(act, sc_filled, n)
                nc.scalar.activation(qT[:, :, 0:QH:2, :].rearrange("p c h t -> p h c t"),
                                     tr0[0:HD, :].rearrange("p (h c t) -> p h c t", t=CH, c=2),
                                     ACT.Copy, scale=qk_g[0:HD, 0:1])
                act.wait_ge(k_moved, n + 1)
                nc.scalar.activation(kTw[:, 0, CH:], sa[0:HD, 0:P], ACT.Copy,
                                     scale=qk_g[0:HD, 1:2]).then_inc(qkT_a, 1)

            def take_gqk(n):
                act.wait_ge(gqk_filled, n + 1)
                wait(act, qkf_ready, n * 2)
                nc.scalar.activation(gqk[:, 0:2, :].rearrange("p c t -> p (c t)"), pj2[:, 0:2 * P], ACT.Copy,
                                     scale=GK ** -0.5)
                nc.scalar.copy(gqk[:, 2:4, :].rearrange("p c t -> p (c t)"), pj2[:, 2 * P:]).then_inc(gqk_ready, 1)

            def exp_gate(n):
                act.wait_ge(og_filled, n + 1)
                wait(act, y_ready, n)
                nc.scalar.activation(ge[:], pj1[:], ACT.Exp, scale=-1.0)
                nc.scalar.copy(gate[:], pj1[:]).then_inc(ge_ready, 1)

            def softplus(n):
                st = Steps(act, zl_steps, n, 1)
                act.wait_ge(z_neg, n + 1)
                st(nc.scalar.activation(zt[:], zt[:], ACT.Exp))
                nc.scalar.activation(zt[:], zt[:], ACT.Ln, bias=1.0).then_inc(zl_ready, 1)
                st.end()

            def softmax_exp(m):
                act.wait_ge(max_ready, m + 1)
                for c in range(2):
                    for j in range(4):
                        nc.scalar.activation(sc[:, c, j * P:(j + 1) * P], sc[:, c, j * P:(j + 1) * P], ACT.Exp,
                                             bias=stat[:, 1, 4 * c + j:4 * c + j + 1],
                                             accum_out=stat[:, 3, 4 * c + j:4 * c + j + 1])
                nc.scalar.activation(stat[:, 4, :], stat[:, 2, :], ACT.Exp).then_inc(p_ready, 1)

            def take_pT(m):
                act.wait_ge(pt_filled, m + 1)
                wait(act, pv_filled, m)
                nc.scalar.copy(pT[:, 0, :], sa[:]).then_inc(pt_a, 1)

            def take_pv(m):
                act.wait_ge(pv_filled, m + 1)
                wait(act, y_stored, m * 16)
                v = sa[0:HD, :].rearrange("p (h q) -> p h q", q=CH)
                nc.scalar.copy(yT[0:HD, 0:4, 0:CH], v[:, 0:QH:2, :])
                nc.scalar.copy(yT[HD:P, 0:4, 0:CH], v[:, 1:QH:2, :]).then_inc(pv_a, 1)

            def factors(m, c):
                act.wait_ge(e_filled, m * 2 + c + 1)
                wait(act, qkf_ready, m * 2 + c)
                nc.scalar.activation(fac[:, 0:4, :].rearrange("p f t -> p (f t)"), gb[:], ACT.Exp)
                nc.scalar.activation(fac[:, 4:7, :].rearrange("p f t -> p (f t)"), tr1[:, 0:3 * P],
                                     ACT.Exp).then_inc(fac_ready, 1)

            def take_kg(m):
                act.wait_ge(kg_filled, m + 1)
                for chunk in range(2):
                    rows_of = slice(chunk * CH, (chunk + 1) * CH)
                    ins = nc.scalar.copy(kg[rows_of, chunk].rearrange("p c d -> p (c d)"), tr0[rows_of, 0:2 * P])
                ins.then_inc(kg_ready, 1)

            def square_o(m):
                act.wait_ge(o_filled, m + 1)
                wait(act, ro_ready, m)
                for hd in range(GH):
                    ins = nc.scalar.activation(osq[:, hd * GV:(hd + 1) * GV], sa[:, hd * GV:(hd + 1) * GV],
                                               ACT.Square, accum_out=sso[:, hd:hd + 1])
                ins.then_inc(so_ready, 1)

            def take_yT(m):
                act.wait_ge(yt_filled, m + 1)
                nc.scalar.copy(yT[:, 4:8, :].rearrange("p k t -> p (k t)"), pj2[:]).then_inc(yT_ready, 1)

            def take_late(m):
                act.wait_ge(mod_filled, m + EARLY)
                apart(act)
                nc.scalar.copy(late[:, bass.ds(m, 1), :].rearrange("p a n -> p (a n)"), gb[:]).then_inc(mod_taken[0], 1)

            def mixer_tile(m, more_tiles, more_x, first=False):
                n = m + 1
                if more_tiles:
                    take_hT(n)
                softmax_exp(m)
                softplus(m)
                if more_tiles:
                    square_q(n)
                if not first:
                    take_late(m)
                    take_yT(m - 1)
                if more_x:
                    square_x(n + 1)
                take_pT(m)
                if more_tiles:
                    square_k(n)
                take_pv(m)
                factors(m, 0)
                if more_tiles:
                    take_q(n)
                factors(m, 1)
                if more_tiles:
                    take_gqk(n)
                take_kg(m)
                square_o(m)
                if more_tiles:
                    exp_gate(n)

            square_x(0)
            take_hT(0)
            square_x(1)
            square_q(0)
            square_k(0)
            take_q(0)
            take_gqk(0)
            exp_gate(0)
            mixer_tile(0, True, True, True)
            with act.Fori(1, NT - 2) as m:
                mixer_tile(m, True, True)
            mixer_tile(NT - 2, True, False)
            mixer_tile(NT - 1, False, False)
            take_yT(NT - 1)

            def square_x1(t, s):
                act.wait_ge(x1_ready, t + 1)
                nc.scalar.activation(h2[s][:], x_res[s][:], ACT.Square, accum_out=ss2[:, 0:1]).then_inc(ss2_ready, 1)

            def take_h2T(t):
                act.wait_ge(h2t_filled, t + 1)
                nc.scalar.copy(h2T[:, 0:4, :].rearrange("p k t -> p (k t)"), tr0[:]).then_inc(h2t_lo, 1)

            def exp_top(t):
                act.wait_ge(top_ready, t + 1)
                nc.scalar.activation(tope[:], topf[:], ACT.Exp, accum_out=tops[:, 0:1]).then_inc(tope_ready, 1)

            square_x1(0, 0)
            square_x1(1, 1)
            take_h2T(0)
            exp_top(0)
            with act.Fori(1, NT // 2) as i:
                for s in range(2):
                    square_x1(i * 2 + s, s)
                    take_h2T(i * 2 + s - 1)
                    exp_top(i * 2 + s - 1)
            take_h2T(NT - 1)
            exp_top(NT - 1)

            act.wait_ge(slots_ready, 2)
            act.wait_ge(bias_filled, 1)
            nc.scalar.copy(b_cols[:, 0].rearrange("p k e -> p (k e)"), pj0[:, 0:KT * NE])
            nc.scalar.activation(b_cols[:, 1].rearrange("p k e -> p (k e)"), pj1[:, 0:KT * NE], ACT.Copy, bias=1.0)
            nc.scalar.copy(b_cols[:, 2].rearrange("p k e -> p (k e)"), pj2[:, 0:KT * NE]).then_inc(bias_ready, 1)

            def high_part(b, ci):
                act.wait_ge(raw_loaded[ci % NRAW], (b * (NCH // NRAW) + ci // NRAW + 1) * 16)
                if ci >= NHL:
                    act.wait_ge(m_filled, (b * NCH + ci - NHL + 1) * 2)
                elif not isinstance(b, int):
                    act.wait_ge(m_filled, (b * NCH + ci - NHL + 1) * 2)
                nc.scalar.copy(w_hi[ci % NHL][:], raw[ci % NRAW][:]).then_inc(hi_ready, 1)

            def x_high(b, q):
                act.wait_ge(xt_filled, b * 4 + q + 1)
                bank = (tr0, tr1)[q % 2]
                nc.scalar.copy(xT[:, 2 * q:2 * q + 2, 0, :],
                               bank[:, 0:2 * CAP].rearrange("p (k t) -> p k t", t=CAP)).then_inc(xt_hi, 1)

            def right_part(b, ci):
                which, pair = chunk_of(ci)
                if which == 0:
                    wait(act, gs_ready, b * 4 + pair)
                else:
                    wait(act, av_ready, b * 4 + pair)
                for f in range(2):
                    q = 2 * ci + f
                    act.wait_ge(m_filled, b * 24 + q + 1)
                    nc.scalar.activation((g_sb, u_sb)[which][:, f, :], (pj0, pj1, pj2, sa)[q % 4][:, CAP:2 * CAP],
                                         ACT.Identity, bias=b_now[:, which, 2 * pair + f:2 * pair + f + 1]
                                         ).then_inc(up_right, 1)

            def sigmoid(b, pair):
                act.wait_ge(g_clipped, b * 4 + pair + 1)
                wait(act, gs_ready, b * 4 + pair)
                nc.scalar.activation(sg_sb[:], g_sb[:], ACT.Sigmoid, scale=ALPHA).then_inc(sig_ready, 1)

            def act_high(b, pair):
                act.wait_ge(av_ready, b * 4 + pair + 1)
                nc.scalar.copy(actT[:, 2 * pair:2 * pair + 2, 0, :], av_sb[:]).then_inc(act_hi, 1)

            def down_right_part(b, pair):
                wait(act, yt2_filled, b * 4)
                for f in range(2):
                    q = 16 + 2 * pair + f
                    act.wait_ge(m_filled, b * 24 + q + 1)
                    nc.scalar.activation(yT2[:, pair, f, :], (pj0, pj1, pj2, sa)[q % 4][:, CAP:2 * CAP], ACT.Identity,
                                         bias=b_now[:, 2, 2 * pair + f:2 * pair + f + 1]).then_inc(down_right, 1)

            def take_rows(b, half):
                act.wait_ge(yt2_filled, b * 4 + 2 * half + 2)
                wait(act, rows_stored, b * 32)
                nc.scalar.copy(y_out[:, 0, half * 512:half * 512 + 512], s_b[:])
                nc.scalar.copy(y_out[0:CAP2, 1, half * 512:half * 512 + 512], gb[0:CAP2, :]).then_inc(y_taken, 1)

            n_blocks = act.value_load(blocks[0:1, 0:1], min_val=NE, max_val=NE + MAXOV)

            def last_part(b, then, high_parts):
                for i in range(LEAD):
                    if high_parts:
                        high_part(then, i)
                    if i == 1:
                        down_right_part(b, 2)
                    if i < 2:
                        x_high(then, 2 + i)
                down_right_part(b, 3)
                take_rows(b, 0)

            def first_part(b, before=None):
                act.wait_ge(b_now_ready, b + 1)
                for slot in range(8):
                    high_part(b, slot + LEAD)
                    if slot % 2:
                        sigmoid(b, slot // 2)
                    elif slot:
                        act_high(b, slot // 2 - 1)
                    right_part(b, slot)
                    if slot == 1 and before is not None:
                        take_rows(before, 1)
                        store_rows(before)
                high_part(b, NCH - 1)
                act_high(b, 3)
                down_right_part(b, 0)
                x_high(b + 1, 0)
                x_high(b + 1, 1)
                down_right_part(b, 1)

            def store_rows(b):
                act.wait_ge(y_taken, b * 2 + 2)
                act.dma_start(rows_dram[bass.ds(b * CAP, P), :], y_out[:, 0, :]).then_inc(rows_stored, 16)
                act.dma_start(rows_dram[bass.ds(b * CAP + P, CAP2), :], y_out[0:CAP2, 1, :]).then_inc(rows_stored, 16)

            further = act.value_load(blocks[0:1, 1:2], min_val=0, max_val=MAXOV)
            with act.If(further > 0):
                for s in range(2):
                    act.wait_ge(c_stored[s], 16 * NT)
                for at_row in range(MAIN, SLOTS, T):
                    n = min(T, SLOTS - at_row)
                    act.dma_start(rows_dram[at_row:at_row + n, :], h2_dram[0:n, :]).then_inc(tail_filled, 16)
                act.wait_ge(tail_filled, 16 * math.ceil((SLOTS - MAIN) / T))
                act.nop()
            with act.Else():
                act.nop()
            act.wait_ge(table_cleared, 16)
            for s in range(2):
                act.wait_ge(c_stored[s], 16 * NT)
            for ci in range(LEAD):
                high_part(0, ci)
            for q in range(4):
                x_high(0, q)
            first_part(0)
            with act.Fori(1, n_blocks) as b:
                last_part(b - 1, b, True)
                first_part(b, b - 1)
            last = act.value_load(blocks[0:1, 2:3], min_val=NE - 1, max_val=NE + MAXOV - 1)
            last_part(last, n_blocks, False)
            take_rows(last, 1)
            store_rows(last)
            act.wait_ge(rows_stored, n_blocks * 32)
            apart(act)
            act.nop()

        @block.vector
        def _(dve):
            st = Steps(dve, c_steps, 0, 3)
            dve.wait_ge(c_exp_ready, 1)
            dve.wait_ge(const_loaded, 16)
            st(nc.vector.tensor_scalar(c_exp[:], c_exp[:], 1.0, None, ALU.add))
            st(nc.vector.reciprocal(c_exp[:], c_exp[:]))
            st(nc.vector.tensor_tensor(c_act[:], c_col[:], c_exp[:], ALU.mult))
            for k in range(KT):
                ins = nc.vector.tensor_scalar(c_wide[:, k, :], cst("ones"), c_act[:, k:k + 1], None, ALU.mult)
            ins.then_inc(c_wide_ready, 1)
            st = Steps(dve, fma_steps, 0, KT - 1)
            dve.wait_ge(ada_loaded[2], 32)
            st(nc.vector.tensor_scalar(fma[:], ada[2][:, 0, :], c_act[:, 0:1], None, ALU.mult))
            for k in range(1, KT):
                ins = nc.vector.scalar_tensor_tensor(fma[:], ada[2][:, k, :], c_act[:, k:k + 1], fma[:],
                                                     ALU.mult, ALU.add)
                if k < KT - 1:
                    st(ins)
            ins.then_inc(fma_ready, 1)
            st.end()
            dve.wait_ge(norms_loaded, 16)
            for i in (2, 3):
                half = slice((i - 2) * ACOLS, (i - 1) * ACOLS)
                dve.wait_ge(mod_filled, i + 1)
                nc.vector.scalar_tensor_tensor(gs1[:, half], (pj0, pj1, pj2)[i % 3][:], 1.0, n1_wide[:, half],
                                               ALU.add, ALU.mult).then_inc(mod_taken[i % 3], 1)
            for s in range(3):
                dve.wait_ge(mod_taken[s], EARLY_TAKEN[s])
            st = Steps(dve, init_ready, 0, 2)
            nc.vector.memset(kTw[:], 0.0)
            nc.vector.memset(v_b[:], 0.0)
            nc.vector.memset(kg[:], 0.0)
            nc.vector.memset(s0[:], 0.0)
            st(nc.vector.tensor_copy(alibi_a[:], cst("alibi")))
            st(nc.vector.memset(alibi_a[:].rearrange("p (j k) -> p j k", k=P)[:, :, 0:CH], NEG))
            dve.wait_ge(small_loaded, 11 * 16)
            nc.vector.tensor_scalar(qk_g[:, 0:1], qk_g[:, 0:1], HD ** -0.5, None, ALU.mult).then_inc(init_ready, 1)
            dve.wait_ge(init_ready, 3)
            st.end()

            def take_hT(n):
                dve.wait_ge(hT_filled, n + 1)
                nc.vector.tensor_copy(hT[:, 4:8, :].rearrange("p k t -> p (k t)"), tr1[:]).then_inc(hT_hi, 1)

            def heads_squared(n):
                dve.wait_ge(sq_squared, n + 1)
                wait(dve, rq_ready, n)
                nc.vector.tensor_reduce(ssq[:, 0:QH], sqs[:, 0:QW].rearrange("p (h d) -> p h d", d=HD),
                                        AX_X, ALU.add).then_inc(ss_ready, 1)

            def keys_squared(n):
                dve.wait_ge(skv_squared, n + 1)
                nc.vector.tensor_reduce(ssq[:, QH:], sqs[:, QW:].rearrange("p (h d) -> p h d", d=HD),
                                        AX_X, ALU.add).then_inc(ss_ready, 1)

            def normed_qk(n):
                dve.wait_ge(rq_ready, n + 1)
                wait(dve, qk_filled, n)
                nc.vector.tensor_tensor(qn[:, 0:QW].rearrange("p (h d) -> p h d", d=HD),
                                        pj0[:].rearrange("p (h d) -> p h d", d=HD),
                                        rq[:, 0:QH].unsqueeze(2).broadcast_to([P, QH, HD]),
                                        ALU.mult).then_inc(qn_ready, 1)
                nc.vector.tensor_tensor(qn[:, QW:].rearrange("p (h d) -> p h d", d=HD),
                                        pj1[:, 0:KW].rearrange("p (h d) -> p h d", d=HD),
                                        rq[:, QH:].unsqueeze(2).broadcast_to([P, KVH, HD]),
                                        ALU.mult).then_inc(qn_ready, 1)

            def take_v(n):
                st = Steps(dve, v_steps, n, 1)
                wait(dve, pv_filled, n)
                st(nc.vector.tensor_copy(v_a[0:CH, :], v_b[CH:P, :]))
                nc.vector.tensor_copy(v_a[CH:P, :], pj1[0:CH, KW:KW + VW])
                nc.vector.tensor_copy(v_b[:], pj1[:, KW:KW + VW]).then_inc(v_ready, 1)
                st.end()

            def take_qk(n):
                wait(dve, sc_filled, n)
                nc.vector.tensor_copy(kTw[:, :, 0:CH], kTw[:, :, P:P + CH]).then_inc(k_moved, 1)
                dve.wait_ge(qk_filled, n + 1)
                nc.vector.tensor_scalar(qT[:, :, 1:QH:2, :].rearrange("p c h t -> p h c t"),
                                        tr0[HD:P, :].rearrange("p (h c t) -> p h c t", t=CH, c=2),
                                        qk_g[HD:P, 0:1], None, ALU.mult)
                dve.wait_ge(k_moved, n + 1)
                nc.vector.tensor_scalar(kTw[:, 1, CH:], sa[HD:P, 0:P], qk_g[HD:P, 1:2], None,
                                        ALU.mult).then_inc(qkT_b, 1)

            def take_gv(n):
                dve.wait_ge(gv_filled, n + 1)
                wait(dve, o_filled, n)
                nc.vector.tensor_copy(gv[:], pj0[:]).then_inc(gv_ready, 1)

            def out_gate(n):
                st = Steps(dve, gate_steps, n, 3)
                dve.wait_ge(ge_ready, n + 1)
                st(nc.vector.tensor_scalar(ge[:], ge[:], 1.0, None, ALU.add))
                st(nc.vector.reciprocal(ge[:], ge[:]))
                st(nc.vector.tensor_tensor(ge[:], gate[:], ge[:], ALU.mult))
                nc.vector.tensor_tensor(gate[:].rearrange("p (h e) -> p h e", e=GV),
                                        ge[:].rearrange("p (h e) -> p h e", e=GV),
                                        gn_wide[:].unsqueeze(1).broadcast_to([P, GH, GV]),
                                        ALU.mult).then_inc(gate_ready, 1)
                st.end()

            def forget_in(n):
                st = Steps(dve, z_steps, n, 1)
                dve.wait_ge(z_filled, n + 1)
                st(nc.vector.tensor_tensor(zb[:], s_b[:, 0:GKW], bg_wide[:], ALU.add))
                nc.vector.scalar_tensor_tensor(zt[:], zb[:], -1.0, zb[:], ALU.mult, ALU.min).then_inc(z_neg, 1)
                st.end()

            def forget_out(n):
                dve.wait_ge(zl_ready, n + 1)
                wait(dve, e_filled, n * 2)
                nc.vector.scalar_tensor_tensor(la[:], zb[:], 0.0, zt[:], ALU.min, ALU.subtract).then_inc(la_ready, 1)

            def softmax_max(m):
                st = Steps(dve, soft_steps, m, 6)
                dve.wait_ge(sc_filled, m + 1)
                st(nc.vector.tensor_tensor(sc[:, 0, :], sa[:], alibi_a[:], ALU.add), False)
                st(nc.vector.tensor_tensor(sc[:, 1, :], s_b[:], cst("alibi"), ALU.add))
                st(nc.vector.tensor_copy(alibi_a[:], cst("alibi")), False)
                st(nc.vector.tensor_reduce(stat[:, 0, :], sc[:].rearrange("p c (j k) -> p (c j) k", k=P), AX_X, ALU.max))
                st(nc.vector.tensor_tensor(stat[:, 0, :], stat[:, 0, :], sink[:], ALU.max))
                st(nc.vector.tensor_scalar(stat[:, 1, :], stat[:, 0, :], -1.0, None, ALU.mult))
                nc.vector.tensor_tensor(stat[:, 2, :], sink[:], stat[:, 1, :], ALU.add).then_inc(max_ready, 1)
                st.end()

            def softmax_norm(m):
                st = Steps(dve, den_steps, m, 2)
                dve.wait_ge(p_ready, m + 1)
                st(nc.vector.tensor_tensor(stat[:, 3, :], stat[:, 3, :], stat[:, 4, :], ALU.add))
                st(nc.vector.reciprocal(stat[:, 5, :], stat[:, 3, :]))
                v = sc[:].rearrange("p c (j k) -> p (c j) k", k=P)
                nc.vector.tensor_tensor(v, v, stat[:, 5, :].unsqueeze(2).broadcast_to([P, 8, P]),
                                        ALU.mult).then_inc(p_norm, 1)
                st.end()

            def take_pT(m):
                dve.wait_ge(pt_filled, m + 1)
                wait(dve, pv_filled, m)
                nc.vector.tensor_copy(pT[:, 1, :], s_b[:]).then_inc(pt_b, 1)

            def take_pv(m):
                dve.wait_ge(pv_filled, m + 1)
                wait(dve, y_stored, m * 16)
                v = s_b[0:HD, :].rearrange("p (h q) -> p h q", q=CH)
                nc.vector.tensor_copy(yT[0:HD, 0:4, CH:P], v[:, 0:QH:2, :])
                nc.vector.tensor_copy(yT[HD:P, 0:4, CH:P], v[:, 1:QH:2, :]).then_inc(pv_b, 1)

            def decayed(m, c):
                dve.wait_ge(fac_ready, m * 2 + c + 1)
                dve.wait_ge(gqk_ready, m + 1)
                wait(dve, o_filled, m)
                wait(dve, s0_ready, m)
                nc.vector.tensor_tensor(qf[:, c], fac[:, 0:5, :],
                                        gqk[:, c, :].unsqueeze(1).broadcast_to([P, 5, P]), ALU.mult)
                nc.vector.tensor_copy(dec[:, c, :], fac[:, 1, CH - 1:P:CH])
                nc.vector.tensor_tensor(kf[:, c], fac[:, 2:7, :],
                                        gqk[:, 2 + c, :].unsqueeze(1).broadcast_to([P, 5, P]),
                                        ALU.mult).then_inc(qkf_ready, 1)

            def scores_within(m, hd):
                dve.wait_ge(at_filled, m * 4 + hd + 1)
                bank = (gb, tr1)[hd % 2]
                if hd >= 2:
                    dve.wait_ge(at_ready, m * 4 + hd - 1)
                else:
                    dve.wait_ge(pt_filled, m + 1)
                    wait(dve, at_ready, m * 4)
                    wait(dve, o_filled, m)
                nc.vector.tensor_tensor(sc[:, hd % 2, :], bank[:], cst("mask"), ALU.mult).then_inc(at_masked, 1)
                dve.wait_ge(at_masked, m * 4 + hd + 1)
                nc.vector.tensor_reduce(at[:, hd, :], sc[:, hd % 2, :].rearrange("p (l t) -> p t l", t=P),
                                        AX_X, ALU.add).then_inc(at_ready, 1)

            def state_mid(m):
                dve.wait_ge(dl_filled, m + 1)
                wait(dve, s0_ready, m)
                for c in range(2):
                    ins = nc.vector.scalar_tensor_tensor(s1[:, c, :], s0[:, c, :], dec[:, c, 0:1],
                                                         s_b[:, (2 * c) * GV:(2 * c + 1) * GV], ALU.mult, ALU.add)
                ins.then_inc(s1_ready, 1)

            def state_end(m):
                dve.wait_ge(o_filled, m + 1)
                dve.wait_ge(s1_ready, m + 1)
                for c in range(2):
                    ins = nc.vector.scalar_tensor_tensor(s0[:, c, :], s1[:, c, :], dec[:, c, 1:2],
                                                         s_b[:, (2 * c + 1) * GV:(2 * c + 2) * GV], ALU.mult, ALU.add)
                ins.then_inc(s0_ready, 1)

            def normed_o(m):
                dve.wait_ge(ro_ready, m + 1)
                dve.wait_ge(gate_ready, m + 1)
                wait(dve, yt_filled, m)
                for hd in range(GH):
                    ins = nc.vector.scalar_tensor_tensor(y[:, hd * GV:(hd + 1) * GV], sa[:, hd * GV:(hd + 1) * GV],
                                                         ro[:, hd:hd + 1], gate[:, hd * GV:(hd + 1) * GV],
                                                         ALU.mult, ALU.mult)
                ins.then_inc(y_ready, 1)

            def late_product(j):
                st = Steps(dve, fma_steps, j + 1, KT - 1)
                dve.wait_ge(ada_loaded[0], j * 32 + 32 * (EARLY_TAKEN[0] + 1))
                st(nc.vector.tensor_scalar(ada_late[:, 0, :], ada_late[:, 0, :], c_act[:, 0:1], None, ALU.mult))
                for k in range(1, KT):
                    ins = nc.vector.scalar_tensor_tensor(ada_late[:, 0, :], ada_late[:, k, :], c_act[:, k:k + 1],
                                                         ada_late[:, 0, :], ALU.mult, ALU.add)
                    if k < KT - 1:
                        st(ins)
                ins.then_inc(fma_ready, 1)
                st.end()

            def mixer_tile(m, more_tiles):
                n = m + 1
                if more_tiles:
                    take_hT(n)
                softmax_max(m)
                softmax_norm(m)
                forget_out(m)
                if more_tiles:
                    heads_squared(n)
                take_pT(m)
                if more_tiles:
                    keys_squared(n)
                    normed_qk(n)
                take_pv(m)
                if more_tiles:
                    take_v(n)
                decayed(m, 0)
                out_gate(m)
                if more_tiles:
                    take_qk(n)
                decayed(m, 1)
                if more_tiles:
                    late_product(m)
                for hd in range(GH):
                    scores_within(m, hd)
                state_mid(m)
                state_end(m)
                normed_o(m)
                if more_tiles:
                    take_gv(n)
                    forget_in(n)

            take_hT(0)
            heads_squared(0)
            keys_squared(0)
            normed_qk(0)
            take_v(0)
            take_qk(0)
            take_gv(0)
            forget_in(0)
            mixer_tile(0, True)
            with dve.Fori(1, NT - 1) as m:
                mixer_tile(m, True)
                apart(dve)
            mixer_tile(NT - 1, False)

            def residual(t, s):
                st = Steps(dve, x1_steps, t, 1)
                dve.wait_ge(wo_filled, t + 1)
                dve.wait_ge(yx_loaded[s], (t - s) * 16 + 32)
                if not (isinstance(t, int) and t < 2):
                    dve.wait_ge(c_stored[s], (t - s) * 16)
                lo, hi = ((pj0, pj1), (pj2, sa))[s]
                nc.vector.tensor_tensor(h2[s][:, 0:512], lo[:], g1[:, 0:512], ALU.mult)
                st(nc.vector.tensor_tensor(h2[s][:, 512:], hi[:], g1[:, 512:], ALU.mult))
                nc.vector.tensor_tensor(x_res[s][:], x_res[s][:], h2[s][:], ALU.add).then_inc(x1_ready, 1)
                st.end()

            def norm_out(t, s):
                st = Steps(dve, h2_steps, t, 1)
                dve.wait_ge(r2_ready, t + 1)
                st(nc.vector.scalar_tensor_tensor(h2[s][:], x_res[s][:], ss2[:, 1:2], gs2, ALU.mult, ALU.mult))
                nc.vector.tensor_tensor(h2[s][:], h2[s][:], sh2, ALU.add).then_inc(h2_ready, 1)
                st.end()

            def take_h2T(t):
                dve.wait_ge(h2t_filled, t + 1)
                nc.vector.tensor_copy(h2T[:, 4:8, :].rearrange("p k t -> p (k t)"), tr1[:]).then_inc(h2t_hi, 1)

            def choose(t):
                st = Steps(dve, lg_steps, t, CHOOSE + PLACE)
                dve.wait_ge(lg_filled, t + 1)
                dve.wait_ge(rt_loaded, 64)
                st(nc.vector.tensor_tensor(lg[:], gb[:, 0:NE], br_wide[:], ALU.add))
                apart(dve)
                st(nc.vector.max(top[:], lg[:]))
                wait(dve, tope_ready, t)
                nc.vector.tensor_scalar(topf[:], top[:, 0:4], top[:, 0:1], None, ALU.subtract).then_inc(top_ready, 1)
                st(nc.vector.max_index(topi[:], top[:], lg[:]))
                dve.wait_ge(tope_ready, t + 1)
                st(nc.vector.tensor_copy(topf[:], topi[:, 0:4]))
                st(nc.vector.tensor_tensor(onehot[:, bass.ds(t, 1)].rearrange("p a k e -> p (a k) e"),
                                           topf[:].unsqueeze(2).broadcast_to([P, TOPK, NE]),
                                           cst("experts").unsqueeze(1).broadcast_to([P, TOPK, NE]), ALU.is_equal), False)
                st(nc.vector.reciprocal(tops[:, 1:2], tops[:, 0:1]))
                nc.vector.tensor_scalar(weights[:, bass.ds(t, 1)].rearrange("p a k -> p (a k)"), tope[:],
                                        tops[:, 1:2], None, ALU.mult)
                st(nc.vector.tensor_reduce(chosen[:, bass.ds(t, 1)].rearrange("p a e -> p (a e)"),
                                           onehot[:, bass.ds(t, 1)].rearrange("p a k e -> p (a e) k"), AX_X, ALU.add))
                st(nc.vector.tensor_tensor(prior[:, bass.ds(t + 1, 1)], prior[:, bass.ds(t, 1)],
                                           chosen[:, bass.ds(t, 1)], ALU.add))
                assert st.n == CHOOSE

            def slots_of_tile(t):
                st = Steps(dve, lg_steps, t, CHOOSE + PLACE)
                st.n = CHOOSE
                dve.wait_ge(ranked, t + 1)
                st(nc.vector.tensor_scalar(now[:, 0, :], s_b[:, 0:NE], float(CAP), float(2 * TABLE), ALU.is_ge, ALU.mult), False)
                st(nc.vector.tensor_tensor(now[:, 1, :], s_b[:, 0:NE], cst("slot0"), ALU.add))
                st(nc.vector.tensor_tensor(now[:, 1, :], now[:, 1, :], now[:, 0, :], ALU.add))
                st(nc.vector.tensor_tensor(now_picked[:], onehot[:, bass.ds(t, 1)].rearrange("p a k e -> p (a k) e"),
                                           now[:, 1, :].unsqueeze(1).broadcast_to([P, TOPK, NE]), ALU.mult))
                st(nc.vector.tensor_reduce(now_slot[:], now_picked[:], AX_X, ALU.add))
                st(nc.vector.tensor_tensor(now_slot[:], now_slot[:], cst("unread"), ALU.min))
                dve.wait_ge(table_written, t * 16 * TOPK + 16)
                apart(dve)
                st(nc.vector.tensor_copy(now_token[:], cst("token")[:, bass.ds(t, 1)]), False)
                nc.vector.tensor_copy(now_i[:], now_slot[:]).then_inc(slots_now, 1)
                st.end()

            dve.wait_ge(mod_taken[0], EARLY_TAKEN[0] + NT - 1)
            dve.wait_ge(rt_loaded, 64)
            nc.vector.memset(prior[:, 0, :], 0.0)
            nc.vector.scalar_tensor_tensor(gs2, gs2, 1.0, n2_wide[:], ALU.add, ALU.mult).then_inc(init_ready, 1)
            dve.wait_ge(init_ready, 4)
            residual(0, 0)
            norm_out(0, 0)
            residual(1, 1)
            take_h2T(0)
            norm_out(1, 1)
            choose(0)
            with dve.Fori(1, NT // 2) as i:
                for s in range(2):
                    t = i * 2 + s
                    residual(t, s)
                    take_h2T(t - 1)
                    norm_out(t, s)
                    slots_of_tile(t - 2)
                    choose(t - 1)
            take_h2T(NT - 1)
            slots_of_tile(NT - 2)
            choose(NT - 1)
            slots_of_tile(NT - 1)

            st = Steps(dve, ct_steps, 0, 0)
            st(nc.vector.tensor_copy(token_i[:], cst("token")), False)
            dve.wait_ge(rank_filled, 1)
            st(nc.vector.tensor_copy(count[:], pj1[:, 0:NE]), False)
            st(nc.vector.tensor_copy(slotmap[:].rearrange("p t e -> p (t e)"), pj0[:, 0:NT * NE]))
            st(nc.vector.tensor_scalar(more[:, 0, :], count[:], float(CAP), None, ALU.is_gt))
            for j in range(1, MAXJ):
                st(nc.vector.scalar_tensor_tensor(more[:, j, :], count[:], float(CAP * (j + 1)), more[:, j - 1, :],
                                                  ALU.is_gt, ALU.add))
            st(nc.vector.tensor_tensor_scan(incl[:], cst("ones")[:, 0:NE], more[:, MAXJ - 1, :], 0.0, ALU.mult, ALU.add))
            st(nc.vector.tensor_tensor(base2[:, 0, :], incl[:], more[:, MAXJ - 1, :], ALU.subtract))
            st(nc.vector.tensor_scalar(base2[:, 0, :], base2[:, 0, :], float(CAP), float((NE - 1) * CAP), ALU.mult, ALU.add))
            st(nc.vector.tensor_tensor(base2[:, 1, :], base2[:, 0, :], cst("slot0"), ALU.subtract))
            st(nc.vector.tensor_scalar(far[:], slotmap[:], float(CAP), None, ALU.is_ge))
            st(nc.vector.tensor_tensor(far[:], far[:], base2[:, 1, :].unsqueeze(1).broadcast_to([P, NT, NE]), ALU.mult))
            st(nc.vector.tensor_tensor(slotmap[:], slotmap[:],
                                       cst("slot0").unsqueeze(1).broadcast_to([P, NT, NE]), ALU.add))
            st(nc.vector.tensor_tensor(slotmap[:], slotmap[:], far[:], ALU.add))
            for t in range(NT):
                st(nc.vector.tensor_tensor(picked[:, t * TOPK:(t + 1) * TOPK, :], onehot[:, t],
                                           slotmap[:, t, :].unsqueeze(1).broadcast_to([P, TOPK, NE]), ALU.mult), t == NT - 1)
            st(nc.vector.tensor_reduce(slotf[:, 0, :], picked[:], AX_X, ALU.add))
            st(nc.vector.tensor_copy(slot_all[:], slotf[:, 0, :]))
            nc.vector.tensor_scalar(slotf[:, 1, :], slotf[:, 0, :], float(MAIN - 1), None, ALU.min).then_inc(slots_ready, 1)
            dve.wait_ge(slots_ready, 1)
            w_all = weights[:].rearrange("p t k -> p (t k)")
            st(nc.vector.tensor_copy(slot_main[:], slotf[:, 1, :]), False)
            st(nc.vector.tensor_scalar(slotf[:, 2, :], slotf[:, 0, :], float(MAIN), None, ALU.is_ge))
            st(nc.vector.tensor_tensor(slotf[:, 3, :], slotf[:, 2, :], slotf[:, 0, :], ALU.mult), False)
            st(nc.vector.tensor_tensor(w_over[:], slotf[:, 2, :], w_all, ALU.mult))
            st(nc.vector.tensor_copy(slot_over[:], slotf[:, 3, :]), False)
            st(nc.vector.tensor_tensor(w_main[:], w_all, w_over[:], ALU.subtract), False)
            for i, more_than in enumerate((NE, 0, NE - 1)):
                st(nc.vector.tensor_scalar(blocks[:, i:i + 1], incl[0:1, NE - 1:NE], float(more_than), None, ALU.add), i == 2)
            st(nc.vector.tensor_scalar(wide_of[:, 0:NE], count[0:1, :], float(WIDTHS[0]), None, ALU.is_gt))
            st(nc.vector.scalar_tensor_tensor(wide_of[:, 0:NE], count[0:1, :], float(WIDTHS[1]), wide_of[:, 0:NE],
                                              ALU.is_gt, ALU.add), False)
            st(nc.vector.memset(wide_of[:, NE:], len(WIDTHS) - 1), False)
            st(nc.vector.tensor_tensor(ovf[:], incl[0:1, :].unsqueeze(1).broadcast_to([1, MAXOV, NE]),
                                       cst("over", 1).rearrange("p (b e) -> p b e", e=NE), ALU.is_le))
            st(nc.vector.tensor_reduce(ovs[:], ovf[:], AX_X, ALU.add))
            st(nc.vector.tensor_scalar(ovs[:], ovs[:], float(NE - 1), None, ALU.min))
            st(nc.vector.tensor_copy(expert_of[:, 0:NE], cst("experts", 1)), False)
            nc.vector.tensor_copy(expert_of[:, NE:], ovs[:]).then_inc(slots_ready, 1)
            dve.wait_ge(slots_ready, 2)

            n_blocks = dve.value_load(blocks[0:1, 0:1], min_val=NE, max_val=NE + MAXOV)
            dve.wait_ge(bias_ready, 1)

            def low_part(b, ci):
                if ci in POOL_CHUNKS:
                    return
                dve.wait_ge(hi_ready, b * NCH + ci + 1)
                nc.vector.tensor_tensor(w_lo[ci % NHL][:], raw[ci % NRAW][:], w_hi[ci % NHL][:].bitcast(F32),
                                        ALU.subtract).then_inc(lo_dve, 1)

            def x_low(b, q):
                dve.wait_ge(xt_hi, b * 4 + q + 1)
                bank = (tr0, tr1)[q % 2]
                nc.vector.tensor_tensor(xT[:, 2 * q:2 * q + 2, 1, :],
                                        bank[:, 0:2 * CAP].rearrange("p (k t) -> p k t", t=CAP),
                                        xT[:, 2 * q:2 * q + 2, 0, :].bitcast(F32), ALU.subtract).then_inc(xt_lo, 1)

            def biases(b):
                e = dve.value_load(expert_of[0:1, bass.ds(b, 1)], min_val=0, max_val=NE - 1)
                nc.vector.tensor_copy(b_now[:], b_cols[:, :, :, bass.ds(e, 1)].rearrange("p j k e -> p j (k e)")
                                      ).then_inc(b_now_ready, 1)
                dve.wait_ge(b_now_ready, b + 1)

            m_banks = (pj0, pj1, pj2, sa)

            def add_left(b, q, dst):
                dve.wait_ge(up_right, b * 16 + q + 1)
                nc.vector.tensor_tensor(dst, m_banks[q % 4][:, 0:CAP], dst, ALU.add).then_inc(up_taken, 1)

            def take_gate(b, pair):
                for f in range(2):
                    add_left(b, 4 * pair + f, g_sb[:, f, :])
                dve.wait_ge(up_taken, b * 16 + 4 * pair + 2)
                nc.vector.tensor_scalar(g_sb[:], g_sb[:], LIMIT, None, ALU.min).then_inc(g_clipped, 1)

            def take_up(b, pair):
                for f in range(2):
                    add_left(b, 4 * pair + 2 + f, u_sb[:, f, :])
                dve.wait_ge(up_taken, b * 16 + 4 * pair + 4)
                nc.vector.tensor_scalar(u_sb[:], u_sb[:], 1.0 + LIMIT, 1.0 - LIMIT, ALU.min, ALU.max).then_inc(u_clipped, 1)

            def activate(b, pair):
                dve.wait_ge(sig_ready, b * 4 + pair + 1)
                nc.vector.tensor_tensor(sg_sb[:], g_sb[:], sg_sb[:], ALU.mult).then_inc(gs_ready, 1)
                take_up(b, pair)
                dve.wait_ge(gs_ready, b * 4 + pair + 1)
                dve.wait_ge(u_clipped, b * 4 + pair + 1)
                nc.vector.tensor_tensor(av_sb[:], u_sb[:], sg_sb[:], ALU.mult).then_inc(av_ready, 1)

            def take_down(b, pair):
                for f in range(2):
                    q = 16 + 2 * pair + f
                    dst = yT2[:, pair, f, :]
                    dve.wait_ge(down_right, b * 8 + 2 * pair + f + 1)
                    nc.vector.tensor_tensor(dst, m_banks[q % 4][:, 0:CAP], dst, ALU.add).then_inc(down_taken, 1)

            def act_low(b, pair):
                dve.wait_ge(act_hi, b * 4 + pair + 1)
                nc.vector.tensor_tensor(actT[:, 2 * pair:2 * pair + 2, 1, :], av_sb[:],
                                        actT[:, 2 * pair:2 * pair + 2, 0, :].bitcast(F32),
                                        ALU.subtract).then_inc(act_lo, 1)

            def first_part(b):
                biases(b)
                for pair in range(4):
                    low_part(b, 2 * pair + LEAD)
                    if pair:
                        act_low(b, pair - 1)
                    take_gate(b, pair)
                    low_part(b, 2 * pair + 1 + LEAD)
                    activate(b, pair)
                act_low(b, 3)
                low_part(b, NCH - 1)
                take_down(b, 0)
                x_low(b + 1, 0)
                x_low(b + 1, 1)
                take_down(b, 1)

            def last_part(b, then, low_parts):
                for i in range(LEAD):
                    if low_parts:
                        low_part(then, i)
                    if i == 1:
                        take_down(b, 2)
                    if i < 2:
                        x_low(then, 2 + i)
                take_down(b, 3)

            for ci in range(LEAD):
                low_part(0, ci)
            for q in range(4):
                x_low(0, q)
            first_part(0)
            with dve.Fori(1, n_blocks) as b:
                last_part(b - 1, b, True)
                first_part(b)
            last = dve.value_load(blocks[0:1, 2:3], min_val=NE - 1, max_val=NE + MAXOV - 1)
            last_part(last, n_blocks, False)

            further = dve.value_load(blocks[0:1, 1:2], min_val=0, max_val=MAXOV)
            dve.wait_ge(rows_stored, n_blocks * 32)
            apart(dve)

            def combine(w, first):
                for t in range(NT):
                    n = first + t
                    s = n % 2
                    st = Steps(dve, add_steps, n, 2)
                    if n >= 2:
                        dve.wait_ge(add_steps, (n - 1) * 2)
                    for k in range(TOPK):
                        j = n * TOPK + k
                        wk = w[:, t * TOPK + k:t * TOPK + k + 1]
                        r = rows[j % NROWS]
                        dve.wait_ge(row_loaded[j % NROWS], 16 * (j // NROWS + 1))
                        if k == 0:
                            ins = nc.vector.tensor_scalar(acc[s][:], r[:], wk, None, ALU.mult)
                        else:
                            ins = nc.vector.scalar_tensor_tensor(acc[s][:], r[:], wk, acc[s][:], ALU.mult, ALU.add)
                        ins.then_inc(row_used, 1)
                        dve.wait_ge(row_used, j + 1)
                    st(nc.vector.tensor_tensor(acc[s][:], acc[s][:], g2, ALU.mult))
                    dve.wait_ge(res_loaded[s], 16 * (n // 2 + 1))
                    st(nc.vector.tensor_tensor(res[s][:], res[s][:], acc[s][:], ALU.add), False)
                    st.end()

            with dve.If(further > 0):
                combine(w_over, 0)
                combine(w_main, NT)
            with dve.Else():
                combine(w_main, 0)
            dve.nop()

        @block.tensor
        def _(pe):
            pe.wait_ge(c_wide_ready, 1)
            for i in range(EARLY):
                bank = (pj0, pj1, pj2)[i % 3]
                pe.wait_ge(ada_loaded[i % 3], (i // 3 + 1) * 32)
                wait(pe, mod_taken[i % 3], i // 3)
                nc.tensor.matmul(bank[:], cst("ones", 1), b_row[i % 3][:], start=True, stop=False)
                if i % 3 == 2:
                    pe.wait_ge(fma_ready, i // 3 + 1)
                    nc.tensor.matmul(bank[:], cst("ones"), fma[:], start=False, stop=True).then_inc(mod_filled, 1)
                    continue
                for k in range(KT):
                    ins = nc.tensor.matmul(bank[:], c_wide[:, k, :], ada[i % 3][:, k, :], start=False, stop=(k == KT - 1))
                ins.then_inc(mod_filled, 1)
            pe.wait_ge(w_in_loaded, 16)
            pe.wait_ge(small_loaded, 11 * 16)

            def transpose_h(n):
                pe.wait_ge(h_steps, n * 6 + 6)
                wait(pe, qkT_a, n)
                wait(pe, qkT_b, n)
                wait(pe, kg_ready, n - 1)
                wait(pe, at_masked, (n - 1) * 4)
                for k in range(KT):
                    ins = nc.tensor.transpose((tr0, tr1)[k // 4][:, (k % 4) * P:(k % 4 + 1) * P],
                                              h[:, k * P:(k + 1) * P], ident)
                ins.then_inc(hT_filled, 1)

            def project(bank, col, width, ks=range(KT)):
                for k in ks:
                    ins = nc.tensor.matmul(bank, hT[:, k, :], w_in[:, k, col:col + width],
                                           start=(k == 0), stop=(k == KT - 1))
                return ins

            def project_across(bank, col, width):
                for k in range(KT):
                    ins = nc.tensor.matmul(bank, w_in[:, k, col:col + width], hT[:, k, :],
                                           start=(k == 0), stop=(k == KT - 1))
                return ins

            def project_q(n):
                pe.wait_ge(hT_lo, n + 1)
                pe.wait_ge(hT_hi, n + 1)
                wait(pe, gv_ready, n)
                project(pj0[:], C_SQ, QW).then_inc(sq_filled, 1)

            def project_kv(n):
                wait(pe, ge_ready, n)
                project(pj1[:, 0:KW + VW], C_SK, KW + VW)
                project_across(pj1[0:RANK, 256:256 + P], C_LR, RANK).then_inc(skv_filled, 1)

            def transpose_qk(n):
                pe.wait_ge(qn_ready, n * 2 + 2)
                wait(pe, pv_a, n)
                for j in range(4):
                    nc.tensor.transpose(tr0[:, j * P:(j + 1) * P], qn[:, j * P:(j + 1) * P], ident)
                nc.tensor.transpose(sa[:, 0:P], qn[:, QW:], ident).then_inc(qk_filled, 1)

            def project_gqk(n):
                wait(pe, gqk_ready, n)
                wait(pe, yT_ready, n - 1)
                for j in range(4):
                    ins = project_across(pj2[:, j * P:(j + 1) * P], C_GQ + j * P, P)
                ins.then_inc(gqk_filled, 1)

            def project_gv(n):
                pe.wait_ge(qn_ready, n * 2 + 2)
                project(pj0[:], C_GV, GVW).then_inc(gv_filled, 1)

            def project_og(n, half):
                if half == 0:
                    pe.wait_ge(v_ready, n + 1)
                    project(pj1[:], C_OG, GVW, range(KT // 2))
                else:
                    project(pj1[:], C_OG, GVW, range(KT // 2, KT)).then_inc(og_filled, 1)

            def forget(n):
                pe.wait_ge(skv_squared, n + 1)
                wait(pe, s0_ready, n)
                nc.tensor.matmul(s_b[:, 0:GKW], glrT[:], w_g2[:], start=True, stop=True).then_inc(z_filled, 1)

            def window_scores(m):
                pe.wait_ge(qkT_a, m + 1)
                pe.wait_ge(qkT_b, m + 1)
                pe.wait_ge(z_neg, m + 1)
                wait(pe, y_ready, m)
                for c in range(2):
                    for j in range(4):
                        ins = nc.tensor.matmul((sa, s_b)[c][:, j * P:(j + 1) * P],
                                               qT[:, c, 2 * j:2 * j + 2, :].rearrange("p h t -> p (h t)"),
                                               kTw[:, j // 2, c * CH:c * CH + P], start=True, stop=True)
                ins.then_inc(sc_filled, 1)

            def transpose_p(m):
                pe.wait_ge(p_norm, m + 1)
                for c in range(2):
                    for j in range(4):
                        ins = nc.tensor.transpose((sa, s_b)[c][:, j * P:(j + 1) * P], sc[:, c, j * P:(j + 1) * P], ident)
                ins.then_inc(pt_filled, 1)

            def window_values(m):
                pe.wait_ge(pt_a, m + 1)
                pe.wait_ge(pt_b, m + 1)
                pe.wait_ge(v_ready, m + 1)
                for c in range(2):
                    for kv in range(KVH):
                        ins = nc.tensor.matmul((sa, s_b)[c][0:HD, kv * 256:(kv + 1) * 256],
                                               (v_a, v_b)[c][:, kv * HD:(kv + 1) * HD],
                                               pT[:, c, kv * 256:(kv + 1) * 256], start=True, stop=True)
                ins.then_inc(pv_filled, 1)

            def decay_sums(m, c):
                pe.wait_ge(la_ready, m + 1)
                if c == 1:
                    pe.wait_ge(fac_ready, m * 2 + 1)
                nc.tensor.matmul(gb[:], la[:, c * P:(c + 1) * P], cst("steps")[:, 0:512], start=True, stop=True)
                nc.tensor.matmul(tr1[:, 0:3 * P], la[:, c * P:(c + 1) * P], cst("steps")[:, 512:NF * P],
                                 start=True, stop=True).then_inc(e_filled, 1)

            def transpose_kg(m):
                pe.wait_ge(qkf_ready, m * 2 + 2)
                for c in range(2):
                    ins = nc.tensor.transpose(tr0[:, c * P:(c + 1) * P], kf[:, c, 4, :], ident)
                ins.then_inc(kg_filled, 1)

            def linear_scores(m):
                pe.wait_ge(fac_ready, m * 2 + 2)
                for hd in range(GH):
                    c, lo = hd // 2, (hd % 2) * GK
                    if hd >= 2:
                        pe.wait_ge(at_masked, m * 4 + hd - 1)
                    for lv in range(4):
                        q_at = (2, 3, 4, 0)[lv]
                        ins = nc.tensor.matmul((gb, tr1)[hd % 2][:, lv * P:(lv + 1) * P],
                                               kf[lo:lo + GK, c, lv, :], qf[lo:lo + GK, c, q_at, :],
                                               start=True, stop=True)
                    ins.then_inc(at_filled, 1)

            def state_terms(m):
                pe.wait_ge(kg_ready, m + 1)
                pe.wait_ge(gv_ready, m + 1)
                pe.wait_ge(pv_b, m + 1)
                for c in range(2):
                    for chunk in range(2):
                        for hh in range(2):
                            ins = nc.tensor.matmul(
                                s_b[hh * GK:(hh + 1) * GK, (2 * c + chunk) * GV:(2 * c + chunk + 1) * GV],
                                kg[:, chunk, c, hh * GK:(hh + 1) * GK],
                                gv[:, (2 * c + hh) * GV:(2 * c + hh + 1) * GV],
                                start=True, stop=True)
                ins.then_inc(dl_filled, 1)

            def linear_out(m):
                pe.wait_ge(s1_ready, m + 1)
                pe.wait_ge(at_ready, m * 4 + 4)
                wait(pe, s0_ready, m)
                for hd in (0, 2, 1, 3):
                    if hd == 1:
                        ins.then_inc(even_filled, 1)
                        pe.wait_ge(even_filled, m + 1)
                    c, lo = hd // 2, (hd % 2) * GK
                    col = slice(hd * GV, (hd + 1) * GV)
                    nc.tensor.matmul(sa[:, col], at[:, hd, :], gv[:, col], start=True, stop=False, skip_group_check=True)
                    for chunk, state in enumerate((s0, s1)):
                        ins = nc.tensor.matmul(sa[chunk * CH:(chunk + 1) * CH, col],
                                               qf[lo:lo + GK, c, 1, chunk * CH:(chunk + 1) * CH],
                                               state[lo:lo + GK, c, :], start=False, stop=True, skip_group_check=True)
                ins.then_inc(o_filled, 1)

            def transpose_y(m):
                pe.wait_ge(y_ready, m + 1)
                pe.wait_ge(gqk_ready, min(m + 2, NT) if isinstance(m, int) else m + 2)
                for j in range(4):
                    ins = nc.tensor.transpose(pj2[:, j * P:(j + 1) * P], y[:, j * P:(j + 1) * P], ident)
                ins.then_inc(yt_filled, 1)

            def late_sum(m):
                pe.wait_ge(fma_ready, m + 1)
                pe.wait_ge(at_masked, m * 4)
                nc.tensor.matmul(gb[:], cst("ones", 1), b_row_late[:], start=True, stop=False)
                nc.tensor.matmul(gb[:], cst("ones"), ada_late[:, 0, :], start=False, stop=True).then_inc(mod_filled, 1)

            def project_out(t, s, half):
                if half == 0:
                    pe.wait_ge(yx_loaded[s], (t - s) * 16 + 32)
                    if not (isinstance(t, int) and t < 2):
                        pe.wait_ge(x1_ready, t - 1)
                bank = ((pj0, pj1), (pj2, sa))[s][half]
                for k in range(KT):
                    ins = nc.tensor.matmul(bank[:], y_in[s][:, k, :], w_o[:, k, half * 512:(half + 1) * 512],
                                           start=(k == 0), stop=(k == KT - 1))
                if half:
                    ins.then_inc(wo_filled, 1)

            def mixer_tile(m, more_tiles, first=False):
                n = m + 1
                if more_tiles:
                    transpose_h(n)
                window_scores(m)
                if more_tiles:
                    project_q(n)
                if not first:
                    late_sum(m)
                    transpose_y(m - 1)
                transpose_p(m)
                if more_tiles:
                    project_kv(n)
                window_values(m)
                if not first:
                    pe.wait_ge(mod_taken[0], m + EARLY_TAKEN[0])
                decay_sums(m, 0)
                if more_tiles:
                    project_gqk(n)
                    transpose_qk(n)
                decay_sums(m, 1)
                if more_tiles:
                    project_gv(n)
                else:
                    pe.wait_ge(gv_ready, NT)
                    pe.wait_ge(ge_ready, NT)
                    pe.wait_ge(rt_loaded, 64)
                    project_out(0, 0, 0)
                transpose_kg(m)
                linear_scores(m)
                state_terms(m)
                if more_tiles:
                    project_og(n, 0)
                else:
                    pe.wait_ge(pv_a, m + 1)
                    project_out(0, 0, 1)
                linear_out(m)
                if more_tiles:
                    project_og(n, 1)
                    forget(n)

            transpose_h(0)
            project_q(0)
            project_kv(0)
            transpose_qk(0)
            project_gqk(0)
            project_gv(0)
            project_og(0, 0)
            project_og(0, 1)
            forget(0)
            mixer_tile(0, True, True)
            with pe.Fori(1, NT - 1) as m:
                mixer_tile(m, True)
            mixer_tile(NT - 1, False)
            transpose_y(NT - 1)

            def transpose_h2(t, s):
                pe.wait_ge(h2_ready, t + 1)
                for k in range(KT):
                    ins = nc.tensor.transpose((tr0, tr1)[k // 4][:, (k % 4) * P:(k % 4 + 1) * P],
                                              h2[s][:, k * P:(k + 1) * P], ident)
                ins.then_inc(h2t_filled, 1)

            def rank(t):
                pe.wait_ge(lg_steps, t * (CHOOSE + PLACE) + CHOOSE)
                nc.tensor.matmul(s_b[:, 0:NE], cst("before"), chosen[:, bass.ds(t, 1)].rearrange("p a e -> p (a e)"),
                                 start=True, stop=False)
                nc.tensor.matmul(s_b[:, 0:NE], cst("ones"), prior[:, bass.ds(t, 1)].rearrange("p a e -> p (a e)"),
                                 start=False, stop=True).then_inc(ranked, 1)

            def router(t):
                pe.wait_ge(h2t_lo, t + 1)
                pe.wait_ge(h2t_hi, t + 1)
                for k in range(KT):
                    ins = nc.tensor.matmul(gb[:, 0:NE], h2T[:, k, :], w_r[:, k, :], start=(k == 0), stop=(k == KT - 1))
                ins.then_inc(lg_filled, 1)

            pe.wait_ge(y_ready, NT)
            pe.wait_ge(yT_ready, NT)
            pe.wait_ge(at_masked, NT * 4)
            for half in range(2):
                project_out(1, 1, half)
            transpose_h2(0, 0)
            with pe.Fori(1, NT // 2) as i:
                for s in range(2):
                    project_out(i * 2 + s, s, 0)
                    router(i * 2 + s - 2)
                    project_out(i * 2 + s, s, 1)
                    rank(i * 2 + s - 2)
                    transpose_h2(i * 2 + s - 1, 1 - s)
            router(NT - 2)
            transpose_h2(NT - 1, 1)
            rank(NT - 2)
            router(NT - 1)
            rank(NT - 1)
            nc.tensor.matmul(pj0[:, 0:NT * NE], cst("before"), chosen[:].rearrange("p t e -> p (t e)"),
                             start=True, stop=False)
            nc.tensor.matmul(pj0[:, 0:NT * NE], cst("ones"), prior[:, 0:NT, :].rearrange("p t e -> p (t e)"),
                             start=False, stop=True)
            nc.tensor.matmul(pj1[:, 0:NE], cst("ones"), prior[:, NT, :], start=True, stop=True).then_inc(rank_filled, 1)

            m_banks = (pj0, pj1, pj2, sa)
            pe.wait_ge(slots_ready, 2)
            pe.wait_ge(bias_loaded, 48)
            for j in range(3):
                for k in range(KT):
                    ins = nc.tensor.transpose(m_banks[j][:, k * NE:(k + 1) * NE], b_rows[:, j, k * P:(k + 1) * P],
                                              ident[0:NE, 0:NE])
            ins.then_inc(bias_filled, 1)

            def split_ready(b, ci):
                on_pool = sum(1 for x in range(ci + 1) if x in POOL_CHUNKS)
                if ci in POOL_CHUNKS:
                    pe.wait_ge(lo_pool, b * len(POOL_CHUNKS) + on_pool)
                else:
                    pe.wait_ge(lo_dve, b * (NCH - len(POOL_CHUNKS)) + (ci + 1 - on_pool))

            def transpose_x(b, q):
                if q < 2:
                    pe.wait_ge(x_gathered, b * 32 + 32)
                    wait(pe, xt_lo, b * 4 + q - 2)
                else:
                    pe.wait_ge(xt_lo, b * 4 + q - 1)
                bank = (tr0, tr1)[q % 2]
                for kk in range(2):
                    k = 2 * q + kk
                    nc.tensor.transpose(bank[:, kk * CAP:kk * CAP + P], x_got[:, 0, k * P:(k + 1) * P], ident)
                    ins = nc.tensor.transpose(bank[:, kk * CAP + P:(kk + 1) * CAP],
                                              x_got[0:CAP2, 1, k * P:(k + 1) * P], ident[0:CAP2, 0:CAP2])
                ins.then_inc(xt_filled, 1)

            def bank_free(b, q):
                if 4 <= q < 20:
                    pe.wait_ge(up_taken, b * 16 + q - 3)
                elif q >= 20:
                    pe.wait_ge(down_taken, b * 8 + q - 19)
                elif not isinstance(b, int):
                    pe.wait_ge(down_taken, b * 8 + q - 3)

            def products(b, ci, moving, width, ks=range(KT)):
                if ks[0] == 0:
                    split_ready(b, ci)
                for f in range(WCOLS // P):
                    q = 2 * ci + f
                    if ks[0] == 0:
                        bank_free(b, q)
                    bank = m_banks[q % 4]
                    both = bank[:, 0:2 * CAP].rearrange("p (two t) -> p two t", two=2)[:, :, 0:width]
                    cols = slice(f * P, (f + 1) * P)
                    for k in ks:
                        nc.tensor.matmul(both, w_hi[ci % NHL][:, k, cols], moving[:, k, :, 0:width],
                                         start=(k == 0), stop=(k == KT - 1), skip_group_check=True)
                        ins = nc.tensor.matmul(bank[:, 0:width], w_lo[ci % NHL][:, k, cols], moving[:, k, 0, 0:width],
                                               start=False, stop=(k == KT - 1), skip_group_check=True)
                    if ks[-1] == KT - 1:
                        ins.then_inc(m_filled, 1)

            def transpose_rows(b, pair):
                pe.wait_ge(down_taken, b * 8 + 2 * pair + 2)
                if pair % 2 == 0:
                    wait(pe, y_taken, b * 2 + pair // 2)
                for f in range(2):
                    col = ((pair % 2) * 2 + f) * P
                    nc.tensor.transpose(s_b[:, col:col + P], yT2[:, pair, f, 0:P], ident)
                    ins = nc.tensor.transpose(gb[0:CAP2, col:col + P], yT2[:, pair, f, P:CAP], ident)
                ins.then_inc(yt2_filled, 1)

            def all_products(b, width, before=None):
                for ci in range(8):
                    products(b, ci, xT, width)
                    if ci < 2 and before is not None:
                        transpose_rows(before, 2 + ci)
                pe.wait_ge(act_lo, b * 4 + 3)
                products(b, 8, actT, width, range(KT - 2))
                products(b, 9, actT, width, range(KT - 2))
                pe.wait_ge(act_lo, b * 4 + 4)
                products(b, 8, actT, width, range(KT - 2, KT))
                transpose_x(b + 1, 0)
                transpose_x(b + 1, 1)
                products(b, 9, actT, width, range(KT - 2, KT))
                transpose_x(b + 1, 2)
                products(b, 10, actT, width)
                transpose_x(b + 1, 3)
                transpose_rows(b, 0)
                products(b, 11, actT, width)
                transpose_rows(b, 1)

            for q in range(4):
                transpose_x(0, q)
            n_blocks = pe.value_load(blocks[0:1, 0:1], min_val=NE, max_val=NE + MAXOV)
            pe.wait_ge(bias_ready, 1)
            pe.wait_ge(xt_lo, 4)
            all_products(0, CAP)
            with pe.Fori(1, n_blocks) as b:
                pe.wait_ge(xt_lo, b * 4 + 4)
                wide = pe.value_load(wide_of[0:1, bass.ds(b, 1)], min_val=0, max_val=len(WIDTHS) - 1)
                with pe.If(wide > 0):
                    with pe.If(wide > 1):
                        all_products(b, WIDTHS[2], b - 1)
                    with pe.Else():
                        all_products(b, WIDTHS[1], b - 1)
                with pe.Else():
                    all_products(b, WIDTHS[0], b - 1)
            last = pe.value_load(blocks[0:1, 2:3], min_val=NE - 1, max_val=NE + MAXOV - 1)
            transpose_rows(last, 2)
            transpose_rows(last, 3)


_INS = ["x", "c", "norm1_g", "w_ada", "b_ada", "w_in", "q_norm_g", "k_norm_g", "sinks", "w_gla_gate2",
        "b_gla_gate", "gla_norm_g", "w_out", "norm2_g", "w_router", "b_router", "w_gate", "b_gate", "w_up",
        "b_up", "w_down", "b_down"]


def kernel(**inputs):
    import concourse.bacc as bacc
    from concourse.bass_utils import run_bass_kernel_spmd

    nc = bacc.Bacc("TRN2", target_bir_lowering=False, num_devices=1)
    arrays, args = {}, {}
    for name in _INS:
        v = np.ascontiguousarray(inputs[name])
        arrays[f"in_{name}"] = v
        args[name] = nc.dram_tensor(f"in_{name}", v.shape, mybir.dt.from_np(v.dtype), kind="ExternalInput").ap()
    arrays["in_const"] = CONST
    args["const"] = nc.dram_tensor("in_const", CONST.shape, F32, kind="ExternalInput").ap()
    out = nc.dram_tensor("out_0", (1, T, D), F32, kind="ExternalOutput").ap()
    build(nc, args, out)
    r = run_bass_kernel_spmd(nc, [arrays], core_ids=[0])
    return r.results[0]["out_0"]
```
